# Optimizing a Trainium2 kernel written in Bass

```python
import jax, jax.numpy as jnp
from jax import lax
import numpy as np

D_MODEL = 2048
BATCH = 1
SEQ = 128
DEPTH = 2
DEC_BATCH = 1
DEC_SEQ = 256
PAST_LEN = 128

GRID_W = 64
HEAD_DIM = 128
A_Q_HEADS = 8
A_KV_HEADS = 2
B_HEADS = 8
A_WIDTH = A_Q_HEADS * HEAD_DIM
A_KV_WIDTH = A_KV_HEADS * HEAD_DIM
B_WIDTH = B_HEADS * HEAD_DIM
L0_WIDTH = A_WIDTH + B_WIDTH
L0_IN = A_WIDTH + 2 * A_KV_WIDTH + 3 * B_WIDTH + L0_WIDTH
NA_WIN_H = 8
NA_WIN_W = 16
MLA_HEADS = 16
Q_LORA = 512
KV_LORA = 512
QK_NOPE = 128
QK_ROPE = 64
V_DIM = 128
L1_WIDTH = MLA_HEADS * V_DIM
L1_IN = Q_LORA + KV_LORA + QK_ROPE + L1_WIDTH
Q_BLOCK = 128
ROPE_THETA = 10000.0
EPS = 1e-6
NEG_INF = -1e30

kernel_name = 'hybrid_diffusion_prefix_step'

def rmsnorm(x, g):
    xf = x.astype(jnp.float32)
    y = xf * lax.rsqrt(jnp.mean(xf * xf, axis=-1, keepdims=True) + EPS)
    return (y * g.astype(jnp.float32)).astype(x.dtype)

def adaln(c, w, b):
    m = jax.nn.silu(c) @ w + b
    shift, scale, gate = jnp.split(m, 3, axis=-1)
    return shift[:, None], scale[:, None], gate[:, None]

def rope_half(x, ang):
    m = x.shape[-1] // 2
    cos = jnp.cos(ang)[:, None, :].astype(x.dtype)
    sin = jnp.sin(ang)[:, None, :].astype(x.dtype)
    x1, x2 = x[..., :m], x[..., m:]
    return jnp.concatenate([x1 * cos - x2 * sin, x2 * cos + x1 * sin], axis=-1)

def axial_rope(x):
    S, d = x.shape[1], x.shape[-1]
    a = d // 2
    t = jnp.arange(S)
    row = (t // GRID_W).astype(jnp.float32)
    col = (t % GRID_W).astype(jnp.float32)
    inv = 1.0 / (ROPE_THETA ** (jnp.arange(a // 2, dtype=jnp.float32) * 2.0 / a))
    return jnp.concatenate([rope_half(x[..., :a], row[:, None] * inv),
                            rope_half(x[..., a:], col[:, None] * inv)], axis=-1)

def blocked_attention(q, k, v, scale):
    B, S, Hkv, G, Dq = q.shape
    nb = S // Q_BLOCK
    qb = jnp.moveaxis(q.reshape(B, nb, Q_BLOCK, Hkv, G, Dq), 1, 0)

    def one_block(qblk):
        s = jnp.einsum('bqhgd,bkhd->bhgqk', qblk, k).astype(jnp.float32) * scale
        p = jax.nn.softmax(s, axis=-1).astype(v.dtype)
        return jnp.einsum('bhgqk,bkhd->bqhgd', p, v)

    out = lax.map(one_block, qb)
    return jnp.moveaxis(out, 0, 1).reshape(B, S, Hkv * G, v.shape[-1])

def neighbourhood_attention(q, k, v, k_ctx, v_ctx, rpb, scale):
    B, S, H, D = q.shape
    rows = S // GRID_W
    wh = min(NA_WIN_H, rows)
    ncb = GRID_W // NA_WIN_W
    ksw = 2 * NA_WIN_W
    row_start = jnp.clip(jnp.arange(rows) - wh // 2, 0, rows - wh)
    key_cols = jnp.clip(jnp.arange(ncb) * NA_WIN_W - NA_WIN_W // 2, 0, GRID_W - ksw)[:, None] + jnp.arange(ksw)
    q_cols = jnp.arange(GRID_W).reshape(ncb, NA_WIN_W)
    col_start = jnp.clip(q_cols - NA_WIN_W // 2, 0, GRID_W - NA_WIN_W)
    kc = key_cols[:, None, :]
    col_ok = (kc >= col_start[..., None]) & (kc < col_start[..., None] + NA_WIN_W)
    dx_idx = jnp.clip(kc - q_cols[..., None] + NA_WIN_W - 1, 0, 2 * NA_WIN_W - 2)
    q_g = q.reshape(B, rows, ncb, NA_WIN_W, H, D)
    k_g = k.reshape(B, rows, GRID_W, H, D)
    v_g = v.reshape(B, rows, GRID_W, H, D)
    n_loc = wh * ksw

    def row_block(r):
        q_r = lax.dynamic_index_in_dim(q_g, r, axis=1, keepdims=False)
        rs = row_start[r]
        k_blk = jnp.take(lax.dynamic_slice_in_dim(k_g, rs, wh, axis=1), key_cols, axis=2)
        v_blk = jnp.take(lax.dynamic_slice_in_dim(v_g, rs, wh, axis=1), key_cols, axis=2)
        dy_idx = rs + jnp.arange(wh) - r + NA_WIN_H - 1
        bias = rpb[:, dy_idx[:, None, None, None], dx_idx[None]]
        bias = jnp.where(col_ok[None, None], bias.astype(jnp.float32), NEG_INF)
        bias = jnp.transpose(bias, (0, 2, 3, 1, 4))[None]
        s_loc = jnp.einsum('bjqhd,bajkhd->bhjqak', q_r, k_blk).astype(jnp.float32) * scale + bias
        s_loc = s_loc.reshape(B, H, ncb, NA_WIN_W, n_loc)
        s_ctx = jnp.einsum('bjqhd,blhd->bhjql', q_r, k_ctx).astype(jnp.float32) * scale
        p = jax.nn.softmax(jnp.concatenate([s_loc, s_ctx], axis=-1), axis=-1).astype(v.dtype)
        p_loc = p[..., :n_loc].reshape(B, H, ncb, NA_WIN_W, wh, ksw)
        o = (jnp.einsum('bhjqak,bajkhd->bjqhd', p_loc, v_blk)
             + jnp.einsum('bhjql,blhd->bjqhd', p[..., n_loc:], v_ctx))
        return o.reshape(B, GRID_W, H, D)

    out = lax.map(row_block, jnp.arange(rows))
    return jnp.moveaxis(out, 0, 1).reshape(B, S, H, D)

def l0_split(h, w_in):
    B, S, _ = h.shape
    idx = np.cumsum([A_WIDTH, A_KV_WIDTH, A_KV_WIDTH, B_WIDTH, B_WIDTH, B_WIDTH]).tolist()
    q_a, k_a, v_a, q_b, k_b, v_b, gate = jnp.split(h @ w_in, idx, axis=-1)
    return (q_a.reshape(B, S, A_Q_HEADS, HEAD_DIM), k_a.reshape(B, S, A_KV_HEADS, HEAD_DIM),
            v_a.reshape(B, S, A_KV_HEADS, HEAD_DIM), q_b.reshape(B, S, B_HEADS, HEAD_DIM),
            k_b.reshape(B, S, B_HEADS, HEAD_DIM), v_b.reshape(B, S, B_HEADS, HEAD_DIM), gate)

def l0_merge(o_a, o_b, gate, w_out):
    B, S = gate.shape[:2]
    o = jnp.concatenate([o_a.reshape(B, S, A_WIDTH), o_b.reshape(B, S, B_WIDTH)], axis=-1)
    return (o * jax.nn.silu(gate)) @ w_out

def l0_context(h, w_in, q_norm, k_norm, w_out):
    B, L, _ = h.shape
    q_a, k_a, v_a, q_b, k_b, v_b, gate = l0_split(h, w_in)
    q_a = rmsnorm(q_a, q_norm)
    k_a = rmsnorm(k_a, k_norm)
    sc = HEAD_DIM ** -0.5
    o_a = blocked_attention(q_a.reshape(B, L, A_KV_HEADS, A_Q_HEADS // A_KV_HEADS, HEAD_DIM), k_a, v_a, sc)
    o_b = blocked_attention(q_b[:, :, :, None], k_b, v_b, sc)
    return l0_merge(o_a, o_b, gate, w_out), (k_a, v_a, k_b, v_b)

def l0_latent(h, ck_a, cv_a, ck_b, cv_b, w_in, q_norm, k_norm, rpb, w_out):
    B, S, _ = h.shape
    q_a, k_a, v_a, q_b, k_b, v_b, gate = l0_split(h, w_in)
    q_a = axial_rope(rmsnorm(q_a, q_norm))
    k_a = axial_rope(rmsnorm(k_a, k_norm))
    sc = HEAD_DIM ** -0.5
    o_a = blocked_attention(q_a.reshape(B, S, A_KV_HEADS, A_Q_HEADS // A_KV_HEADS, HEAD_DIM),
                            jnp.concatenate([ck_a, k_a], axis=1), jnp.concatenate([cv_a, v_a], axis=1), sc)
    o_b = neighbourhood_attention(q_b, k_b, v_b, ck_b, cv_b, rpb, sc)
    return l0_merge(o_a, o_b, gate, w_out)

def l1_split(h, w_in, q_a_norm, w_q_b, kv_a_norm):
    B, S, _ = h.shape
    q_lat, kv_lat, k_rope, gate = jnp.split(h @ w_in, np.cumsum([Q_LORA, KV_LORA, QK_ROPE]).tolist(), axis=-1)
    q = (rmsnorm(q_lat, q_a_norm) @ w_q_b).reshape(B, S, MLA_HEADS, QK_NOPE + QK_ROPE)
    ckv = rmsnorm(kv_lat, kv_a_norm)
    return q[..., :QK_NOPE], q[..., QK_NOPE:], ckv, k_rope, gate

def mla_attend(q_nope, q_rope, ckv, k_rope, w_kv_b):
    B, T, _ = ckv.shape
    kv = (ckv @ w_kv_b).reshape(B, T, MLA_HEADS, QK_NOPE + V_DIM)
    k = jnp.concatenate([kv[..., :QK_NOPE],
                         jnp.broadcast_to(k_rope[:, :, None, :], (B, T, MLA_HEADS, QK_ROPE))], axis=-1)
    q = jnp.concatenate([q_nope, q_rope], axis=-1)[:, :, :, None]
    return blocked_attention(q, k, kv[..., QK_NOPE:], (QK_NOPE + QK_ROPE) ** -0.5)

def l1_context(h, w_in, q_a_norm, w_q_b, kv_a_norm, w_kv_b, w_out):
    B, L, _ = h.shape
    q_nope, q_rope, ckv, k_rope, gate = l1_split(h, w_in, q_a_norm, w_q_b, kv_a_norm)
    o = mla_attend(q_nope, q_rope, ckv, k_rope, w_kv_b).reshape(B, L, L1_WIDTH)
    return (o * jax.nn.silu(gate)) @ w_out, (ckv, k_rope)

def l1_latent(h, c_ckv, c_krope, w_in, q_a_norm, w_q_b, kv_a_norm, w_kv_b, w_out):
    B, S, _ = h.shape
    q_nope, q_rope, ckv, k_rope, gate = l1_split(h, w_in, q_a_norm, w_q_b, kv_a_norm)
    q_rope = axial_rope(q_rope)
    k_rope = axial_rope(k_rope[:, :, None, :])[:, :, 0]
    o = mla_attend(q_nope, q_rope, jnp.concatenate([c_ckv, ckv], axis=1),
                   jnp.concatenate([c_krope, k_rope], axis=1), w_kv_b).reshape(B, S, L1_WIDTH)
    return (o * jax.nn.silu(gate)) @ w_out

def setup_inputs(seed: int = 0) -> dict:
    key = jax.random.key(seed)
    ks = jax.random.split(key, 28)
    f32 = jnp.float32

    def nrm(k, shape, scale=1.0):
        return jax.random.normal(k, shape, f32) * scale

    def gain(k, n):
        return 1.0 + 0.05 * jax.random.normal(k, (n,), f32)

    D = D_MODEL
    return {
        'x_prompt': nrm(ks[0], (BATCH, SEQ, D)),
        'x_sample': nrm(ks[1], (DEC_BATCH, DEC_SEQ, D)),
        'cache_l0_a_k': nrm(ks[2], (DEC_BATCH, PAST_LEN, A_KV_HEADS, HEAD_DIM)),
        'cache_l0_a_v': nrm(ks[3], (DEC_BATCH, PAST_LEN, A_KV_HEADS, HEAD_DIM)),
        'cache_l0_b_k': nrm(ks[4], (DEC_BATCH, PAST_LEN, B_HEADS, HEAD_DIM)),
        'cache_l0_b_v': nrm(ks[5], (DEC_BATCH, PAST_LEN, B_HEADS, HEAD_DIM)),
        'cache_l1_ckv': nrm(ks[6], (DEC_BATCH, PAST_LEN, KV_LORA)),
        'cache_l1_krope': nrm(ks[7], (DEC_BATCH, PAST_LEN, QK_ROPE)),
        'c': nrm(ks[8], (DEC_BATCH, D)),
        'c_ctx': nrm(ks[9], (D,)),
        'l0_norm': gain(ks[10], D),
        'l0_ada_w': nrm(ks[11], (D, 3 * D), 0.5 * D ** -0.5),
        'l0_ada_b': nrm(ks[12], (3 * D,), 0.02),
        'l0_w_in': nrm(ks[13], (D, L0_IN), D ** -0.5),
        'l0_q_norm': gain(ks[14], HEAD_DIM),
        'l0_k_norm': gain(ks[15], HEAD_DIM),
        'l0_rpb': nrm(ks[16], (B_HEADS, 2 * NA_WIN_H - 1, 2 * NA_WIN_W - 1), 0.2),
        'l0_w_out': nrm(ks[17], (L0_WIDTH, D), L0_WIDTH ** -0.5),
        'l1_norm': gain(ks[18], D),
        'l1_ada_w': nrm(ks[19], (D, 3 * D), 0.5 * D ** -0.5),
        'l1_ada_b': nrm(ks[20], (3 * D,), 0.02),
        'l1_w_in': nrm(ks[21], (D, L1_IN), D ** -0.5),
        'l1_q_a_norm': gain(ks[22], Q_LORA),
        'l1_w_q_b': nrm(ks[23], (Q_LORA, MLA_HEADS * (QK_NOPE + QK_ROPE)), Q_LORA ** -0.5),
        'l1_kv_a_norm': gain(ks[24], KV_LORA),
        'l1_w_kv_b': nrm(ks[25], (KV_LORA, MLA_HEADS * (QK_NOPE + V_DIM)), KV_LORA ** -0.5),
        'l1_w_out': nrm(ks[26], (L1_WIDTH, D), L1_WIDTH ** -0.5),
        'final_norm': gain(ks[27], D),
    }

def reference(x_prompt, x_sample, cache_l0_a_k, cache_l0_a_v, cache_l0_b_k, cache_l0_b_v,
              cache_l1_ckv, cache_l1_krope, c, c_ctx,
              l0_norm, l0_ada_w, l0_ada_b, l0_w_in, l0_q_norm, l0_k_norm, l0_rpb, l0_w_out,
              l1_norm, l1_ada_w, l1_ada_b, l1_w_in, l1_q_a_norm, l1_w_q_b, l1_kv_a_norm,
              l1_w_kv_b, l1_w_out, final_norm):
    norms = [l0_norm, l1_norm]
    ada_ws = [l0_ada_w, l1_ada_w]
    ada_bs = [l0_ada_b, l1_ada_b]
    caches = [(cache_l0_a_k, cache_l0_a_v, cache_l0_b_k, cache_l0_b_v), (cache_l1_ckv, cache_l1_krope)]

    x = x_prompt
    ctx_states = []
    for i in range(DEPTH):
        shift, scale, gate = adaln(c_ctx[None], ada_ws[i], ada_bs[i])
        h = rmsnorm(x, norms[i]) * (1.0 + scale) + shift
        if i % 2 == 0:
            out, st = l0_context(h, l0_w_in, l0_q_norm, l0_k_norm, l0_w_out)
        else:
            out, st = l1_context(h, l1_w_in, l1_q_a_norm, l1_w_q_b, l1_kv_a_norm, l1_w_kv_b, l1_w_out)
        x = x + gate * out
        ctx_states.append(st)
    y_prompt = rmsnorm(x, final_norm)
    new_l0_a_k, new_l0_a_v, new_l0_b_k, new_l0_b_v = ctx_states[0]
    new_l1_ckv, new_l1_krope = ctx_states[1]

    x = x_sample
    for i in range(DEPTH):
        shift, scale, gate = adaln(c, ada_ws[i], ada_bs[i])
        h = rmsnorm(x, norms[i]) * (1.0 + scale) + shift
        if i % 2 == 0:
            ck_a, cv_a, ck_b, cv_b = caches[i]
            out = l0_latent(h, ck_a, cv_a, ck_b, cv_b, l0_w_in, l0_q_norm, l0_k_norm, l0_rpb, l0_w_out)
        else:
            c_ckv, c_krope = caches[i]
            out = l1_latent(h, c_ckv, c_krope, l1_w_in, l1_q_a_norm, l1_w_q_b, l1_kv_a_norm, l1_w_kv_b, l1_w_out)
        x = x + gate * out
    y_sample = rmsnorm(x, final_norm)

    return (y_prompt, y_sample, new_l0_a_k, new_l0_a_v, new_l0_b_k, new_l0_b_v, new_l1_ckv, new_l1_krope)


_drawn_inputs = setup_inputs


def setup_inputs(seed=0):
    import zlib

    import numpy as np

    out = dict(_drawn_inputs(seed))
    spreads = {}
    factors = {'cache_l0_a_k': 8.0,
     'cache_l0_a_v': 8.0,
     'cache_l0_b_k': 38.88,
     'cache_l0_b_v': 32.144,
     'cache_l1_ckv': 5.829,
     'cache_l1_krope': 8.0,
     'l0_q_norm': 8.0,
     'l0_rpb': 64.0,
     'l1_q_a_norm': 8.0,
     'l1_w_q_b': 2.676}
    for name, (base, spread) in spreads.items():
        noise = np.random.default_rng([zlib.crc32(name.encode()), seed]).standard_normal(out[name].shape)
        drawn = base * np.exp(spread * noise) if base else spread * noise
        out[name] = __import__('jax').numpy.asarray(drawn.astype(out[name].dtype))
    for name, factor in factors.items():
        out[name] = (out[name] * factor).astype(out[name].dtype)
    return out
```

```python
from contextlib import ExitStack

import numpy as np

import concourse.bass as bass
from concourse import mybir

F32 = mybir.dt.float32
F32R = mybir.dt.float32r
ALU = mybir.AluOpType
ACT = mybir.ActivationFunctionType
X = mybir.AxisListType.X

P = 128
D = 2048
KT = D // P
CH = 512
NT = 3
TOK = NT * P
KEYS = 4 * P
KEY_TILE = [0, 2, 3]
GRID_W = 64
WIN = 16
HEAD = 128
ROPE = 64
SLOT = 1024
SPC = KT * CH // SLOT
KPS = SLOT // CH
RAW_RING, SPLIT_RING, ADA_RING = 4, 2, 8
HALVES = 2 * KT
EPS = 1e-6
SC0 = HEAD ** -0.5
SC1 = (HEAD + ROPE) ** -0.5
GROUP = 4
UNITS = GROUP * NT

N_A, N_B, N_OUT, N_GATE, N_H = 2, 2, D // CH, D // CH, 4
W_KV = 0
W_A = W_KV + SPC
W_B = W_A + N_A * 2 * SPC
W_O0 = W_B + N_B * 4 * SPC
W_QL = W_O0 + N_OUT * SPC
W_KR = W_QL + 2 * SPC
W_G = W_KR + 1
W_H = W_G + N_GATE * SPC
W_O1 = W_H + N_H * GROUP * 2
W_END = W_O1 + N_OUT * SPC
M_KV = 0
M_A = M_KV + NT
M_B = M_A + N_A * 2 * NT
M_O0 = M_B + N_B * 4 * NT
M_QL = M_O0 + N_OUT * NT
M_KR = M_QL + 2 * NT
M_G = M_KR + 1
M_H = M_G + N_GATE * NT
M_O1 = M_H + N_H * GROUP * 4
M_END = M_O1 + N_OUT * NT
T_A_PER = 1 + GROUP + UNITS
T_B_PER = 2 * GROUP + UNITS
T_H_PER = GROUP + UNITS
T_A = 0
T_B = T_A + N_A * T_A_PER
T_H = T_B + N_B * T_B_PER
X_VEC = 0
X_X0 = X_VEC + 1
X_MOD0 = X_X0 + KT
X_U0 = X_MOD0 + 2
X_MOD1 = X_U0 + KT
X_X1 = X_MOD1 + 2
X_QN = X_X1 + KT
X_CKV = X_QN + 4
X_KR = X_CKV + 4
X_U1 = X_KR + 1
X_END = X_U1 + KT
XH_U0, XH_QN, XH_CKV, XH_U1 = 0, KT, KT + 4, KT + 8
N_UA, N_UB, N_UH = 0, N_A * UNITS, (N_A + N_B) * UNITS


MM_G = 2 * (M_KR - M_KV) // NT
MM_H = MM_G + 2 * N_GATE
MM_O1 = MM_H + 2 * N_H * GROUP


class At:

    def __init__(self, fixed, turn=None, per=0):
        self.fixed, self.turn, self.per = fixed, turn, per

    def plus(self, k):
        return At(self.fixed + k, self.turn, self.per)

    def count(self, off=0):
        c = self.fixed + off
        return c if self.turn is None else self.turn * self.per + c

    def ring(self, n):
        assert self.per % n == 0
        return self.fixed % n

    def lap(self, n):
        c = self.fixed // n
        return c if self.turn is None else self.turn * (self.per // n) + c


def finished(m):
    for start, base, size in ((M_O1, MM_O1, NT), (M_H, MM_H, 4), (M_G, MM_G, NT), (M_KV, 0, NT)):
        if m.fixed >= start:
            return At(base + 2 * ((m.fixed - start) // size), m.turn, 2 * m.per // size)


def need(eng, sem, at, off=0):
    if at.turn is None:
        if at.fixed + off > 0:
            eng.wait_ge(sem, at.fixed + off)
    else:
        eng.wait_ge(sem, at.count(max(off, -at.fixed)))


def landed(eng, sems, at):
    n = len(sems)
    lap = at.lap(n)
    eng.wait_ge(sems[at.ring(n)], lap * 16 + 16)


class Chain:

    def __init__(self, eng, sem):
        self.eng, self.sem, self.at, self.k = eng, sem, At(0), 0

    def add(self, ins):
        ins.then_inc(self.sem, 1)
        self.k += 1

    def sync(self):
        self.eng.wait_ge(self.sem, self.at.count(self.k))

    def enter(self, turn, per):
        self.at, self.k = At(self.at.fixed + self.k, turn, per), 0

    def leave(self, turns):
        assert self.k == self.at.per, (self.k, self.at.per)
        self.at, self.k = At(self.at.fixed + turns * self.k), 0


def spread(ap, dims):
    return bass.AP(ap.tensor, ap.offset, [list(ap.ap[0])] + dims)


def build(nc, t_in, t_out):
    ctx = ExitStack()
    with ctx:
        top = [(nc.sbuf_base + 63) // 64 * 64]

        def sb(name, shape, dt=F32, at=None):
            size = int(np.prod(shape[1:])) * 4
            offset = top[0] if at is None else at
            if at is None:
                top[0] += (size + 31) // 32 * 32
            return nc.alloc_sbuf_tensor_at(name, [P] + list(shape[1:]), dt, offset=offset)

        def sem(name):
            return ctx.enter_context(nc.semaphore(name))

        act_hi = sb("act_hi", [P, KT, TOK], F32R)
        lo_at = top[0]
        act_lo = sb("act_lo", [P, KT, TOK], F32R)
        act_f = sb("act_f", [P, KT, TOK], F32, at=lo_at)
        u = sb("u", [P, NT, D])
        w_raw = sb("w_raw", [P, RAW_RING, SLOT])
        w_hi = sb("w_hi", [P, SPLIT_RING, SLOT], F32R)
        w_lo = sb("w_lo", [P, SPLIT_RING, SLOT], F32R)
        ada_at = top[0]
        ada = sb("ada", [P, ADA_RING, SLOT])
        gate_bc = sb("gate_bc", [P, 2, D], F32, at=ada_at)
        fnorm = sb("fnorm", [P, D], F32, at=ada_at + 2 * D * 4)
        ckv_hi = sb("ckv_hi", [P, 4, KEYS], F32R, at=ada_at)
        ckv_lo = sb("ckv_lo", [P, 4, KEYS], F32R, at=ada_at + 4 * KEYS * 4)
        qn_hi = sb("qn_hi", [P, 4, TOK], F32R, at=ada_at + 8 * KEYS * 4)
        qn_lo = sb("qn_lo", [P, 4, TOK], F32R, at=ada_at + 8 * KEYS * 4 + 4 * TOK * 4)
        st = sb("st", [P, 2, NT, CH])
        qT = sb("qT", [P, GROUP, TOK])
        kT = sb("kT", [P, GROUP, KEYS])
        k_group = kT[:, 1, :].rearrange("p (t d) -> p t d", t=4)
        v_group = kT[:, 2, :].rearrange("p (t d) -> p t d", t=4)
        v4 = sb("v4", [P, 4, CH])
        prob = sb("prob", [P, 3, 3 * P])
        probT = sb("probT", [P, 2, 3 * P])
        rows = sb("rows", [P, 6, CH])
        bias_at = top[0]
        bias = sb("bias", [P, GROUP, 2, 4, GRID_W])
        gain_ql = sb("gain_ql", [P, CH], at=bias_at)
        gain_kv = sb("gain_kv", [P, CH], at=bias_at + CH * 4)
        krT = sb("krT", [P, KEYS], at=bias_at + 2 * CH * 4)
        krows = sb("krows", [P, 4, ROPE], at=bias_at + (2 * CH + KEYS) * 4)
        swapped = sb("swapped", [P, CH])
        kcache = swapped
        cos0 = sb("cos0", [P, 2, HEAD]); sin0 = sb("sin0", [P, 2, HEAD])
        cos1 = sb("cos1", [P, 2, ROPE]); sin1 = sb("sin1", [P, 2, ROPE])
        mask = sb("mask", [P, GRID_W])
        ident = sb("ident", [P, P])
        gain_q = sb("gain_q", [P, HEAD]); gain_k = sb("gain_k", [P, HEAD])
        vec = sb("vec", [P, P])
        vecT = sb("vecT", [P, 4, KT])
        half_tanh = sb("half_tanh", [P, 2, KT])
        silu_c = sb("silu_c", [P, KT, 32])
        mod = sb("mod", [P, 2, 2, KT])
        ss = sb("ss", [P, 16]); ms = sb("ms", [P, 16]); rstd = sb("rstd", [P, 16])
        mhalf = sb("mhalf", [P, 16])
        nmax = sb("nmax", [P, 4]); rsum = sb("rsum", [P, 4]); rinv = sb("rinv", [P, 4])
        assert top[0] <= nc.sbuf_usable_end, top[0] - nc.sbuf_usable_end
        stage = [st[:, 0], st[:, 1]]
        stage_flat = st[:, :, :, :].rearrange("p a t n -> p (a t n)")
        q_rope = stage[0].rearrange("p t n -> p (t n)")[:, 0:GROUP * NT * ROPE]\
            .rearrange("p (h t d) -> p h t d", h=GROUP, t=NT)
        q_ropeT = stage[1].rearrange("p t n -> p (t n)").rearrange("p (h n) -> p h n", h=GROUP)

        def bank(name):
            return ctx.enter_context(nc.psum_tensor(name, [P, CH], F32))

        G = [bank(f"gemm{i}") for i in range(3)]
        AD = bank("ada_bank")
        S = [bank("scores0"), bank("scores1")]
        TB = bank("turned")
        OB = bank("attended")
        BX = [S[0], S[1], TB, OB]

        raw_in = [sem(f"raw_in{i}") for i in range(RAW_RING)]
        ada_in = [sem(f"ada_in{i}") for i in range(ADA_RING)]
        hi_ready = sem("hi_ready")
        lo_ready = sem("lo_ready")
        w_used = sem("w_used")
        ada_used = sem("ada_used")
        rows_free = sem("rows_free")
        mm_done = sem("mm_done")
        evac = sem("evac")
        t_done = sem("t_done"); t_free = sem("t_free")
        x_done = sem("x_done"); x_free = sem("x_free")
        xhi = sem("xhi")
        h_ready = sem("h_ready"); hhi = sem("hhi"); hlo = sem("hlo")
        s_done = sem("s_done"); mx_ready = sem("mx_ready"); p_ready = sem("p_ready")
        pv_done = sem("pv_done"); o_done = sem("o_done")
        v_own = sem("v_own")
        ss_ready = sem("ss_ready"); ms_ready = sem("ms_ready"); rstd_ready = sem("rstd_ready")
        xn_ready = sem("xn_ready")
        gate_done = sem("gate_done")
        tanh_ready = sem("tanh_ready"); silu_ready = sem("silu_ready")
        x_in = [sem(f"x_in{i}") for i in range(NT)]
        const_in = sem("const_in"); vec_in = sem("vec_in"); rows_in = sem("rows_in")
        set_up = sem("set_up")
        kvn_ready = sem("kvn_ready"); qn_ready = sem("qn_ready"); group_copied = sem("group_copied")
        cache_in = sem("cache_in"); kc_in = sem("kc_in"); vc_in = sem("vc_in")
        bias_in = sem("bias_in"); bias_ready = sem("bias_ready")
        kb_out = sem("kb_out"); vb_out = sem("vb_out"); side_out = sem("side_out")
        rope_ready = sem("rope_ready")
        grow_out = sem("grow_out"); gbc_in = sem("gbc_in"); res_in = sem("res_in")
        res_done = sem("res_done"); x1_out = sem("x1_out"); y_ready = sem("y_ready")
        y_out = sem("y_out"); fn_in = sem("fn_in"); lc_in = sem("lc_in"); table_out = sem("table_out"); gain_in = sem("gain_in")

        x1_dram = nc.dram_tensor("x1_scratch", [P, NT, D], F32, kind="Internal").ap()
        gate_dram = nc.dram_tensor("gate_scratch", [2, 2, D], F32, kind="Internal").ap()
        bias_dram = nc.dram_tensor("bias_scratch", [N_B * GROUP, 2 * P, 2 * P], F32,
                                   kind="Internal").ap()
        block = ctx.enter_context(nc.Block())

        H_ORDER = []
        H_ORDER.append(("q", 0))
        for n in range(UNITS):
            H_ORDER.append(("p", n))
            if n % NT == 1 and n // NT + 1 < GROUP:
                H_ORDER.append(("q", n // NT + 1))
        H_AT = {key: at for at, key in enumerate(H_ORDER)}

        @block.sync
        def _(sp):
            def load_w(w, width=SLOT):
                need(sp, lo_ready, w, 1 - RAW_RING)
                r = w.ring(RAW_RING)
                sp.dma_start(w_raw[:, r, 0:width], t_in["w_all"][w.count(), :, 0:width])\
                    .then_inc(raw_in[r], 16)

            def load_ada(a):
                need(sp, ada_used, a, 1 - ADA_RING)
                r = a.ring(ADA_RING)
                sp.dma_start(ada[:, r, :], t_in["ada_all"][a.count()]).then_inc(ada_in[r], 16)

            first = 2 * HALVES - 2 * ADA_RING
            for j in range(ADA_RING):
                load_ada(At(j))
            with sp.Fori(0, first // ADA_RING - 1) as i:
                for j in range(ADA_RING):
                    load_ada(At(ADA_RING + j, i, ADA_RING))
            for j in range(RAW_RING):
                load_w(At(W_KV + j))
            with sp.Fori(0, 2) as i:
                for j in range(ADA_RING):
                    load_ada(At(first + j, i, ADA_RING))
            for j in range(RAW_RING, SPC):
                load_w(At(W_KV + j))
            with sp.Fori(0, N_A) as i:
                for j in range(2 * SPC):
                    load_w(At(W_A + j, i, 2 * SPC))
                    for half in range(2):
                        load_ada(At(2 * HALVES + 2 * j + half, i, HALVES))
            with sp.Fori(0, N_B) as i:
                for j in range(4 * SPC):
                    load_w(At(W_B + j, i, 4 * SPC))
                    if j % 2 == 0:
                        for half in range(2):
                            load_ada(At((2 + N_A) * HALVES + j + half, i, HALVES))
            with sp.Fori(0, N_OUT) as i:
                for j in range(SPC):
                    load_w(At(W_O0 + j, i, SPC))
            for j in range(W_QL, W_G):
                load_w(At(j))
            with sp.Fori(0, N_GATE) as i:
                for j in range(SPC):
                    load_w(At(W_G + j, i, SPC))
            with sp.Fori(0, N_H) as i:
                for j in range(2 * GROUP):
                    load_w(At(W_H + j, i, 2 * GROUP), GROUP * (HEAD + ROPE) if j % 2 == 0 else SLOT)
            with sp.Fori(0, N_OUT) as i:
                for j in range(SPC):
                    load_w(At(W_O1 + j, i, SPC))

        @block.tensor
        def _(pe):
            def product(out, pairs):
                last = None
                for n, ((ahi, alo), (bhi, blo)) in enumerate(pairs):
                    pe.matmul(out, alo, bhi, start=(n == 0), stop=False)
                    pe.matmul(out, ahi, blo, start=False, stop=False)
                    last = pe.matmul(out, ahi, bhi, start=False, stop=(n == len(pairs) - 1))
                return last

            def split_pair(hi, lo, *index):
                return hi[index], lo[index]

            def chunk_slot(w, j, m, made=None):
                r = w.ring(SPLIT_RING)
                need(pe, lo_ready, w, 1)
                if made is not None:
                    pe.wait_ge(made[0], made[1] + KPS * (j + 1))
                whi = w_hi[:, r, :].rearrange("p (k n) -> p k n", k=KPS)
                wlo = w_lo[:, r, :].rearrange("p (k n) -> p k n", k=KPS)
                for t in range(NT):
                    if j == 0:
                        need(pe, evac, m.plus(t), 1 - NT)
                    rows_t = slice(t * P, (t + 1) * P)
                    for kk in range(KPS):
                        k = KPS * j + kk
                        first, end = (k == 0), (k == KT - 1)
                        ahi, alo = act_hi[:, k, rows_t], act_lo[:, k, rows_t]
                        pe.matmul(G[t][:], alo, whi[:, kk], start=first, stop=False)
                        pe.matmul(G[t][:], ahi, wlo[:, kk], start=False, stop=False)
                        last = pe.matmul(G[t][:], ahi, whi[:, kk], start=False, stop=end)
                    if j == SPC - 1 and t < NT - 1:
                        last.then_inc(mm_done, 1)
                last.then_inc(w_used, 1)

            def ada_k(a, k, third):
                if k == 0:
                    need(pe, rows_free, third)
                for half in range(2):
                    at = a.plus(2 * k + half)
                    landed(pe, ada_in, at)
                    r = at.ring(ADA_RING)
                    for gg in range(2):
                        g = 2 * half + gg
                        last = pe.matmul(AD[32 * g:32 * g + 32, :], silu_c[:, k, :],
                                         ada[:, r, gg * CH:(gg + 1) * CH],
                                         start=(k == 0), stop=(k == KT - 1), tile_position=(0, 32 * g))
                    last.then_inc(ada_used, 1)

            def turn(bank_, parts, width=P, height=P):
                for n, part in enumerate(parts):
                    last = pe.transpose(bank_[0:width, n * height:(n + 1) * height], part,
                                        ident[0:height, 0:height])
                return last

            def turn_out(x, parts, width=P, height=P):
                need(pe, x_free, x, 1 - len(BX))
                turn(BX[x.ring(len(BX))], parts, width, height).then_inc(x_done, 1)

            def turn_in(tau, parts, width=P):
                need(pe, t_free, tau)
                if width == P:
                    last = turn(TB, parts)
                else:
                    for n, part in enumerate(parts):
                        last = pe.matmul(TB[0:width, n * P:(n + 1) * P], part, ident[:])
                last.then_inc(t_done, 1)

            def token_blocks(rows_, col):
                return [rows_[:, t, col:col + P] for t in range(NT)]

            def score(n, h, t, kh, latent=False):
                need(pe, p_ready, n, -1)
                s = S[n.ring(2)]
                keys = slice(0, P) if t == 0 else slice(P, KEYS)
                width = P if t == 0 else 3 * P
                last = pe.matmul(s[:, 0:width], qT[:, h, t * P:(t + 1) * P], kT[:, kh, keys],
                                 start=True, stop=not latent)
                if latent:
                    last = pe.matmul(s[:, 0:width], q_ropeT[0:ROPE, h, t * P:(t + 1) * P],
                                     krT[0:ROPE, keys], start=False, stop=True)
                last.then_inc(s_done, 1)

            def prob_turn(n, t, tau):
                need(pe, p_ready, n, 1)
                blocks = [prob[:, n.ring(3), b * P:(b + 1) * P] for b in range(1 if t == 0 else 3)]
                turn_in(tau, blocks)

            def attend(n, t, tau, values):
                need(pe, t_free, tau, 1)
                need(pe, o_done, n, -3)
                out = OB[:, n.ring(4) * P:(n.ring(4) + 1) * P]
                tiles = [0] if t == 0 else [1, 2, 3]
                for b, kt in enumerate(tiles):
                    last = pe.matmul(out, probT[:, n.ring(2), b * P:(b + 1) * P], values(kt),
                                     start=(b == 0), stop=(b == len(tiles) - 1))
                last.then_inc(pv_done, 1)

            pe.wait_ge(const_in, CONSTS * 16)
            pe.wait_ge(vec_in, 64)
            turn_out(At(X_VEC), [vec[0:4 * KT, :]], P, 4 * KT)
            pe.wait_ge(xn_ready, NT)
            for k in range(KT):
                turn_out(At(X_X0 + k), token_blocks(u, k * P))
            pe.wait_ge(silu_ready, 1)
            with pe.Fori(0, 2) as i:
                for k in range(KT):
                    ada_k(At(0, i, HALVES), k, At(0, i, 1))
            pe.wait_ge(rows_free, 2)
            for which in range(2):
                turn_out(At(X_MOD0 + which), [rows[:, which, j * P:(j + 1) * P] for j in range(4)])
            for j in range(SPC):
                chunk_slot(At(W_KV + j), j, At(M_KV), (hlo, 0))
            with pe.Fori(0, N_A) as i:
                m, tau, n0 = At(M_A, i, 2 * NT), At(T_A, i, T_A_PER), At(N_UA, i, UNITS)
                for j in range(2 * SPC):
                    if j == 2 * SPC - 1:
                        need(pe, t_free, tau, 1 + GROUP)
                        score(n0, 0, 0, 0)
                        score(n0.plus(1), 0, 1, 0)
                    chunk_slot(At(W_A + j, i, 2 * SPC), j % SPC, m.plus(NT * (j // SPC)))
                    ada_k(At(2 * HALVES, i, HALVES), j, At(2, i, 1))
                    if j == 4:
                        need(pe, group_copied, At(2, i, 2))
                        turn_in(tau, [k_group[:, kt, :] for kt in range(4)])
                    if SPC + 3 <= j < SPC + 7:
                        h = j - SPC - 3
                        if h == 0:
                            need(pe, qn_ready, At(NT, i, NT))
                        turn_in(tau.plus(1 + h), token_blocks(stage[0], h * P))
                for n in range(UNITS):
                    t = n % NT
                    prob_turn(n0.plus(n), t, tau.plus(1 + GROUP + n))
                    if n + 2 < UNITS:
                        score(n0.plus(n + 2), (n + 2) // NT, (n + 2) % NT, 0)
                    attend(n0.plus(n), t, tau.plus(1 + GROUP + n), lambda kt: v_group[:, kt, :])
            with pe.Fori(0, N_B) as i:
                m, tau, n0 = At(M_B, i, 4 * NT), At(T_B, i, T_B_PER), At(N_UB, i, UNITS)
                for j in range(4 * SPC):
                    if j == 4 * SPC - 1:
                        need(pe, t_free, tau, 2 * GROUP)
                        score(n0, 0, 0, 0)
                        score(n0.plus(1), 0, 1, 0)
                    chunk_slot(At(W_B + j, i, 4 * SPC), j % SPC, m.plus(NT * (j // SPC)))
                    if j % 2 == 0:
                        ada_k(At((2 + N_A) * HALVES, i, HALVES), j // 2, At(2 + N_A, i, 1))
                    if SPC + 1 <= j < SPC + 5:
                        h = j - SPC - 1
                        need(pe, evac, m, NT)
                        turn_in(tau.plus(h), token_blocks(stage[0], h * P))
                    if 2 * SPC + 1 <= j < 2 * SPC + 5:
                        h = j - 2 * SPC - 1
                        need(pe, evac, m, 2 * NT)
                        need(pe, kc_in, At(16, i, 16))
                        b = token_blocks(stage[1], h * P)
                        turn_in(tau.plus(GROUP + h), [b[0], kcache[:, h * P:(h + 1) * P], b[1], b[2]])
                need(pe, vc_in, At(16, i, 16))
                for n in range(UNITS):
                    t, h = n % NT, n // NT
                    prob_turn(n0.plus(n), t, tau.plus(2 * GROUP + n))
                    if n + 2 < UNITS:
                        score(n0.plus(n + 2), (n + 2) // NT, (n + 2) % NT, (n + 2) // NT)
                    attend(n0.plus(n), t, tau.plus(2 * GROUP + n),
                           lambda kt: v4[:, kt, h * P:(h + 1) * P])
            pe.wait_ge(o_done, N_UH)
            pe.wait_ge(t_free, T_H)
            for k in range(KT):
                turn_out(At(X_U0 + k), token_blocks(u, k * P))
            pe.wait_ge(rows_free, 6)
            for which in range(2):
                turn_out(At(X_MOD1 + which), [rows[:, 3 + which, j * P:(j + 1) * P] for j in range(4)])
            with pe.Fori(0, N_OUT) as i:
                for j in range(SPC):
                    chunk_slot(At(W_O0 + j, i, SPC), j, At(M_O0, i, NT), (x_free, X_U0))
            pe.wait_ge(xn_ready, 2 * NT)
            for k in range(KT):
                turn_out(At(X_X1 + k), token_blocks(u, k * P))
            for c in range(2):
                for j in range(SPC):
                    chunk_slot(At(W_QL + c * SPC + j), j, At(M_QL + c * NT), (hlo, KT))
            w = At(W_KR)
            need(pe, lo_ready, w, 1)
            whi = w_hi[:, w.ring(SPLIT_RING), :].rearrange("p (k n) -> p k n", k=KT)
            wlo = w_lo[:, w.ring(SPLIT_RING), :].rearrange("p (k n) -> p k n", k=KT)
            for t in range(NT):
                rows_t = slice(t * P, (t + 1) * P)
                last = product(AD[:, t * ROPE:(t + 1) * ROPE],
                               [((act_hi[:, k, rows_t], act_lo[:, k, rows_t]), (whi[:, k], wlo[:, k]))
                                for k in range(KT)])
            last.then_inc(w_used, 1)
            with pe.Fori(0, N_GATE) as i:
                for j in range(SPC):
                    chunk_slot(At(W_G + j, i, SPC), j, At(M_G, i, NT))
            pe.wait_ge(qn_ready, N_A * NT + NT)
            for k in range(4):
                turn_out(At(X_QN + k), token_blocks(stage[0], k * P))
            pe.wait_ge(kvn_ready, 2)
            pe.wait_ge(lc_in, 32)
            for k in range(4):
                turn_out(At(X_CKV + k), [v4[:, kt, k * P:(k + 1) * P] for kt in range(4)])
            turn_out(At(X_KR), [krows[:, kt, :] for kt in range(4)], ROPE)
            pe.wait_ge(x_free, X_U1)
            with pe.Fori(0, N_H) as i:
                tau, n0 = At(T_H, i, T_H_PER), At(N_UH, i, UNITS)

                def head_products(h):
                    w = At(W_H + 2 * h, i, 2 * GROUP)
                    m = At(M_H + 4 * h, i, 4 * GROUP)
                    need(pe, lo_ready, w, 1)
                    wq = [x[:, w.ring(SPLIT_RING), 0:4 * (HEAD + ROPE)].rearrange("p (k n) -> p k n", k=4)
                          for x in (w_hi, w_lo)]
                    need(pe, evac, m, 1 - NT)
                    for t in range(NT):
                        rows_t = slice(t * P, (t + 1) * P)
                        last = product(AD[:, t * ROPE:(t + 1) * ROPE],
                                       [((qn_hi[:, k, rows_t], qn_lo[:, k, rows_t]),
                                         (wq[0][:, k, HEAD:], wq[1][:, k, HEAD:])) for k in range(4)])
                    last.then_inc(mm_done, 1)
                    need(pe, evac, m, 2 - NT)
                    product(G[0][:, 0:TOK],
                            [((wq[0][:, k, 0:HEAD], wq[1][:, k, 0:HEAD]), (qn_hi[:, k], qn_lo[:, k]))
                             for k in range(4)]).then_inc(w_used, 1)
                    w = w.plus(1)
                    need(pe, lo_ready, w, 1)
                    wkv = [x[:, w.ring(SPLIT_RING), :].rearrange("p (k n) -> p k n", k=4)
                           for x in (w_hi, w_lo)]
                    need(pe, evac, m, 3 - NT)
                    product(G[1][:],
                            [((wkv[0][:, k, 0:HEAD], wkv[1][:, k, 0:HEAD]), (ckv_hi[:, k], ckv_lo[:, k]))
                             for k in range(4)]).then_inc(mm_done, 1)
                    need(pe, evac, m, 4 - NT)
                    for kt in range(4):
                        rows_t = slice(kt * P, (kt + 1) * P)
                        last = product(G[2][:, rows_t],
                                       [((ckv_hi[:, k, rows_t], ckv_lo[:, k, rows_t]),
                                         (wkv[0][:, k, HEAD:], wkv[1][:, k, HEAD:])) for k in range(4)])
                    last.then_inc(w_used, 1)

                def rope_turn(h):
                    need(pe, rope_ready, At(h + 1, i, GROUP))
                    turn_in(tau.plus(H_AT["q", h]), [q_rope[:, h, t, :] for t in range(NT)], ROPE)

                def head_score(n):
                    h, t = n // NT, n % NT
                    if t == 0:
                        need(pe, evac, At(M_H + 4 * h, i, 4 * GROUP), 3)
                        need(pe, t_free, tau.plus(H_AT["q", h]), 1)
                    score(n0.plus(n), h, t, h, latent=True)

                head_products(0)
                rope_turn(0)
                head_score(0)
                head_score(1)
                for n in range(UNITS):
                    t, h = n % NT, n // NT
                    prob_turn(n0.plus(n), t, tau.plus(H_AT["p", n]))
                    if ("q", h + 1) in H_AT and t == 1:
                        rope_turn(h + 1)
                    if n + 2 < UNITS:
                        head_score(n + 2)
                    need(pe, evac, At(M_H + 4 * h, i, 4 * GROUP), 4)
                    attend(n0.plus(n), t, tau.plus(H_AT["p", n]),
                           lambda kt: v4[:, kt, h * P:(h + 1) * P])
                    if t == 0 and h + 1 < GROUP:
                        head_products(h + 1)
            pe.wait_ge(o_done, N_UH + N_H * UNITS)
            pe.wait_ge(t_free, T_H + N_H * T_H_PER)
            for k in range(KT):
                turn_out(At(X_U1 + k), token_blocks(u, k * P))
            with pe.Fori(0, N_OUT) as i:
                for j in range(SPC):
                    chunk_slot(At(W_O1 + j, i, SPC), j, At(M_O1, i, NT), (x_free, X_U1))

        @block.scalar
        def _(act):
            copy = lambda out, in_, scale=1.0: act.activation(out, in_, ACT.Copy, scale=scale)

            def split_hi(w, width=SLOT):
                landed(act, raw_in, w)
                need(act, w_used, w, 1 - SPLIT_RING)
                copy(w_hi[:, w.ring(SPLIT_RING), 0:width], w_raw[:, w.ring(RAW_RING), 0:width])\
                    .then_inc(hi_ready, 1)

            def act_high(k, base):
                act.wait_ge(h_ready, base + k + 1)
                copy(act_hi[:, k, :], act_f[:, k, :]).then_inc(hhi, 1)

            def turned_high(x, out, width):
                need(act, x_done, x, 1)
                copy(out, BX[x.ring(len(BX))][:, 0:width]).then_inc(xhi, 1)

            def tile_done(m, w, t):
                if t < NT - 1:
                    need(act, mm_done, finished(m), t + 1)
                else:
                    need(act, w_used, w, 1)

            def evacuate(m, w, outs, scale=1.0):
                for t, out in enumerate(outs):
                    tile_done(m, w, t)
                    copy(out, G[t][:], scale).then_inc(evac, 1)

            def evacuate_gate(m, w, col):
                for t in range(NT):
                    tile_done(m, w, t)
                    copy(u[:, t, bass.ds(col, CH)], G[t][:], 0.5)
                    act.activation(stage[1][:, t, :], G[t][:], ACT.Tanh, scale=0.5).then_inc(evac, 1)

            def exponent(n, t):
                width = P if t == 0 else 3 * P
                need(act, mx_ready, n, 1)
                need(act, pv_done, n, -2)
                need(act, o_done, n, -3)
                act.activation(prob[:, n.ring(3), 0:width], S[n.ring(2)][:, 0:width], ACT.Exp,
                               bias=nmax[:, n.ring(4):n.ring(4) + 1],
                               accum_out=rsum[:, n.ring(4):n.ring(4) + 1]).then_inc(p_ready, 1)

            def square_sums(rows_, sizes, at, width, before):
                for t, tile in enumerate(sizes):
                    if before + t > 0:
                        act.wait_ge(ss_ready, before + t)
                    act.activation(stage_flat[:, 0:width], rows_[:, tile, 0:width], ACT.Square,
                                   accum_out=ss[:, at + t:at + t + 1]).then_inc(ss_ready, 1)

            act.dma_start(u[:, 0, :], t_in["x_prompt"][0]).then_inc(x_in[0], 16)
            for t in range(2):
                act.dma_start(u[:, 1 + t, :], t_in["x_sample"][0, t * P:(t + 1) * P, :])\
                    .then_inc(x_in[1 + t], 16)
            act.wait_ge(x_free, X_VEC + 1)
            act.activation(half_tanh[:], vecT[:, 0:2, :], ACT.Tanh, scale=0.5).then_inc(tanh_ready, 1)
            for t in range(NT):
                act.wait_ge(x_in[t], 16)
                square_sums(u, [t], t, D, t)
            split_hi(At(0))
            split_hi(At(1))
            act_high(0, 0)
            act_high(1, 0)
            for j in range(SPC):
                for k in range(2 * j + 2, min(2 * j + 4, KT)):
                    act_high(k, 0)
                if j == SPC - 1:
                    evacuate(At(M_KV), At(W_KV + j), [v4[:, kt, :] for kt in KEY_TILE])
                split_hi(At(W_KV + j + 2))
            act.wait_ge(evac, NT)
            for t in range(NT):
                act.activation(stage[1][:, t, 0:2 * HEAD], v4[:, KEY_TILE[t], 0:2 * HEAD], ACT.Square)\
                    .then_inc(ss_ready, 1)
            with act.Fori(0, N_A) as i:
                m, tau, n0 = At(M_A, i, 2 * NT), At(T_A, i, T_A_PER), At(N_UA, i, UNITS)
                for j in range(2 * SPC):
                    if j == 2:
                        act.wait_ge(kvn_ready, 1)
                        act.wait_ge(cache_in, 32)
                        need(act, t_done, tau)
                        need(act, pv_done, n0)
                        copy(k_group, v4[:, :, bass.ds(i * HEAD, HEAD)]).then_inc(group_copied, 1)
                        copy(v_group, v4[:, :, bass.ds(i * HEAD + 2 * HEAD, HEAD)])\
                            .then_inc(group_copied, 1)
                    if j == SPC - 1:
                        need(act, t_done, tau)
                        evacuate(m, At(W_A + j, i, 2 * SPC), [stage[0][:, t, :] for t in range(NT)])
                        for t in range(NT):
                            need(act, evac, m.plus(t), 1)
                            act.activation(stage[1][:, t, :], stage[0][:, t, :], ACT.Square)\
                                .then_inc(ss_ready, 1)
                    if j == 2 * SPC - 1:
                        exponent(n0, 0)
                        exponent(n0.plus(1), 1)
                        need(act, qn_ready, At(NT, i, NT))
                        evacuate_gate(m.plus(NT), At(W_A + j, i, 2 * SPC), i * CH)
                    split_hi(At(W_A + j + 2, i, 2 * SPC))
                for n in range(2, UNITS):
                    exponent(n0.plus(n), n % NT)
            with act.Fori(0, N_B) as i:
                m, tau, n0 = At(M_B, i, 4 * NT), At(T_B, i, T_B_PER), At(N_UB, i, UNITS)
                for j in range(4 * SPC):
                    w = At(W_B + j, i, 4 * SPC)
                    if j == SPC - 1:
                        need(act, t_done, tau)
                        evacuate(m, w, [stage[0][:, t, :] for t in range(NT)], SC0)
                    if j == 2 * SPC - 1:
                        need(act, o_done, n0)
                        evacuate(m.plus(NT), w, [stage[1][:, t, :] for t in range(NT)])
                    if j == 3 * SPC - 1:
                        need(act, vb_out, At(0, i, 16))
                        evacuate(m.plus(2 * NT), w, [v4[:, kt, :] for kt in KEY_TILE])
                    if j == 4 * SPC - 1:
                        exponent(n0, 0)
                        exponent(n0.plus(1), 1)
                        need(act, kb_out, At(16, i, 16))
                        need(act, t_done, tau, 2 * GROUP)
                        evacuate_gate(m.plus(3 * NT), w, i * CH + N_A * CH)
                    split_hi(w.plus(2))
                for n in range(2, UNITS):
                    exponent(n0.plus(n), n % NT)
            for k in range(KT):
                turned_high(At(X_U0 + k), act_hi[:, k, :], TOK)
            with act.Fori(0, N_OUT) as i:
                for j in range(SPC):
                    if j == SPC - 1:
                        need(act, res_done, At(0, i, NT))
                        evacuate(At(M_O0, i, NT), At(W_O0 + j, i, SPC), [stage[0][:, t, :] for t in range(NT)])
                    split_hi(At(W_O0 + j + 2, i, SPC))
            act.wait_ge(res_done, N_OUT * NT)
            square_sums(u, range(NT), 0, D, SS_AT[2 + N_A] - NT)
            act_high(0, KT)
            act_high(1, KT)
            for c in range(2):
                for j in range(SPC):
                    if c == 0:
                        for k in range(2 * j + 2, min(2 * j + 4, KT)):
                            act_high(k, KT)
                    if j == SPC - 1 and c == 0:
                        evacuate(At(M_QL), At(W_QL + j), [stage[0][:, t, :] for t in range(NT)])
                    if j == SPC - 1 and c == 1:
                        act.wait_ge(vb_out, N_B * 16)
                        evacuate(At(M_QL + NT), At(W_QL + SPC + j), [v4[:, kt, :] for kt in KEY_TILE])
                    split_hi(At(W_QL + c * SPC + j + 2))
            for t in range(NT):
                act.wait_ge(evac, M_QL + 1 + t)
                act.activation(stage[1][:, t, :], stage[0][:, t, :], ACT.Square,
                               accum_out=ss[:, t:t + 1]).then_inc(ss_ready, 1)
            for t in range(NT):
                act.wait_ge(evac, M_QL + NT + 1 + t)
                act.wait_ge(ss_ready, SS_LAT - 2 * NT + 1 + t)
                act.activation(stage[1][:, t, :], v4[:, KEY_TILE[t], :], ACT.Square,
                               accum_out=ss[:, NT + t:NT + t + 1]).then_inc(ss_ready, 1)
            act.wait_ge(w_used, W_KR + 1)
            for t in range(NT):
                last = copy(krows[:, KEY_TILE[t], :], AD[:, t * ROPE:(t + 1) * ROPE])
            last.then_inc(evac, 1)
            split_hi(At(W_G + 1))
            with act.Fori(0, N_GATE) as i:
                for j in range(SPC):
                    if j == SPC - 1:
                        need(act, gate_done, At((N_A + N_B) * NT, i, NT))
                        evacuate_gate(At(M_G, i, NT), At(W_G + j, i, SPC), i * CH)
                    split_hi(At(W_G + j + 2, i, SPC))
            for k in range(4):
                turned_high(At(X_QN + k), qn_hi[:, k, :], TOK)
            for k in range(4):
                turned_high(At(X_CKV + k), ckv_hi[:, k, :], KEYS)
            act.wait_ge(side_out, 64)
            with act.Fori(0, N_H) as i:
                n0 = At(N_UH, i, UNITS)

                def head_rows(h):
                    m, w = At(M_H + 4 * h, i, 4 * GROUP), At(W_H + 2 * h, i, 2 * GROUP)
                    need(act, mm_done, finished(m), 1)
                    copy(q_rope[:, h, :, :], AD[:, 0:NT * ROPE].rearrange("p (t d) -> p t d", t=NT), SC1)\
                        .then_inc(evac, 1)
                    need(act, w_used, w, 1)
                    copy(qT[:, h, :], G[0][:, 0:TOK], SC1).then_inc(evac, 1)
                    split_hi(w.plus(2))
                    need(act, mm_done, finished(m), 2)
                    copy(kT[:, h, :], G[1][:]).then_inc(evac, 1)
                    need(act, w_used, w, 2)
                    copy(v4[:, :, h * P:(h + 1) * P], G[2][:].rearrange("p (t d) -> p t d", t=4))\
                        .then_inc(evac, 1)
                    split_hi(w.plus(3))

                head_rows(0)
                exponent(n0, 0)
                exponent(n0.plus(1), 1)
                for n in range(UNITS):
                    if n + 2 < UNITS:
                        exponent(n0.plus(n + 2), (n + 2) % NT)
                    if n % NT == 0 and n // NT + 1 < GROUP:
                        head_rows(n // NT + 1)
            for k in range(KT):
                turned_high(At(X_U1 + k), act_hi[:, k, :], TOK)

            def out_chunk(i, last=False):
                for j in range(SPC):
                    if j == SPC - 1:
                        need(act, res_done, At(N_OUT * NT, i, NT))
                        evacuate(At(M_O1, i, NT), At(W_O1 + j, i, SPC), [stage[0][:, t, :] for t in range(NT)])
                    if not (last and j >= SPC - 2):
                        split_hi(At(W_O1 + j + 2, i, SPC))

            with act.Fori(0, N_OUT - 1) as i:
                out_chunk(i)
            out_chunk(N_OUT - 1, last=True)
            act.wait_ge(res_done, 2 * N_OUT * NT)
            square_sums(u, range(NT), 0, D, SS_LAT)

        @block.vector
        def _(dve):
            own = Chain(dve, v_own)

            def split_lo(w, width=SLOT):
                need(dve, hi_ready, w, 1)
                r = w.ring(SPLIT_RING)
                dve.tensor_tensor(w_lo[:, r, 0:width], w_raw[:, w.ring(RAW_RING), 0:width],
                                  w_hi[:, r, 0:width].bitcast(F32), ALU.subtract).then_inc(lo_ready, 1)

            def modulate(k, base):
                for v, cols in ((0, slice(0, P)), (1, slice(P, TOK))):
                    last = dve.tensor_scalar(act_f[:, k, cols], act_f[:, k, cols], mod[:, 1, v, k:k + 1],
                                             mod[:, 0, v, k:k + 1], ALU.mult, ALU.add)
                last.then_inc(h_ready, 1)

            def act_low(k, base):
                dve.wait_ge(hhi, base + k + 1)
                dve.tensor_tensor(act_lo[:, k, :], act_f[:, k, :], act_hi[:, k, :].bitcast(F32),
                                  ALU.subtract).then_inc(hlo, 1)

            def tokens_turned(first):
                for k in range(KT):
                    dve.wait_ge(x_done, first + k + 1)
                    dve.tensor_copy(act_f[:, k, :], BX[(first + k) % 4][:, 0:TOK]).then_inc(x_free, 1)

            def modulation(first, third, gain):
                for which in range(2):
                    x = first + which
                    dve.wait_ge(x_done, x + 1)
                    for v in range(2):
                        part = BX[x % 4][:].rearrange("p (j g q) -> p q g j", j=4, g=4)[:, v]
                        out = mod[:, which, v, :].rearrange("p (g j) -> p g j", g=4)
                        if which == 0:
                            ins = dve.tensor_copy(out, part)
                        else:
                            ins = dve.scalar_tensor_tensor(
                                out=out, in0=part, scalar=1.0,
                                in1=vecT[:, gain, :].rearrange("p (g j) -> p g j", g=4),
                                op0=ALU.add, op1=ALU.mult)
                        if v == 0:
                            own.add(ins)
                    ins.then_inc(x_free, 1)
                dve.wait_ge(x_free, first + 2)
                own.sync()

            def add_rows(third_at):
                need(dve, ada_used, At(HALVES * (third_at.fixed + 1), third_at.turn, HALVES * third_at.per))
                rows_at = rows[:, bass.ds(third_at.count(), 1), :].rearrange("p o n -> p (o n)") \
                    if third_at.turn is not None else rows[:, third_at.fixed, :]
                dve.tensor_tensor(rows_at, AD[:], rows_at, ALU.add).then_inc(rows_free, 1)

            powers = [0, None, 0]

            def root(turn, base, width, inverse):
                own.sync()
                dve.tensor_scalar(ms[:, 0:width], ss[:, 0:width], inverse, EPS, ALU.mult, ALU.add)\
                    .then_inc(ms_ready, 1)
                need(dve, rstd_ready, At(base + 1, turn, 1) if turn is not None else At(base + 1))

            def normalise_tokens(power):
                dve.wait_ge(ss_ready, SS_AT[power])
                root(None, power, NT, 1.0 / D)

            def head_norm(x, heads, at, gain):
                r = rstd[:, at:at + heads]
                own.add(dve.tensor_tensor(x, x, spread(r, [[1, heads], [0, HEAD]]), ALU.mult))
                own.sync()
                own.add(dve.tensor_tensor(x, x, spread(gain[:], [[0, heads], [1, HEAD]]), ALU.mult))
                own.sync()

            def rotate(x, heads, width, cos, sin, done=None):
                q = width // 4
                xr = x.rearrange("p h (a s m) -> p h a s m", a=2, s=2)
                sw = swapped[:, 0:heads * width].rearrange("p (h a s m) -> p h a s m", h=heads, a=2, s=2)
                sv = sin.rearrange("p (a s m) -> p a s m", a=2, s=2)
                for s in range(2):
                    tab = sv[:, :, s, :]
                    tab = spread(tab, [[0, heads]] + [list(d) for d in tab.ap[1:]])
                    own.add(dve.tensor_tensor(sw[:, :, :, s, :], xr[:, :, :, 1 - s, :], tab, ALU.mult))
                own.sync()
                own.add(dve.tensor_tensor(x, x, spread(cos, [[0, heads], [1, width]]), ALU.mult))
                own.sync()
                last = dve.tensor_tensor(x, x, swapped[:, 0:heads * width].rearrange("p (h d) -> p h d", h=heads),
                                         ALU.add)
                if done is None:
                    own.add(last)
                    own.sync()
                else:
                    last.then_inc(done, 1)

            def maximum(n, t, h=0, biased=False):
                width = P if t == 0 else 3 * P
                s = S[n.ring(2)]
                need(dve, s_done, n, 1)
                need(dve, p_ready, n, -3)
                if biased and t > 0:
                    own.add(dve.tensor_tensor(
                        s[:, P:3 * P], s[:, P:3 * P],
                        bias[:, h, t - 1, :, :].rearrange("p r c -> p (r c)"), ALU.add))
                    own.sync()
                dve.tensor_reduce(nmax[:, n.ring(4):n.ring(4) + 1], s[:, 0:width], X, ALU.max,
                                  negate=True).then_inc(mx_ready, 1)

            def copy_turned(tau, out, cols, parts=P):
                need(dve, t_done, tau, 1)
                dve.tensor_copy(out, TB[0:parts, 0:cols]).then_inc(t_free, 1)

            def prob_copy(n, t, tau):
                need(dve, pv_done, n, -1)
                width = P if t == 0 else 3 * P
                copy_turned(tau, probT[:, n.ring(2), 0:width], width)

            def output(n, t, col):
                need(dve, p_ready, n, 1)
                own.add(dve.reciprocal(rinv[:, n.ring(4):n.ring(4) + 1], rsum[:, n.ring(4):n.ring(4) + 1]))
                own.sync()
                need(dve, pv_done, n, 1)
                at = u[:, t, bass.ds(col, P)]
                dve.scalar_tensor_tensor(out=at, in0=OB[:, n.ring(4) * P:(n.ring(4) + 1) * P],
                                         scalar=rinv[:, n.ring(4):n.ring(4) + 1], in1=at,
                                         op0=ALU.mult, op1=ALU.mult).then_inc(o_done, 1)

            def finish_gate(m, gates, col):
                for t in range(NT):
                    need(dve, evac, m.plus(t), 1)
                    at = u[:, t, bass.ds(col, CH)]
                    dve.scalar_tensor_tensor(out=at, in0=stage[1][:, t, :], scalar=1.0, in1=at,
                                             op0=ALU.add, op1=ALU.mult).then_inc(gate_done, 1)
                need(dve, gate_done, gates, NT)

            def turned_low(x, hi, out, width, high_at):
                dve.wait_ge(xhi, high_at + 1)
                dve.tensor_tensor(out, BX[x % 4][:, 0:width], hi.bitcast(F32), ALU.subtract)\
                    .then_inc(x_free, 1)

            def residual(i, col):
                for t in range(NT):
                    own.add(dve.tensor_tensor(stage[0][:, t, :], stage[0][:, t, :],
                                              gate_bc[:, min(t, 1), bass.ds(col, CH)], ALU.mult))
                own.sync()
                for t in range(NT):
                    dve.tensor_tensor(u[:, t, bass.ds(col, CH)], stage[0][:, t, :], stage[1][:, t, :],
                                      ALU.add).then_inc(res_done, 1)

            dve.memset(silu_c[:], 0.0).then_inc(set_up, 1)
            dve.memset(mhalf[:], -0.5).then_inc(set_up, 1)
            dve.memset(ms[:], 1.0).then_inc(set_up, 1)
            dve.wait_ge(set_up, 3)
            dve.wait_ge(x_done, X_VEC + 1)
            dve.tensor_copy(vecT[:].rearrange("p a k -> p (a k)"), BX[X_VEC % 4][:, 0:4 * KT])\
                .then_inc(x_free, 1)
            dve.wait_ge(tanh_ready, 1)
            own.add(dve.scalar_tensor_tensor(out=half_tanh[:], in0=half_tanh[:], scalar=1.0,
                                             in1=vecT[:, 0:2, :], op0=ALU.add, op1=ALU.mult))
            own.sync()
            dve.tensor_scalar(silu_c[:, :, 0:2].rearrange("p k v -> p v k"), half_tanh[:], 0.5, None,
                              ALU.mult).then_inc(silu_ready, 1)
            own.add(dve.tensor_scalar(gain_q[:], gain_q[:], SC0, None, ALU.mult))
            normalise_tokens(0)
            for t in range(NT):
                dve.tensor_scalar(u[:, t, :], u[:, t, :], rstd[:, t:t + 1], None, ALU.mult)\
                    .then_inc(xn_ready, 1)
            tokens_turned(X_X0)
            dve.wait_ge(rows_in, 8 * 16)
            add_rows(At(0))
            add_rows(At(1))
            split_lo(At(0))
            split_lo(At(1))
            dve.wait_ge(x_free, X_MOD0)
            modulation(X_MOD0, 0, 2)
            for k in range(2):
                modulate(k, 0)
            for k in range(2):
                act_low(k, 0)
            for j in range(SPC):
                for k in range(2 * j + 2, min(2 * j + 4, KT)):
                    modulate(k, 0)
                for k in range(2 * j + 2, min(2 * j + 4, KT)):
                    act_low(k, 0)
                split_lo(At(W_KV + j + 2))
            dve.wait_ge(ss_ready, 2 * NT)
            for t in range(NT):
                own.add(dve.reduce_sum(ss[:, 2 * t:2 * t + 2],
                                       stage[1][:, t, 0:2 * HEAD].rearrange("p (h d) -> p h d", h=2), X))
            root(None, 1, 2 * NT, 1.0 / HEAD)
            for t in range(NT):
                x = v4[:, KEY_TILE[t], 0:2 * HEAD].rearrange("p (h d) -> p h d", h=2)
                head_norm(x, 2, 2 * t, gain_k)
                if t > 0:
                    rotate(x, 2, HEAD, cos0[:, t - 1, :], sin0[:, t - 1, :])
            dve.memset(ms[:, 15:16], 1.0).then_inc(kvn_ready, 1)
            with dve.Fori(0, N_A) as i:
                m, tau, n0 = At(M_A, i, 2 * NT), At(T_A, i, T_A_PER), At(N_UA, i, UNITS)
                own.enter(i, OWN_A)
                for j in range(2 * SPC):
                    if j == 5:
                        copy_turned(tau, kT[:, 0, :], KEYS)
                    if j == SPC:
                        need(dve, ss_ready, At(3 * NT, i, NT))
                        own.add(dve.reduce_sum(ss[:, 0:NT * GROUP],
                                               stage[1].rearrange("p t (h d) -> p (t h) d", h=GROUP), X))
                        root(i, 2, NT * GROUP, 1.0 / HEAD)
                    if SPC <= j < SPC + 3:
                        t = j - SPC
                        x = stage[0][:, t, :].rearrange("p (h d) -> p h d", h=GROUP)
                        if t == 0:
                            r = rstd[:, 0:GROUP]
                            own.add(dve.tensor_tensor(x, x, spread(r, [[1, GROUP], [0, HEAD]]), ALU.mult))
                            own.sync()
                            dve.tensor_tensor(x, x, spread(gain_q[:], [[0, GROUP], [1, HEAD]]), ALU.mult)\
                                .then_inc(qn_ready, 1)
                        else:
                            head_norm(x, GROUP, t * GROUP, gain_q)
                            rotate(x, GROUP, HEAD, cos0[:, t - 1, :], sin0[:, t - 1, :], qn_ready)
                    if SPC + 4 <= j:
                        h = j - SPC - 4
                        copy_turned(tau.plus(1 + h), qT[:, h, :], TOK)
                    if j == 2 * SPC - 1:
                        maximum(n0, 0)
                        maximum(n0.plus(1), 1)
                    split_lo(At(W_A + j + 2, i, 2 * SPC))
                finish_gate(m.plus(NT), At(0, i, NT), i * CH)
                add_rows(At(2, i, 1))
                for n in range(UNITS):
                    t, h = n % NT, n // NT
                    prob_copy(n0.plus(n), t, tau.plus(1 + GROUP + n))
                    if n + 2 < UNITS:
                        maximum(n0.plus(n + 2), (n + 2) % NT)
                    output(n0.plus(n), t, i * CH + h * P)
                own_a = own.k
            own.leave(N_A)
            with dve.Fori(0, N_B) as i:
                m, tau, n0 = At(M_B, i, 4 * NT), At(T_B, i, T_B_PER), At(N_UB, i, UNITS)
                own.enter(i, OWN_B)
                for j in range(4 * SPC):
                    if SPC + 2 <= j < SPC + 6:
                        copy_turned(tau.plus(j - SPC - 2), qT[:, j - SPC - 2, :], TOK)
                    if 2 * SPC + 2 <= j < 2 * SPC + 6:
                        h = j - 2 * SPC - 2
                        copy_turned(tau.plus(GROUP + h), kT[:, h, :], KEYS)
                    if j == 4 * SPC - 1:
                        add_rows(At(2 + N_A, i, 1))
                        need(dve, bias_ready, At(1, i, 1))
                        maximum(n0, 0, 0, True)
                        maximum(n0.plus(1), 1, 0, True)
                    split_lo(At(W_B + j + 2, i, 4 * SPC))
                finish_gate(m.plus(3 * NT), At(N_A * NT, i, NT), i * CH + N_A * CH)
                for n in range(UNITS):
                    t, h = n % NT, n // NT
                    prob_copy(n0.plus(n), t, tau.plus(2 * GROUP + n))
                    if n + 2 < UNITS:
                        maximum(n0.plus(n + 2), (n + 2) % NT, (n + 2) // NT, True)
                    output(n0.plus(n), t, i * CH + N_A * CH + h * P)
            own.leave(N_B)
            for k in range(KT):
                turned_low(X_U0 + k, act_hi[:, k, :], act_lo[:, k, :], TOK, XH_U0 + k)
            modulation(X_MOD1, 3, 3)
            with dve.Fori(0, N_OUT) as i:
                own.enter(i, NT)
                for j in range(SPC):
                    split_lo(At(W_O0 + j + 2, i, SPC))
                need(dve, evac, At(M_O0 + NT, i, NT))
                dve.wait_ge(gbc_in, 32)
                need(dve, res_in, At(32, i, 32))
                need(dve, x1_out, At(0, i, 16))
                residual(i, i * CH)
            own.leave(N_OUT)
            normalise_tokens(2 + N_A)
            dve.wait_ge(x1_out, N_OUT * 16)
            for t in range(NT):
                dve.tensor_scalar(u[:, t, :], u[:, t, :], rstd[:, t:t + 1], None, ALU.mult)\
                    .then_inc(xn_ready, 1)
            tokens_turned(X_X1)
            dve.wait_ge(x_free, X_X1 + KT)
            for k in range(2):
                modulate(k, KT)
            for k in range(2):
                act_low(k, KT)
            for c in range(2):
                for j in range(SPC):
                    if c == 0:
                        for k in range(2 * j + 2, min(2 * j + 4, KT)):
                            modulate(k, KT)
                        for k in range(2 * j + 2, min(2 * j + 4, KT)):
                            act_low(k, KT)
                    split_lo(At(W_QL + c * SPC + j + 2))
            split_lo(At(W_G + 1))
            dve.wait_ge(ss_ready, SS_LAT)
            dve.wait_ge(gain_in, 32)
            root(None, 3 + N_A, 2 * NT, 1.0 / CH)
            for t in range(NT):
                x = stage[0][:, t, :]
                dve.scalar_tensor_tensor(out=x, in0=x, scalar=rstd[:, t:t + 1], in1=gain_ql[:],
                                         op0=ALU.mult, op1=ALU.mult).then_inc(qn_ready, 1)
            for t in range(NT):
                x = v4[:, KEY_TILE[t], :]
                own.add(dve.scalar_tensor_tensor(out=x, in0=x, scalar=rstd[:, NT + t:NT + t + 1],
                                                 in1=gain_kv[:], op0=ALU.mult, op1=ALU.mult))
            dve.wait_ge(evac, M_KR + 1)
            for t in range(2):
                rotate(krows[:, 2 + t:3 + t, :], 1, ROPE, cos1[:, t, :], sin1[:, t, :])
            dve.memset(ms[:, 15:16], 1.0).then_inc(kvn_ready, 1)
            with dve.Fori(0, N_GATE) as i:
                for j in range(SPC):
                    split_lo(At(W_G + j + 2, i, SPC))
                finish_gate(At(M_G, i, NT), At((N_A + N_B) * NT, i, NT), i * CH)
            for k in range(4):
                turned_low(X_QN + k, qn_hi[:, k, :], qn_lo[:, k, :], TOK, XH_QN + k)
            for k in range(4):
                turned_low(X_CKV + k, ckv_hi[:, k, :], ckv_lo[:, k, :], KEYS, XH_CKV + k)
            dve.wait_ge(x_done, X_KR + 1)
            dve.tensor_copy(krT[0:ROPE, :], BX[X_KR % 4][0:ROPE, :]).then_inc(x_free, 1)
            with dve.Fori(0, N_H) as i:
                tau, n0 = At(T_H, i, T_H_PER), At(N_UH, i, UNITS)
                own.enter(i, OWN_H)

                def head_rows(h):
                    need(dve, evac, At(M_H + 4 * h, i, 4 * GROUP), 1)
                    for t in range(2):
                        rotate(q_rope[:, h, 1 + t:2 + t, :], 1, ROPE, cos1[:, t, :], sin1[:, t, :],
                               rope_ready if t == 1 else None)
                    split_lo(At(W_H + 2 * h + 2, i, 2 * GROUP))
                    split_lo(At(W_H + 2 * h + 3, i, 2 * GROUP))

                def rope_copy(h):
                    copy_turned(tau.plus(H_AT["q", h]), q_ropeT[0:ROPE, h, :], TOK, ROPE)

                head_rows(0)
                rope_copy(0)
                maximum(n0, 0)
                maximum(n0.plus(1), 1)
                for n in range(UNITS):
                    t, h = n % NT, n // NT
                    prob_copy(n0.plus(n), t, tau.plus(H_AT["p", n]))
                    if ("q", h + 1) in H_AT and t == 1:
                        rope_copy(h + 1)
                    if n + 2 < UNITS:
                        maximum(n0.plus(n + 2), (n + 2) % NT)
                    output(n0.plus(n), t, i * CH + h * P)
                    if t == 0 and h + 1 < GROUP:
                        head_rows(h + 1)
            own.leave(N_H)
            for k in range(KT):
                turned_low(X_U1 + k, act_hi[:, k, :], act_lo[:, k, :], TOK, XH_U1 + k)

            def out_chunk(i, last=False):
                for j in range(SPC):
                    if not (last and j >= SPC - 2):
                        split_lo(At(W_O1 + j + 2, i, SPC))
                need(dve, evac, At(M_O1 + NT, i, NT))
                dve.wait_ge(gbc_in, 64)
                need(dve, res_in, At(32 * N_OUT + 16, i, 16))
                residual(i, i * CH)

            with dve.Fori(0, N_OUT - 1) as i:
                own.enter(i, NT)
                out_chunk(i)
            own.leave(N_OUT - 1)
            out_chunk(N_OUT - 1, last=True)
            normalise_tokens(4 + N_A)
            dve.wait_ge(fn_in, 16)
            for t in range(NT):
                dve.scalar_tensor_tensor(out=u[:, t, :], in0=u[:, t, :], scalar=rstd[:, t:t + 1],
                                         in1=fnorm[:], op0=ALU.mult, op1=ALU.mult).then_inc(y_ready, 1)

        @block.gpsimd
        def _(pool):
            def power(at):
                need(pool, ms_ready, at, 1)
                pool.tensor_tensor(rstd[:], ms[:], mhalf[:], ALU.pow).then_inc(rstd_ready, 1)

            def to_all(out, vector, sem_):
                pool.dma_start(out, spread_rows(vector)).then_inc(sem_, 16)

            def spread_rows(vector):
                return bass.AP(vector.tensor, vector.offset, [[0, P]] + [list(d) for d in vector.ap])

            for n, name in enumerate(("c_ctx", "c", "l0_norm", "l1_norm")):
                src = t_in[name]
                src = src[0] if name == "c" else src
                pool.dma_start(vec[KT * n:KT * n + KT, :], src.rearrange("(k p) -> k p", p=P))\
                    .then_inc(vec_in, 16)
            for name, tile in (("ident", ident), ("cos0", cos0), ("sin0", sin0), ("cos1", cos1),
                               ("sin1", sin1), ("mask", mask)):
                pool.dma_start(tile[:], t_in[name]).then_inc(const_in, 16)
            for name, tile in (("l0_q_norm", gain_q), ("l0_k_norm", gain_k)):
                to_all(tile[:], t_in[name], const_in)
            for layer in range(2):
                b = t_in[f"l{layer}_ada_b"]
                for g in range(4):
                    src = bass.AP(b.tensor, b.offset + g * CH, [[0, 32], [D, 3], [1, CH]])
                    pool.dma_start(rows[32 * g:32 * g + 32, 3 * layer:3 * layer + 3, :], src)\
                        .then_inc(rows_in, 16)
            pool.dma_start(v4[:, 1, 0:2 * HEAD], t_in["cache_l0_a_k"][0].rearrange("t h d -> t (h d)"))\
                .then_inc(cache_in, 16)
            pool.dma_start(v4[:, 1, 2 * HEAD:4 * HEAD], t_in["cache_l0_a_v"][0].rearrange("t h d -> t (h d)"))\
                .then_inc(cache_in, 16)
            pool.wait_ge(set_up, 3)
            power(At(0))
            power(At(1))
            pool.wait_ge(kvn_ready, 1)
            pool.dma_start(t_out["a_k"][0].rearrange("t h d -> t (h d)"), v4[:, 0, 0:2 * HEAD])\
                .then_inc(side_out, 16)
            pool.dma_start(t_out["a_v"][0].rearrange("t h d -> t (h d)"), v4[:, 0, 2 * HEAD:4 * HEAD])\
                .then_inc(side_out, 16)
            rpb = t_in["l0_rpb"]
            table = (2 * 8 - 1) * (2 * WIN - 1)
            for h in range(N_B * GROUP):
                for qr in range(4):
                    base = h * table + (7 - qr) * (2 * WIN - 1) + WIN - 1
                    src = bass.AP(rpb.tensor, base, [[2 * WIN - 1, 4], [-1, GRID_W], [1, GRID_W]])
                    pool.dma_start(bias_dram[h, GRID_W * qr:GRID_W * (qr + 1), :]
                                   .rearrange("q (r c) -> r q c", r=4), src).then_inc(table_out, 16)
            with pool.Fori(0, N_A) as i:
                power(At(2, i, 1))
            pool.wait_ge(table_out, 16 * 4 * N_B * GROUP)
            kc = t_in["cache_l0_b_k"][0].rearrange("t h d -> t (h d)")
            vc = t_in["cache_l0_b_v"][0].rearrange("t h d -> t (h d)")
            kb = t_out["b_k"][0].rearrange("t h d -> t (h d)")
            vb = t_out["b_v"][0].rearrange("t h d -> t (h d)")
            pool.wait_ge(side_out, 32)
            for i in range(N_B):
                m, n0 = At(M_B + i * 4 * NT), At(N_UB + i * UNITS)
                need(pool, o_done, n0)
                pool.dma_start(kcache[:], kc[:, bass.ds(i * CH, CH)]).then_inc(kc_in, 16)
                pool.dma_start(v4[:, 1, :], vc[:, bass.ds(i * CH, CH)]).then_inc(vc_in, 16)
                pool.dma_start(bias[:].rearrange("p h q r c -> p (h q) (r c)"),
                               bias_dram.rearrange("h (q p) n -> p (h q) n", p=P)
                               [:, bass.ds(i * 2 * GROUP, 2 * GROUP), :]).then_inc(bias_in, 16)
                pool.wait_ge(bias_in, 16 * (i + 1))
                flat = bias[:].rearrange("p h q r c -> p (h q r) c")
                pool.tensor_tensor(flat, flat, spread(mask[:], [[0, 8 * GROUP], [1, GRID_W]]), ALU.add)\
                    .then_inc(bias_ready, 1)
                need(pool, evac, m, 2 * NT)
                pool.dma_start(kb[:, bass.ds(i * CH, CH)], stage[1][:, 0, :]).then_inc(kb_out, 16)
                need(pool, evac, m, 3 * NT)
                pool.dma_start(vb[:, bass.ds(i * CH, CH)], v4[:, 0, :]).then_inc(vb_out, 16)

            def gate_rows(layer, third, after):
                pool.wait_ge(*after)
                pool.wait_ge(rows_free, 6)
                for v in range(2):
                    pool.dma_start(gate_dram[layer, v].rearrange("(g n) -> g n", g=4),
                                   rows[v:v + 97:32, third, :]).then_inc(grow_out, 16)
                pool.wait_ge(grow_out, 32 * (layer + 1))
                for v in range(2):
                    to_all(gate_bc[:, v, :], gate_dram[layer, v], gbc_in)

            pool.wait_ge(o_done, N_UH)
            for name, tile in (("l1_q_a_norm", gain_ql), ("l1_kv_a_norm", gain_kv)):
                to_all(tile[:], t_in[name], gain_in)
            gate_rows(0, 2, (o_done, N_UH))
            for i in range(N_OUT):
                need(pool, res_done, At(i * NT))
                cols = bass.ds(i * CH, CH)
                pool.dma_start(stage[1][:, 0, :], t_in["x_prompt"][0][:, cols]).then_inc(res_in, 16)
                pool.dma_start(stage[1][:, 1:3, :],
                               t_in["x_sample"][0].rearrange("(t p) n -> p t n", p=P)[:, :, cols])\
                    .then_inc(res_in, 16)
                need(pool, res_done, At(NT + i * NT))
                pool.dma_start(x1_dram[:, :, cols], u[:, :, cols]).then_inc(x1_out, 16)
            power(At(2 + N_A))
            pool.wait_ge(vb_out, N_B * 16)
            pool.dma_start(v4[:, 1, :], t_in["cache_l1_ckv"][0]).then_inc(lc_in, 16)
            pool.dma_start(krows[:, 1, :], t_in["cache_l1_krope"][0]).then_inc(lc_in, 16)
            power(At(3 + N_A))
            pool.wait_ge(kvn_ready, 2)
            pool.dma_start(t_out["ckv"][0], v4[:, 0, :]).then_inc(side_out, 16)
            pool.dma_start(t_out["krope"][0], krows[:, 0, :]).then_inc(side_out, 16)
            gate_rows(1, 5, (o_done, N_UH + N_H * UNITS))
            to_all(fnorm[:], t_in["final_norm"], fn_in)
            for i in range(N_OUT):
                need(pool, res_done, At((N_OUT + i) * NT))
                pool.dma_start(stage[1], x1_dram[:, :, bass.ds(i * CH, CH)]).then_inc(res_in, 16)
            power(At(4 + N_A))
            pool.wait_ge(y_ready, 1)
            pool.dma_start(t_out["y_prompt"][0], u[:, 0, :]).then_inc(y_out, 16)
            for t in range(2):
                pool.wait_ge(y_ready, 2 + t)
                pool.dma_start(t_out["y_sample"][0, t * P:(t + 1) * P, :], u[:, 1 + t, :])\
                    .then_inc(y_out, 16)
            pool.wait_ge(y_out, 48)
            pool.wait_ge(side_out, 64)
            pool.wait_ge(kb_out, N_B * 16)
            pool.wait_ge(vb_out, N_B * 16)
            pool.wait_ge(x1_out, N_OUT * 16)


CONSTS = 8
OWN_A = 1 + 1 + 2 * (2 + 3) + UNITS
OWN_B = 2 * GROUP + UNITS
OWN_H = GROUP * (4 + 3) + UNITS
SS_AT = {0: NT, 2 + N_A: 3 * NT + NT * N_A - NT + NT, 4 + N_A: 0}
SS_AT[2 + N_A] = NT + NT + N_A * NT + NT
SS_LAT = SS_AT[2 + N_A] + 2 * NT
SS_AT[4 + N_A] = SS_LAT + NT


def slots(w, columns):
    out = []
    for c in columns:
        part = w[:, c:c + CH].reshape(KT // KPS, KPS, P, CH)
        out.append(part.transpose(0, 2, 1, 3).reshape(KT // KPS, P, SLOT))
    return out


def lay_out(x):
    f = {k: np.ascontiguousarray(v) for k, v in x.items()}
    kv, qb, gate = 1024, 1536, 4608
    parts = slots(f["l0_w_in"], [kv])
    for g in range(N_A):
        parts += slots(f["l0_w_in"], [g * CH, gate + g * CH])
    for g in range(N_B):
        parts += slots(f["l0_w_in"], [qb + g * CH, qb + 1024 + g * CH, qb + 2048 + g * CH,
                                      gate + (N_A + g) * CH])
    parts += slots(f["l0_w_out"], range(0, D, CH))
    parts += slots(f["l1_w_in"], [0, CH])
    parts.append(f["l1_w_in"][:, 2 * CH:2 * CH + ROPE].reshape(KT, P, ROPE).transpose(1, 0, 2)
                 .reshape(1, P, SLOT))
    parts += slots(f["l1_w_in"], range(2 * CH + ROPE, 2 * CH + ROPE + D, CH))
    qw = f["l1_w_q_b"].reshape(4, P, 16, HEAD + ROPE).transpose(2, 1, 0, 3).reshape(16, P, 4 * (HEAD + ROPE))
    kvw = f["l1_w_kv_b"].reshape(4, P, 16, 2 * HEAD).transpose(2, 1, 0, 3).reshape(16, P, SLOT)
    heads = np.zeros((16, 2, P, SLOT), np.float32)
    heads[:, 0, :, :4 * (HEAD + ROPE)] = qw
    heads[:, 1] = kvw
    parts.append(heads.reshape(32, P, SLOT))
    parts += slots(f["l1_w_out"], range(0, D, CH))
    arrays = {"w_all": np.concatenate(parts)}
    assert len(arrays["w_all"]) == W_END
    arrays["ada_all"] = np.stack([f["l0_ada_w"], f["l1_ada_w"]]).reshape(2, KT, P, 3, 2, SLOT)\
        .transpose(0, 3, 1, 4, 2, 5).reshape(6 * HALVES, P, SLOT)
    for name in NAMES:
        arrays[name] = f[name]
    token = np.arange(2 * P)
    for n, width in ((0, HEAD), (1, ROPE)):
        a = width // 2
        inv = (1.0 / (np.float32(10000.0) ** (np.arange(a // 2, dtype=np.float32) * np.float32(2.0) / np.float32(a)))).astype(np.float32)
        angles = [(np.float32(1) * pos.astype(np.float32))[:, None] * inv for pos in (token // GRID_W, token % GRID_W)]
        cos = np.concatenate([np.tile(np.cos(g), (1, 2)) for g in angles], 1)
        sin = np.concatenate([np.concatenate([-np.sin(g), np.sin(g)], 1) for g in angles], 1)
        for name, table in (("cos", cos), ("sin", sin)):
            arrays[f"{name}{n}"] = np.ascontiguousarray(
                table.astype(np.float32).reshape(2, P, width).transpose(1, 0, 2))
    col = np.arange(P)[:, None] % GRID_W
    start = np.clip(col - WIN // 2, 0, GRID_W - WIN)
    key = np.arange(GRID_W)[None]
    arrays["mask"] = np.where((key >= start) & (key < start + WIN), 0.0, -1e30).astype(np.float32)
    arrays["ident"] = np.eye(P, dtype=np.float32)
    return arrays


NAMES = ["x_prompt", "x_sample", "cache_l0_a_k", "cache_l0_a_v", "cache_l0_b_k", "cache_l0_b_v",
         "cache_l1_ckv", "cache_l1_krope", "c", "c_ctx", "l0_norm", "l0_ada_b", "l0_q_norm",
         "l0_k_norm", "l0_rpb", "l1_norm", "l1_ada_b", "l1_q_a_norm", "l1_kv_a_norm", "final_norm"]
OUTS = [("y_prompt", (1, P, D)), ("y_sample", (1, 2 * P, D)), ("a_k", (1, P, 2, HEAD)),
        ("a_v", (1, P, 2, HEAD)), ("b_k", (1, P, 8, HEAD)), ("b_v", (1, P, 8, HEAD)),
        ("ckv", (1, P, CH)), ("krope", (1, P, ROPE))]


def kernel(**inputs):
    from concourse import bacc
    from concourse.bass_utils import run_bass_kernel_spmd

    nc = bacc.Bacc("TRN2", target_bir_lowering=False, num_devices=1)
    arrays = lay_out(inputs)
    t_in = {n: nc.dram_tensor(f"in_{n}", a.shape, F32, kind="ExternalInput").ap()
            for n, a in arrays.items()}
    t_out = {n: nc.dram_tensor(f"out_{n}", s, F32, kind="ExternalOutput").ap() for n, s in OUTS}
    build(nc, t_in, t_out)
    r = run_bass_kernel_spmd(nc, [{f"in_{n}": a for n, a in arrays.items()}], core_ids=[0])
    return tuple(r.results[0][f"out_{n}"] for n, _ in OUTS)
```

```python
from contextlib import ExitStack

import numpy as np

import concourse.bass as bass
from concourse import mybir

F32 = mybir.dt.float32
F32R = mybir.dt.float32r
ALU = mybir.AluOpType
ACT = mybir.ActivationFunctionType
X = mybir.AxisListType.X

P = 128
D = 2048
KT = D // P
CH = 512
NT = 3
TOK = NT * P
KEYS = 4 * P
KEY_TILE = [0, 2, 3]
GRID_W = 64
WIN = 16
HEAD = 128
ROPE = 64
SLOT = 1024
SPC = KT * CH // SLOT
KPS = SLOT // CH
RAW_RING, SPLIT_RING, ADA_RING = 4, 2, 8
HALVES = 2 * KT
EPS = 1e-6
SC0 = HEAD ** -0.5
SC1 = (HEAD + ROPE) ** -0.5
GROUP = 4
UNITS = GROUP * NT
PAIR_SLOTS = 4
PAIR_EVAC = 6
PAIR_UNITS = 2 * NT

N_A, N_B, N_OUT, N_GATE, N_H = 2, 2, D // CH, D // CH, 4
W_KV = 0
W_A = W_KV + SPC
W_B = W_A + N_A * 2 * SPC
W_O0 = W_B + N_B * 4 * SPC
W_QL = W_O0 + N_OUT * SPC
W_KR = W_QL + 2 * SPC
W_G = W_KR + 1
W_H = W_G + N_GATE * SPC
W_O1 = W_H + N_H * 2 * PAIR_SLOTS
W_END = W_O1 + N_OUT * SPC
M_KV = 0
M_A = M_KV + NT
M_B = M_A + N_A * 2 * NT
M_O0 = M_B + N_B * 4 * NT
M_QL = M_O0 + N_OUT * NT
M_KR = M_QL + 2 * NT
M_G = M_KR + 1
M_H = M_G + N_GATE * NT
M_O1 = M_H + N_H * 2 * PAIR_EVAC
M_END = M_O1 + N_OUT * NT
T_A_PER = 1 + GROUP + UNITS
T_B_PER = 2 * GROUP + UNITS
T_H_PER = UNITS
T_A = 1
T_B = T_A + N_A * T_A_PER
T_H = T_B + N_B * T_B_PER
X_VEC = 0
X_X0 = X_VEC + 1
X_MOD0 = X_X0 + KT
X_U0 = X_MOD0 + 2
X_MOD1 = X_U0 + KT
X_X1 = X_MOD1 + 2
X_KROW = X_X1 + KT
X_QN = X_KROW + 1
X_CKV = X_QN + 4
X_KR = X_CKV + 4
X_U1 = X_KR + 1
X_END = X_U1 + KT
XH_U0, XH_QN, XH_CKV, XH_U1 = 0, KT, KT + 4, KT + 8
N_UA = 4
N_UB = N_UA + N_A * UNITS
N_UH = N_UB + N_B * UNITS
RES_0, ROWS_0 = 1, 1


MM_G = 2 * (M_KR - M_KV) // NT
MM_H = MM_G + 2 * N_GATE
MM_O1 = MM_H + N_H * 2 * PAIR_SLOTS


class At:

    def __init__(self, fixed, turn=None, per=0):
        self.fixed, self.turn, self.per = fixed, turn, per

    def plus(self, k):
        return At(self.fixed + k, self.turn, self.per)

    def count(self, off=0):
        c = self.fixed + off
        return c if self.turn is None else self.turn * self.per + c

    def ring(self, n):
        assert self.per % n == 0
        return self.fixed % n

    def lap(self, n):
        c = self.fixed // n
        return c if self.turn is None else self.turn * (self.per // n) + c


def finished(m):
    for start, base in ((M_O1, MM_O1), (M_G, MM_G), (M_KV, 0)):
        if m.fixed >= start:
            return At(base + 2 * ((m.fixed - start) // NT), m.turn, 2 * m.per // NT)


def need(eng, sem, at, off=0):
    if at.turn is None:
        if at.fixed + off > 0:
            eng.wait_ge(sem, at.fixed + off)
    else:
        assert at.fixed + off > 0
        eng.wait_ge(sem, at.count(off))


def landed(eng, sems, at):
    n = len(sems)
    lap = at.lap(n)
    eng.wait_ge(sems[at.ring(n)], lap * 16 + 16)


class Pair:

    def __init__(self, index, turn=None):
        def at(start, per):
            return At(start + index * per, turn, 2 * per)

        self.index, self.turn, self.parity = index, turn, index % 2
        self.w, self.m, self.mm = at(W_H, PAIR_SLOTS), at(M_H, PAIR_EVAC), at(MM_H, PAIR_SLOTS)
        self.r, self.n = at(0, 2), at(N_UH, PAIR_UNITS)
        self.before = Pair(index - 1, turn) if index > 0 else None

    def column(self, h):
        fixed = (2 * self.index + h) * P
        return fixed if self.turn is None else self.turn * (4 * P) + fixed


class Chain:

    def __init__(self, eng, sem):
        self.eng, self.sem, self.at, self.k = eng, sem, At(0), 0

    def add(self, ins):
        ins.then_inc(self.sem, 1)
        self.k += 1

    def sync(self):
        self.eng.wait_ge(self.sem, self.at.count(self.k))

    def enter(self, turn, per):
        self.at, self.k = At(self.at.fixed + self.k, turn, per), 0

    def leave(self, turns):
        assert self.k == self.at.per, (self.k, self.at.per)
        self.at, self.k = At(self.at.fixed + turns * self.k), 0


def spread(ap, dims):
    return bass.AP(ap.tensor, ap.offset, [list(ap.ap[0])] + dims)


def build(nc, t_in, t_out):
    ctx = ExitStack()
    with ctx:
        top = [(nc.sbuf_base + 63) // 64 * 64]

        def sb(name, shape, dt=F32, at=None):
            size = int(np.prod(shape[1:])) * 4
            offset = top[0] if at is None else at
            if at is None:
                top[0] += (size + 31) // 32 * 32
            return nc.alloc_sbuf_tensor_at(name, [P] + list(shape[1:]), dt, offset=offset)

        def sem(name):
            return ctx.enter_context(nc.semaphore(name))

        act_hi = sb("act_hi", [P, KT, TOK], F32R)
        lo_at = top[0]
        act_lo = sb("act_lo", [P, KT, TOK], F32R)
        act_f = sb("act_f", [P, KT, TOK], F32, at=lo_at)
        u = sb("u", [P, NT, D])
        w_raw = sb("w_raw", [P, RAW_RING, SLOT])
        w_hi = sb("w_hi", [P, SPLIT_RING, SLOT], F32R)
        w_lo = sb("w_lo", [P, SPLIT_RING, SLOT], F32R)
        ada_at = top[0]
        ada = sb("ada", [P, ADA_RING, SLOT])
        gate_bc = sb("gate_bc", [P, 2, D], F32, at=ada_at)
        fnorm = sb("fnorm", [P, D], F32, at=ada_at + 2 * D * 4)
        ckv_hi = sb("ckv_hi", [P, 4, KEYS], F32R, at=ada_at)
        ckv_lo = sb("ckv_lo", [P, 4, KEYS], F32R, at=ada_at + 4 * KEYS * 4)
        qn_hi = sb("qn_hi", [P, 4, TOK], F32R, at=ada_at + 8 * KEYS * 4)
        qn_lo = sb("qn_lo", [P, 4, TOK], F32R, at=ada_at + 8 * KEYS * 4 + 4 * TOK * 4)
        rope_q = sb("rope_q", [P, TOK], at=ada_at + 8 * (KEYS + TOK) * 4)
        st = sb("st", [P, 2, NT, CH])
        qT = sb("qT", [P, GROUP, TOK])
        kT = sb("kT", [P, GROUP, KEYS])
        k_group = kT[:, 1, :].rearrange("p (t d) -> p t d", t=4)
        v_group = kT[:, 2, :].rearrange("p (t d) -> p t d", t=4)
        v4 = sb("v4", [P, 4, CH])
        prob = sb("prob", [P, 3, 3 * P])
        probT = sb("probT", [P, 2, 3 * P])
        rows = sb("rows", [P, 6, CH])
        bias_at = top[0]
        bias = sb("bias", [P, GROUP, 2, 4, GRID_W])
        gain_ql = sb("gain_ql", [P, CH], at=bias_at)
        gain_kv = sb("gain_kv", [P, CH], at=bias_at + CH * 4)
        krot = qT[:, 0, :]
        krT = sb("krT", [P, KEYS], at=bias_at + 2 * CH * 4)
        krows = sb("krows", [P, 4, 2, ROPE], at=bias_at + (2 * CH + KEYS) * 4)
        swapped = sb("swapped", [P, CH])
        kcache = swapped
        cos0 = sb("cos0", [P, 2, HEAD]); sin0 = sb("sin0", [P, 2, HEAD])
        cos1 = sb("cos1", [P, 2, ROPE]); sin1 = sb("sin1", [P, 2, ROPE])
        mask = sb("mask", [P, GRID_W])
        ident = sb("ident", [P, P])
        gain_q = sb("gain_q", [P, HEAD]); gain_k = sb("gain_k", [P, HEAD])
        vec = sb("vec", [P, P])
        vecT = sb("vecT", [P, 4, KT])
        half_tanh = sb("half_tanh", [P, 2, KT])
        silu_c = sb("silu_c", [P, KT, 32])
        mod = sb("mod", [P, 2, 2, KT])
        ss = sb("ss", [P, 16]); ms = sb("ms", [P, 16]); rstd = sb("rstd", [P, 16])
        mhalf = sb("mhalf", [P, 16])
        begun = sb("begun", [P, 32])
        nmax = sb("nmax", [P, 4]); rsum = sb("rsum", [P, 4]); rinv = sb("rinv", [P, 4])
        assert top[0] <= nc.sbuf_usable_end, top[0] - nc.sbuf_usable_end
        stage = [st[:, 0], st[:, 1]]
        stage_flat = st[:, :, :, :].rearrange("p a t n -> p (a t n)")
        q_turned = stage[1].rearrange("p t n -> p (t n)").rearrange("p (h n) -> p h n", h=GROUP)

        def bank(name):
            return ctx.enter_context(nc.psum_tensor(name, [P, CH], F32))

        G = [bank(f"gemm{i}") for i in range(3)]
        AD = bank("ada_bank")
        S = [bank("scores0"), bank("scores1")]
        TB = bank("turned")
        OB = bank("attended")
        BX = [S[0], S[1], TB, OB]
        PAIR_BANKS = G + [AD]

        raw_in = [sem(f"raw_in{i}") for i in range(RAW_RING)]
        ada_in = [sem(f"ada_in{i}") for i in range(ADA_RING)]
        hi_ready = sem("hi_ready")
        lo_ready = sem("lo_ready")
        w_used = sem("w_used")
        ada_used = sem("ada_used")
        rows_free = sem("rows_free")
        mm_done = sem("mm_done")
        evac = sem("evac")
        t_done = sem("t_done"); t_free = sem("t_free")
        x_done = sem("x_done"); x_free = sem("x_free")
        xhi = sem("xhi")
        h_ready = sem("h_ready"); hhi = sem("hhi"); hlo = sem("hlo")
        s_done = sem("s_done"); mx_ready = sem("mx_ready"); p_ready = sem("p_ready")
        pv_done = sem("pv_done"); o_done = sem("o_done")
        v_own = sem("v_own")
        ss_ready = sem("ss_ready"); ms_ready = sem("ms_ready"); rstd_ready = sem("rstd_ready")
        xn_ready = sem("xn_ready")
        gate_done = sem("gate_done")
        tanh_ready = sem("tanh_ready"); silu_ready = sem("silu_ready")
        x_in = [sem(f"x_in{i}") for i in range(NT)]
        const_in = sem("const_in"); vec_in = sem("vec_in"); rows_in = sem("rows_in")
        set_up = sem("set_up")
        kvn_ready = sem("kvn_ready"); qn_ready = sem("qn_ready"); group_copied = sem("group_copied")
        cache_in = sem("cache_in"); kc_in = sem("kc_in"); vc_in = sem("vc_in")
        bias_in = sem("bias_in"); bias_ready = sem("bias_ready")
        kb_out = sem("kb_out"); vb_out = sem("vb_out"); side_out = sem("side_out")
        rope_ready = sem("rope_ready")
        grow_out = sem("grow_out"); gbc_in = sem("gbc_in"); res_in = sem("res_in")
        res_done = sem("res_done"); x1_out = sem("x1_out"); y_ready = sem("y_ready")
        y_out = sem("y_out"); fn_in = sem("fn_in"); lc_in = sem("lc_in"); table_out = sem("table_out"); gain_in = sem("gain_in")

        x1_dram = nc.dram_tensor("x1_scratch", [P, NT, D], F32, kind="Internal").ap()
        gate_dram = nc.dram_tensor("gate_scratch", [2, 2, D], F32, kind="Internal").ap()
        bias_dram = nc.dram_tensor("bias_scratch", [N_B * GROUP, 2 * P, 2 * P], F32,
                                   kind="Internal").ap()
        block = ctx.enter_context(nc.Block())

        def load_step(c):
            return (0, 0, 1, 1, 2, 3, 4, 5)[c]

        def evac_of(pair, c):
            return pair.plus((0, None, 1, None, 2, 3, 4, 5)[c])

        @block.sync
        def _(sp):
            def load_w(w):
                need(sp, lo_ready, w, 1 - RAW_RING)
                r = w.ring(RAW_RING)
                sp.dma_start(w_raw[:, r, :], t_in["w_all"][w.count()])\
                    .then_inc(raw_in[r], 16)

            def load_ada(a):
                need(sp, ada_used, a, 1 - ADA_RING)
                r = a.ring(ADA_RING)
                sp.dma_start(ada[:, r, :], t_in["ada_all"][a.count()]).then_inc(ada_in[r], 16)

            first = 2 * HALVES - 2 * ADA_RING
            for n, name in enumerate(("c_ctx", "c", "l0_norm", "l1_norm")):
                src = t_in[name]
                src = src[0] if name == "c" else src
                sp.dma_start(vec[KT * n:KT * n + KT, :], src.rearrange("(k p) -> k p", p=P))\
                    .then_inc(vec_in, 16)
            sp.dma_start(ident[:], t_in["ident"]).then_inc(vec_in, 16)
            for j in range(ADA_RING):
                load_ada(At(j))
            with sp.Fori(0, first // ADA_RING - 1) as i:
                for j in range(ADA_RING):
                    load_ada(At(ADA_RING + j, i, ADA_RING))
            for j in range(RAW_RING):
                load_w(At(W_KV + j))
            with sp.Fori(0, 2) as i:
                for j in range(ADA_RING):
                    load_ada(At(first + j, i, ADA_RING))
            for j in range(RAW_RING, SPC):
                load_w(At(W_KV + j))
            with sp.Fori(0, N_A) as i:
                for j in range(2 * SPC):
                    load_w(At(W_A + j, i, 2 * SPC))
                    for half in range(2):
                        load_ada(At(2 * HALVES + 2 * j + half, i, HALVES))
            with sp.Fori(0, N_B) as i:
                for j in range(4 * SPC):
                    load_w(At(W_B + j, i, 4 * SPC))
                    if j % 2 == 0:
                        for half in range(2):
                            load_ada(At((2 + N_A) * HALVES + j + half, i, HALVES))
            with sp.Fori(0, N_OUT) as i:
                for j in range(SPC):
                    load_w(At(W_O0 + j, i, SPC))
            for j in range(W_QL, W_G):
                load_w(At(j))
            with sp.Fori(0, N_GATE) as i:
                for j in range(SPC):
                    load_w(At(W_G + j, i, SPC))
            with sp.Fori(0, N_H) as i:
                for j in range(2 * PAIR_SLOTS):
                    load_w(At(W_H + j, i, 2 * PAIR_SLOTS))
            with sp.Fori(0, N_OUT) as i:
                for j in range(SPC):
                    load_w(At(W_O1 + j, i, SPC))

        @block.tensor
        def _(pe):
            def product(out, pairs):
                last = None
                for n, ((ahi, alo), (bhi, blo)) in enumerate(pairs):
                    pe.matmul(out, alo, bhi, start=(n == 0), stop=False)
                    pe.matmul(out, ahi, blo, start=False, stop=False)
                    last = pe.matmul(out, ahi, bhi, start=False, stop=(n == len(pairs) - 1))
                return last

            def split_pair(hi, lo, *index):
                return hi[index], lo[index]

            def chunk_slot(w, j, m, made=None):
                r = w.ring(SPLIT_RING)
                need(pe, lo_ready, w, 1)
                if made is not None:
                    pe.wait_ge(made[0], made[1] + KPS * (j + 1))
                whi = w_hi[:, r, :].rearrange("p (k n) -> p k n", k=KPS)
                wlo = w_lo[:, r, :].rearrange("p (k n) -> p k n", k=KPS)
                for t in range(NT):
                    if j == 0:
                        need(pe, evac, m.plus(t), 1 - NT)
                    rows_t = slice(t * P, (t + 1) * P)
                    for kk in range(KPS):
                        k = KPS * j + kk
                        first, end = (k == 0), (k == KT - 1)
                        ahi, alo = act_hi[:, k, rows_t], act_lo[:, k, rows_t]
                        pe.matmul(G[t][:], alo, whi[:, kk], start=first, stop=False)
                        pe.matmul(G[t][:], ahi, wlo[:, kk], start=False, stop=False)
                        last = pe.matmul(G[t][:], ahi, whi[:, kk], start=False, stop=end)
                    if j == SPC - 1 and t < NT - 1:
                        last.then_inc(mm_done, 1)
                last.then_inc(w_used, 1)

            def ada_k(a, k, third):
                if k == 0:
                    need(pe, rows_free, third)
                for half in range(2):
                    at = a.plus(2 * k + half)
                    landed(pe, ada_in, at)
                    r = at.ring(ADA_RING)
                    for gg in range(2):
                        g = 2 * half + gg
                        last = pe.matmul(AD[32 * g:32 * g + 32, :], silu_c[:, k, :],
                                         ada[:, r, gg * CH:(gg + 1) * CH],
                                         start=(k == 0), stop=(k == KT - 1), tile_position=(0, 32 * g))
                    last.then_inc(ada_used, 1)

            def turn(bank_, parts, width=P, height=P):
                for n, part in enumerate(parts):
                    last = pe.transpose(bank_[0:width, n * height:(n + 1) * height], part,
                                        ident[0:height, 0:height])
                return last

            def turn_out(x, parts, width=P, height=P):
                need(pe, x_free, x, 1 - len(BX))
                turn(BX[x.ring(len(BX))], parts, width, height).then_inc(x_done, 1)

            def turn_in(tau, parts):
                need(pe, t_free, tau)
                turn(TB, parts).then_inc(t_done, 1)

            def token_blocks(rows_, col):
                return [rows_[:, t, col:col + P] for t in range(NT)]

            def turned_chunk(x, w, m, made):
                for k in range(2 * KPS):
                    turn_out(At(x + k), token_blocks(u, k * P))
                for j in range(SPC):
                    chunk_slot(At(w + j), j, At(m), made)
                    for k in range(KPS * (j + 2), min(KPS * (j + 3), KT)):
                        turn_out(At(x + k), token_blocks(u, k * P))

            def score(n, h, t, kh, latent=False):
                need(pe, p_ready, n, -1)
                s = S[n.ring(2)]
                keys = slice(0, P) if t == 0 else slice(P, KEYS)
                width = P if t == 0 else 3 * P
                last = pe.matmul(s[:, 0:width], qT[:, h, t * P:(t + 1) * P], kT[:, kh, keys],
                                 start=True, stop=not latent)
                if latent:
                    last = pe.matmul(s[:, 0:width], q_turned[:, h, t * P:(t + 1) * P],
                                     krT[:, keys], start=False, stop=True)
                last.then_inc(s_done, 1)

            def prob_turn(n, t, tau):
                need(pe, p_ready, n, 1)
                blocks = [prob[:, n.ring(3), b * P:(b + 1) * P] for b in range(1 if t == 0 else 3)]
                turn_in(tau, blocks)

            def attend(n, t, tau, values):
                need(pe, t_free, tau, 1)
                need(pe, o_done, n)
                out = OB[:, n.ring(4) * P:(n.ring(4) + 1) * P]
                tiles = [0] if t == 0 else [1, 2, 3]
                for b, kt in enumerate(tiles):
                    last = pe.matmul(out, probT[:, n.ring(2), b * P:(b + 1) * P], values(kt),
                                     start=(b == 0), stop=(b == len(tiles) - 1))
                last.then_inc(pv_done, 1)

            pe.wait_ge(vec_in, 80)
            turn_out(At(X_VEC), [vec[0:4 * KT, :]], P, 4 * KT)
            pe.wait_ge(silu_ready, 1)
            for k in range(KT):
                ada_k(At(0), k, At(ROWS_0))
            pe.wait_ge(xn_ready, NT)
            for k in range(KT):
                turn_out(At(X_X0 + k), token_blocks(u, k * P))
            for k in range(KT):
                ada_k(At(HALVES), k, At(ROWS_0 + 1))
            pe.wait_ge(rows_free, ROWS_0 + 2)
            for which in range(2):
                turn_out(At(X_MOD0 + which), [rows[:, which, j * P:(j + 1) * P] for j in range(4)])
            for j in range(SPC):
                chunk_slot(At(W_KV + j), j, At(M_KV), (hlo, 0))
            with pe.Fori(0, N_A) as i:
                m, tau, n0 = At(M_A, i, 2 * NT), At(T_A, i, T_A_PER), At(N_UA, i, UNITS)
                for j in range(2 * SPC):
                    if j == 2 * SPC - 1:
                        need(pe, t_free, tau, 1 + GROUP)
                        score(n0, 0, 0, 0)
                        score(n0.plus(1), 0, 1, 0)
                    chunk_slot(At(W_A + j, i, 2 * SPC), j % SPC, m.plus(NT * (j // SPC)))
                    ada_k(At(2 * HALVES, i, HALVES), j, At(ROWS_0 + 2, i, 1))
                    if j == 4:
                        need(pe, group_copied, At(2, i, 2))
                        turn_in(tau, [k_group[:, kt, :] for kt in range(4)])
                    if SPC + 3 <= j < SPC + 7:
                        h = j - SPC - 3
                        if h == 0:
                            need(pe, qn_ready, At(NT, i, NT))
                        turn_in(tau.plus(1 + h), token_blocks(stage[0], h * P))

                def attend_a(n):
                    attend(n0.plus(n), n % NT, tau.plus(1 + GROUP + n), lambda kt: v_group[:, kt, :])

                for n in range(UNITS):
                    prob_turn(n0.plus(n), n % NT, tau.plus(1 + GROUP + n))
                    if n + 2 < UNITS:
                        score(n0.plus(n + 2), (n + 2) // NT, (n + 2) % NT, 0)
                    if n > 0:
                        attend_a(n - 1)
                attend_a(UNITS - 1)
            with pe.Fori(0, N_B) as i:
                m, tau, n0 = At(M_B, i, 4 * NT), At(T_B, i, T_B_PER), At(N_UB, i, UNITS)
                for j in range(4 * SPC):
                    if j == 4 * SPC - 1:
                        need(pe, t_free, tau, 2 * GROUP)
                        score(n0, 0, 0, 0)
                        score(n0.plus(1), 0, 1, 0)
                    chunk_slot(At(W_B + j, i, 4 * SPC), j % SPC, m.plus(NT * (j // SPC)))
                    if j % 2 == 0:
                        ada_k(At((2 + N_A) * HALVES, i, HALVES), j // 2, At(ROWS_0 + 2 + N_A, i, 1))
                    if SPC + 1 <= j < SPC + 5:
                        h = j - SPC - 1
                        need(pe, evac, m, NT)
                        turn_in(tau.plus(h), token_blocks(stage[0], h * P))
                    if 2 * SPC + 1 <= j < 2 * SPC + 5:
                        h = j - 2 * SPC - 1
                        need(pe, evac, m, 2 * NT)
                        need(pe, kc_in, At(16, i, 16))
                        b = token_blocks(stage[1], h * P)
                        turn_in(tau.plus(GROUP + h), [b[0], kcache[:, h * P:(h + 1) * P], b[1], b[2]])
                need(pe, vc_in, At(16, i, 16))

                def attend_b(n):
                    h = n // NT
                    attend(n0.plus(n), n % NT, tau.plus(2 * GROUP + n),
                           lambda kt: v4[:, kt, h * P:(h + 1) * P])

                for n in range(UNITS):
                    prob_turn(n0.plus(n), n % NT, tau.plus(2 * GROUP + n))
                    if n + 2 < UNITS:
                        score(n0.plus(n + 2), (n + 2) // NT, (n + 2) % NT, (n + 2) // NT)
                    if n > 0:
                        attend_b(n - 1)
                attend_b(UNITS - 1)
            pe.wait_ge(o_done, N_UH)
            pe.wait_ge(t_free, T_H)
            turned_chunk(X_U0, W_O0, M_O0, (x_free, X_U0))
            pe.wait_ge(rows_free, ROWS_0 + 6)
            for which in range(2):
                turn_out(At(X_MOD1 + which), [rows[:, 3 + which, j * P:(j + 1) * P] for j in range(4)])
            with pe.Fori(0, N_OUT - 1) as i:
                for j in range(SPC):
                    chunk_slot(At(W_O0 + SPC + j, i, SPC), j, At(M_O0 + NT, i, NT))
            pe.wait_ge(xn_ready, 2 * NT)
            turned_chunk(X_X1, W_QL, M_QL, (hlo, KT))
            for j in range(SPC):
                chunk_slot(At(W_QL + SPC + j), j, At(M_QL + NT))
            w = At(W_KR)
            need(pe, lo_ready, w, 1)
            whi = w_hi[:, w.ring(SPLIT_RING), :].rearrange("p (k n) -> p k n", k=KT)
            wlo = w_lo[:, w.ring(SPLIT_RING), :].rearrange("p (k n) -> p k n", k=KT)
            product(AD[0:ROPE, 0:TOK], [((whi[:, k], wlo[:, k]), (act_hi[:, k, :], act_lo[:, k, :]))
                                        for k in range(KT)]).then_inc(w_used, 1)
            pe.wait_ge(evac, M_KR + 1)
            turn_out(At(X_KROW), [krot[0:ROPE, t * P:(t + 1) * P] for t in range(NT)], P, ROPE)
            with pe.Fori(0, N_GATE - 1) as i:
                for j in range(SPC):
                    chunk_slot(At(W_G + j, i, SPC), j, At(M_G, i, NT))
            pe.wait_ge(qn_ready, N_A * NT + NT)
            pe.wait_ge(kvn_ready, 2)
            pe.wait_ge(lc_in, 32)
            for j in range(SPC):
                chunk_slot(At(W_G + (N_GATE - 1) * SPC + j), j, At(M_G + (N_GATE - 1) * NT))
                if j < 4:
                    turn_out(At(X_QN + j), token_blocks(stage[0], j * P))
                else:
                    k = j - 4
                    turn_out(At(X_CKV + k), [v4[:, kt, k * P:(k + 1) * P] for kt in range(4)])
            turn_out(At(X_KR), [krows[:, kt, :, :].rearrange("p s d -> p (s d)") for kt in range(4)])
            pe.wait_ge(x_free, X_U1)
            def pair_product(g, c):
                w, s_ = g.w.plus(c // 2), c // 2
                if c % 2 == 0:
                    need(pe, lo_ready, w, 1)
                hi_, lo_ = (x[:, w.ring(SPLIT_RING), :].rearrange("p (k n) -> p k n", k=4)
                            for x in (w_hi, w_lo))
                if c in (5, 7):
                    need(pe, rope_ready, g.r, (c - 3) // 2)
                elif c >= 4:
                    need(pe, evac, evac_of(g.m, c - 4), 1)
                else:
                    need(pe, evac, evac_of(g.m, c + 4), 1 - PAIR_EVAC)
                bank_ = PAIR_BANKS[c % 4]
                if c < 4:
                    cols = slice((c % 2) * P, (c % 2 + 1) * P)
                    last = product(bank_[:, 0:TOK], [((hi_[:, k, cols], lo_[:, k, cols]),
                                                      (qn_hi[:, k], qn_lo[:, k])) for k in range(4)])
                elif c < 6:
                    cols = slice((c - 4) * P, (c - 3) * P)
                    last = product(bank_[:], [((hi_[:, k, cols], lo_[:, k, cols]),
                                               (ckv_hi[:, k], ckv_lo[:, k])) for k in range(4)])
                else:
                    for n in range(2):
                        kt = 2 * (c - 6) + n
                        rows_t = slice(kt * P, (kt + 1) * P)
                        last = product(bank_[:, 2 * P * n:2 * P * (n + 1)],
                                       [((ckv_hi[:, k, rows_t], ckv_lo[:, k, rows_t]),
                                         (hi_[:, k], lo_[:, k])) for k in range(4)])
                last.then_inc(mm_done if c % 2 == 0 else w_used, 1)

            def head_score(g, n, at):
                h, t = n // NT, n % NT
                if t == 0:
                    need(pe, evac, evac_of(g.m, 4 + h), 1)
                    need(pe, rope_ready, g.r, h + 1)
                score(at, 2 * g.parity + h, t, 2 * g.parity + h, latent=True)

            def attend_pair(g, n, at):
                h = 2 * g.parity + n // NT
                if n == 0:
                    need(pe, evac, evac_of(g.m, 7), 1)
                attend(at, n % NT, At(T_H - N_UH).plus(at.fixed) if at.turn is None
                       else At(at.fixed + T_H - N_UH, at.turn, at.per),
                       lambda kt: v4[:, kt, h * P:(h + 1) * P])

            def pair_attention(g, following):
                for n in range(PAIR_UNITS):
                    at = g.n.plus(n)
                    prob_turn(at, n % NT, At(at.fixed + T_H - N_UH, at.turn, at.per))
                    if n + 2 < PAIR_UNITS:
                        head_score(g, n + 2, at.plus(2))
                    elif following is not None:
                        head_score(following, n + 2 - PAIR_UNITS, at.plus(2))
                    if n > 0:
                        attend_pair(g, n - 1, at.plus(-1))
                    elif g.before is not None:
                        attend_pair(g.before, PAIR_UNITS - 1, at.plus(-1))
                    if following is not None:
                        for c in range(8):
                            if load_step(c) == n:
                                pair_product(following, c)

            for c in range(8):
                pair_product(Pair(0), c)
            for n in range(2):
                head_score(Pair(0), n, Pair(0).n.plus(n))
            pair_attention(Pair(0), Pair(1))
            with pe.Fori(0, N_H - 1) as i:
                for p in (1, 2):
                    pair_attention(Pair(p, i), Pair(p + 1, i))
            pair_attention(Pair(2 * N_H - 1), None)
            attend_pair(Pair(2 * N_H - 1), PAIR_UNITS - 1, At(N_UH + N_H * UNITS - 1))
            pe.wait_ge(o_done, N_UH + N_H * UNITS)
            pe.wait_ge(t_free, T_H + N_H * T_H_PER)
            turned_chunk(X_U1, W_O1, M_O1, (x_free, X_U1))
            with pe.Fori(0, N_OUT - 1) as i:
                for j in range(SPC):
                    chunk_slot(At(W_O1 + SPC + j, i, SPC), j, At(M_O1 + NT, i, NT))

        @block.scalar
        def _(act):
            copy = lambda out, in_, scale=1.0: act.activation(out, in_, ACT.Copy, scale=scale)

            def split_hi(w, width=SLOT):
                landed(act, raw_in, w)
                need(act, w_used, w, 1 - SPLIT_RING)
                copy(w_hi[:, w.ring(SPLIT_RING), 0:width], w_raw[:, w.ring(RAW_RING), 0:width])\
                    .then_inc(hi_ready, 1)

            def act_high(k, base):
                if base == 0:
                    act.wait_ge(h_ready, k + 1)
                else:
                    act.wait_ge(x_free, X_X1 + k + 1)
                copy(act_hi[:, k, :], act_f[:, k, :]).then_inc(hhi, 1)

            def turned_high(x, out, width):
                need(act, x_done, x, 1)
                copy(out, BX[x.ring(len(BX))][:, 0:width]).then_inc(xhi, 1)

            def tile_done(m, w, t):
                if t < NT - 1:
                    need(act, mm_done, finished(m), t + 1)
                else:
                    need(act, w_used, w, 1)

            def evacuate(m, w, outs, scale=1.0):
                for t, out in enumerate(outs):
                    tile_done(m, w, t)
                    copy(out, G[t][:], scale).then_inc(evac, 1)

            def evacuate_gate(m, w, col):
                for t in range(NT):
                    tile_done(m, w, t)
                    copy(u[:, t, bass.ds(col, CH)], G[t][:], 0.5)
                    act.activation(stage[1][:, t, :], G[t][:], ACT.Tanh, scale=0.5).then_inc(evac, 1)

            def exponent(n, t):
                width = P if t == 0 else 3 * P
                need(act, mx_ready, n, 1)
                need(act, pv_done, n, -2)
                need(act, o_done, n, -3)
                act.activation(prob[:, n.ring(3), 0:width], S[n.ring(2)][:, 0:width], ACT.Exp,
                               bias=nmax[:, n.ring(4):n.ring(4) + 1],
                               accum_out=rsum[:, n.ring(4):n.ring(4) + 1]).then_inc(p_ready, 1)

            def square_sums(rows_, sizes, at, width, before):
                for t, tile in enumerate(sizes):
                    if before + t > 0:
                        act.wait_ge(ss_ready, before + t)
                    act.activation(stage_flat[:, 0:width], rows_[:, tile, 0:width], ACT.Square,
                                   accum_out=ss[:, at + t:at + t + 1]).then_inc(ss_ready, 1)

            act.dma_start(u[:, 0, :], t_in["x_prompt"][0]).then_inc(x_in[0], 16)
            for t in range(2):
                act.dma_start(u[:, 1 + t, :], t_in["x_sample"][0, t * P:(t + 1) * P, :])\
                    .then_inc(x_in[1 + t], 16)
            act.wait_ge(x_free, X_VEC + 1)
            act.activation(half_tanh[:], vecT[:, 0:2, :], ACT.Tanh, scale=0.5).then_inc(tanh_ready, 1)
            for t in range(NT):
                act.wait_ge(x_in[t], 16)
                square_sums(u, [t], t, D, t)
            split_hi(At(0))
            split_hi(At(1))
            act_high(0, 0)
            act_high(1, 0)
            for j in range(SPC):
                for k in range(2 * j + 2, min(2 * j + 4, KT)):
                    act_high(k, 0)
                if j == SPC - 1:
                    evacuate(At(M_KV), At(W_KV + j), [v4[:, kt, :] for kt in KEY_TILE])
                split_hi(At(W_KV + j + 2))
            act.wait_ge(evac, NT)
            for t in range(NT):
                act.activation(stage[1][:, t, 0:2 * HEAD], v4[:, KEY_TILE[t], 0:2 * HEAD], ACT.Square)\
                    .then_inc(ss_ready, 1)
            with act.Fori(0, N_A) as i:
                m, tau, n0 = At(M_A, i, 2 * NT), At(T_A, i, T_A_PER), At(N_UA, i, UNITS)
                for j in range(2 * SPC):
                    if j == 2:
                        act.wait_ge(kvn_ready, 1)
                        act.wait_ge(cache_in, 32)
                        need(act, t_done, tau)
                        need(act, pv_done, n0)
                        copy(k_group, v4[:, :, bass.ds(i * HEAD, HEAD)]).then_inc(group_copied, 1)
                        copy(v_group, v4[:, :, bass.ds(i * HEAD + 2 * HEAD, HEAD)])\
                            .then_inc(group_copied, 1)
                    if j == SPC - 1:
                        need(act, t_done, tau)
                        evacuate(m, At(W_A + j, i, 2 * SPC), [stage[0][:, t, :] for t in range(NT)])
                        for t in range(NT):
                            need(act, evac, m.plus(t), 1)
                            act.activation(stage[1][:, t, :], stage[0][:, t, :], ACT.Square)\
                                .then_inc(ss_ready, 1)
                    if j == 2 * SPC - 1:
                        exponent(n0, 0)
                        exponent(n0.plus(1), 1)
                        need(act, qn_ready, At(NT, i, NT))
                        evacuate_gate(m.plus(NT), At(W_A + j, i, 2 * SPC), i * CH)
                    split_hi(At(W_A + j + 2, i, 2 * SPC))
                for n in range(2, UNITS):
                    exponent(n0.plus(n), n % NT)
            with act.Fori(0, N_B) as i:
                m, tau, n0 = At(M_B, i, 4 * NT), At(T_B, i, T_B_PER), At(N_UB, i, UNITS)
                for j in range(4 * SPC):
                    w = At(W_B + j, i, 4 * SPC)
                    if j == SPC - 1:
                        need(act, t_done, tau)
                        evacuate(m, w, [stage[0][:, t, :] for t in range(NT)], SC0)
                    if j == 2 * SPC - 1:
                        need(act, o_done, n0)
                        evacuate(m.plus(NT), w, [stage[1][:, t, :] for t in range(NT)])
                    if j == 3 * SPC - 1:
                        need(act, kc_in, At(16, i, 16))
                        evacuate(m.plus(2 * NT), w, [v4[:, kt, :] for kt in KEY_TILE])
                    if j == 4 * SPC - 1:
                        exponent(n0, 0)
                        exponent(n0.plus(1), 1)
                        need(act, kb_out, At(16, i, 16))
                        need(act, t_done, tau, 2 * GROUP)
                        evacuate_gate(m.plus(3 * NT), w, i * CH + N_A * CH)
                    split_hi(w.plus(2))
                for n in range(2, UNITS):
                    exponent(n0.plus(n), n % NT)

            def chunk_squares(i, res, sums):
                cols = bass.ds(i * CH, CH)
                for t in range(NT):
                    need(act, res_done, res, t + 1)
                    need(act, ss_ready, sums, t)
                    act.activation(prob[:, 0:2, :].rearrange("p a n -> p (a n)")[:, 0:CH], u[:, t, cols],
                                   ACT.Square, accum_out=ss[:, bass.ds(i * NT + t, 1)])\
                        .then_inc(ss_ready, 1)

            def out_product(x, xh, w, m, res, sums, last):
                for k in range(2 * KPS):
                    turned_high(At(x + k), act_hi[:, k, :], TOK)
                for j in range(SPC):
                    for k in range(KPS * (j + 2), min(KPS * (j + 3), KT)):
                        turned_high(At(x + k), act_hi[:, k, :], TOK)
                    if j == SPC - 1:
                        evacuate(At(m), At(w + j), [stage[0][:, t, :] for t in range(NT)])
                    split_hi(At(w + j + 2))

                def chunk(i, place, ends=False):
                    for j in range(SPC):
                        if j == SPC - 1:
                            chunk_squares(i, place(res, NT), place(sums, NT))
                            evacuate(place(m + NT, NT), place(w + SPC + j, SPC),
                                     [stage[0][:, t, :] for t in range(NT)])
                        if not (ends and j >= SPC - 2):
                            split_hi(place(w + SPC + j + 2, SPC))

                turns = N_OUT - 1 - last
                with act.Fori(0, turns) as i:
                    chunk(i, lambda fixed, per: At(fixed, i, per))
                if last:
                    chunk(turns, lambda fixed, per: At(fixed + turns * per), True)
                chunk_squares(N_OUT - 1, At(res + (N_OUT - 1) * NT), At(sums + (N_OUT - 1) * NT))

            out_product(X_U0, XH_U0, W_O0, M_O0, RES_0, SS_OUT0, False)
            act_high(0, KT)
            act_high(1, KT)
            for c in range(2):
                for j in range(SPC):
                    if c == 0:
                        for k in range(2 * j + 2, min(2 * j + 4, KT)):
                            act_high(k, KT)
                    if j == SPC - 1 and c == 0:
                        evacuate(At(M_QL), At(W_QL + j), [stage[0][:, t, :] for t in range(NT)])
                    if j == SPC - 1 and c == 1:
                        act.wait_ge(vb_out, N_B * 16)
                        evacuate(At(M_QL + NT), At(W_QL + SPC + j), [v4[:, kt, :] for kt in KEY_TILE])
                    split_hi(At(W_QL + c * SPC + j + 2))
            for t in range(NT):
                act.wait_ge(evac, M_QL + 1 + t)
                act.activation(stage[1][:, t, :], stage[0][:, t, :], ACT.Square,
                               accum_out=ss[:, t:t + 1]).then_inc(ss_ready, 1)
            for t in range(NT):
                act.wait_ge(evac, M_QL + NT + 1 + t)
                act.wait_ge(ss_ready, SS_LAT - 2 * NT + 1 + t)
                act.activation(stage[1][:, t, :], v4[:, KEY_TILE[t], :], ACT.Square,
                               accum_out=ss[:, NT + t:NT + t + 1]).then_inc(ss_ready, 1)
            act.wait_ge(w_used, W_KR + 1)
            copy(krot[0:ROPE, :], AD[0:ROPE, 0:TOK]).then_inc(evac, 1)
            split_hi(At(W_G + 1))

            def gate_chunk(place, last=False):
                for j in range(SPC):
                    if last and j < 4:
                        turned_high(At(X_QN + j), qn_hi[:, j, :], TOK)
                    elif last:
                        turned_high(At(X_CKV + j - 4), ckv_hi[:, j - 4, :], KEYS)
                    if j == SPC - 1:
                        need(act, gate_done, place((N_A + N_B) * NT, NT))
                        evacuate_gate(place(M_G, NT), place(W_G + j, SPC), gate_column(place))
                    split_hi(place(W_G + j + 2, SPC))

            def gate_column(place):
                return place(0, CH).count()

            with act.Fori(0, N_GATE - 1) as i:
                gate_chunk(lambda fixed, per: At(fixed, i, per))
            gate_chunk(lambda fixed, per: At(fixed + (N_GATE - 1) * per), True)
            act.wait_ge(side_out, 64)

            def pair_out(g, c):
                if c % 2 == 0:
                    need(act, mm_done, g.mm, c // 2 + 1)
                else:
                    need(act, w_used, g.w, c // 2 + 1)
                bank_, h = PAIR_BANKS[c % 4], 2 * g.parity
                if c == 0 and g.index > 1:
                    need(act, pv_done, g.n, -PAIR_UNITS)
                if c in (0, 2):
                    copy(qT[:, h + c // 2, :], bank_[:, 0:TOK], SC1).then_inc(evac, 1)
                elif c in (4, 5):
                    copy(kT[:, h + c - 4, :], bank_[:]).then_inc(evac, 1)
                elif c >= 6:
                    copy(v4[:, 2 * (c - 6):2 * (c - 5), h * P:(h + 2) * P],
                         bank_[:].rearrange("p (t d) -> p t d", t=2)).then_inc(evac, 1)
                if c % 2 == 1:
                    split_hi(g.w.plus(c // 2 + 2))

            def pair_attention(g, following):
                for n in range(PAIR_UNITS):
                    if n + 2 < PAIR_UNITS or following is not None:
                        exponent(g.n.plus(n + 2), (n + 2) % NT)
                    for c in range(8):
                        if following is not None and load_step(c) == n:
                            pair_out(following, c)

            for c in range(8):
                pair_out(Pair(0), c)
            for n in range(2):
                exponent(At(N_UH + n), n)
            pair_attention(Pair(0), Pair(1))
            with act.Fori(0, N_H - 1) as i:
                for p in (1, 2):
                    pair_attention(Pair(p, i), Pair(p + 1, i))
            pair_attention(Pair(2 * N_H - 1), None)
            out_product(X_U1, XH_U1, W_O1, M_O1, RES_0 + N_OUT * NT, SS_LAT, True)

        @block.vector
        def _(dve):
            own = Chain(dve, v_own)

            def split_lo(w, width=SLOT):
                need(dve, hi_ready, w, 1)
                r = w.ring(SPLIT_RING)
                dve.tensor_tensor(w_lo[:, r, 0:width], w_raw[:, w.ring(RAW_RING), 0:width],
                                  w_hi[:, r, 0:width].bitcast(F32), ALU.subtract).then_inc(lo_ready, 1)

            def modulate(k, base):
                for v, cols in ((0, slice(0, P)), (1, slice(P, TOK))):
                    last = dve.tensor_scalar(act_f[:, k, cols], act_f[:, k, cols], mod[:, 1, v, k:k + 1],
                                             mod[:, 0, v, k:k + 1], ALU.mult, ALU.add)
                last.then_inc(h_ready, 1)

            def modulate_turned(k):
                dve.wait_ge(x_done, X_X1 + k + 1)
                for v, cols in ((0, slice(0, P)), (1, slice(P, TOK))):
                    last = dve.tensor_scalar(act_f[:, k, cols], BX[(X_X1 + k) % 4][:, cols],
                                             mod[:, 1, v, k:k + 1], mod[:, 0, v, k:k + 1],
                                             ALU.mult, ALU.add)
                last.then_inc(x_free, 1)

            def act_low(k, base):
                dve.wait_ge(hhi, base + k + 1)
                dve.tensor_tensor(act_lo[:, k, :], act_f[:, k, :], act_hi[:, k, :].bitcast(F32),
                                  ALU.subtract).then_inc(hlo, 1)

            def tokens_turned(first):
                for k in range(KT):
                    dve.wait_ge(x_done, first + k + 1)
                    dve.tensor_copy(act_f[:, k, :], BX[(first + k) % 4][:, 0:TOK]).then_inc(x_free, 1)

            def modulation(first, third, gain):
                for which in range(2):
                    x = first + which
                    dve.wait_ge(x_done, x + 1)
                    for v in range(2):
                        part = BX[x % 4][:].rearrange("p (j g q) -> p q g j", j=4, g=4)[:, v]
                        out = mod[:, which, v, :].rearrange("p (g j) -> p g j", g=4)
                        if which == 0:
                            ins = dve.tensor_copy(out, part)
                        else:
                            ins = dve.scalar_tensor_tensor(
                                out=out, in0=part, scalar=1.0,
                                in1=vecT[:, gain, :].rearrange("p (g j) -> p g j", g=4),
                                op0=ALU.add, op1=ALU.mult)
                        if v == 0:
                            own.add(ins)
                    ins.then_inc(x_free, 1)
                dve.wait_ge(x_free, first + 2)
                own.sync()

            def add_rows(third_at):
                need(dve, ada_used, At(HALVES * (third_at.fixed + 1), third_at.turn, HALVES * third_at.per))
                rows_at = rows[:, bass.ds(third_at.count(), 1), :].rearrange("p o n -> p (o n)") \
                    if third_at.turn is not None else rows[:, third_at.fixed, :]
                dve.tensor_tensor(rows_at, AD[:], rows_at, ALU.add).then_inc(rows_free, 1)

            powers = [0, None, 0]

            def root(turn, base, width, inverse, at=0):
                own.sync()
                dve.tensor_scalar(ms[:, 0:width], ss[:, at:at + width], inverse, EPS, ALU.mult, ALU.add)\
                    .then_inc(ms_ready, 1)
                need(dve, rstd_ready, At(base + 1, turn, 1) if turn is not None else At(base + 1))

            def normalise_tokens(power):
                dve.wait_ge(ss_ready, SS_AT[power])
                if power > 0:
                    own.add(dve.reduce_sum(ss[:, N_OUT * NT:N_OUT * NT + NT],
                                           spread(ss[:], [[1, NT], [NT, N_OUT]]), X))
                root(None, power, NT, 1.0 / D, 0 if power == 0 else N_OUT * NT)

            def head_norm(x, heads, at, gain):
                r = rstd[:, at:at + heads]
                own.add(dve.tensor_tensor(x, x, spread(r, [[1, heads], [0, HEAD]]), ALU.mult))
                own.sync()
                own.add(dve.tensor_tensor(x, x, spread(gain[:], [[0, heads], [1, HEAD]]), ALU.mult))
                own.sync()

            def rotate(x, heads, width, cos, sin, done=None):
                q = width // 4
                xr = x.rearrange("p h (a s m) -> p h a s m", a=2, s=2)
                sw = swapped[:, 0:heads * width].rearrange("p (h a s m) -> p h a s m", h=heads, a=2, s=2)
                sv = sin.rearrange("p (a s m) -> p a s m", a=2, s=2)
                for s in range(2):
                    tab = sv[:, :, s, :]
                    tab = spread(tab, [[0, heads]] + [list(d) for d in tab.ap[1:]])
                    own.add(dve.tensor_tensor(sw[:, :, :, s, :], xr[:, :, :, 1 - s, :], tab, ALU.mult))
                own.sync()
                own.add(dve.tensor_tensor(x, x, spread(cos, [[0, heads], [1, width]]), ALU.mult))
                own.sync()
                last = dve.tensor_tensor(x, x, swapped[:, 0:heads * width].rearrange("p (h d) -> p h d", h=heads),
                                         ALU.add)
                if done is None:
                    own.add(last)
                    own.sync()
                else:
                    last.then_inc(done, 1)

            def maximum(n, t, h=0, biased=False):
                width = P if t == 0 else 3 * P
                s = S[n.ring(2)]
                need(dve, s_done, n, 1)
                need(dve, p_ready, n, -3)
                if biased and t > 0:
                    own.add(dve.tensor_tensor(
                        s[:, P:3 * P], s[:, P:3 * P],
                        bias[:, h, t - 1, :, :].rearrange("p r c -> p (r c)"), ALU.add))
                    own.sync()
                dve.tensor_reduce(nmax[:, n.ring(4):n.ring(4) + 1], s[:, 0:width], X, ALU.max,
                                  negate=True).then_inc(mx_ready, 1)

            def copy_turned(tau, out, cols, parts=P):
                need(dve, t_done, tau, 1)
                dve.tensor_copy(out, TB[0:parts, 0:cols]).then_inc(t_free, 1)

            def prob_copy(n, t, tau):
                need(dve, pv_done, n, -1)
                width = P if t == 0 else 3 * P
                copy_turned(tau, probT[:, n.ring(2), 0:width], width)

            def output(n, t, col):
                need(dve, p_ready, n, 1)
                own.add(dve.reciprocal(rinv[:, n.ring(4):n.ring(4) + 1], rsum[:, n.ring(4):n.ring(4) + 1]))
                own.sync()
                need(dve, pv_done, n, 1)
                at = u[:, t, bass.ds(col, P)]
                dve.scalar_tensor_tensor(out=at, in0=OB[:, n.ring(4) * P:(n.ring(4) + 1) * P],
                                         scalar=rinv[:, n.ring(4):n.ring(4) + 1], in1=at,
                                         op0=ALU.mult, op1=ALU.mult).then_inc(o_done, 1)

            def finish_gate(m, gates, col):
                for t in range(NT):
                    need(dve, evac, m.plus(t), 1)
                    at = u[:, t, bass.ds(col, CH)]
                    dve.scalar_tensor_tensor(out=at, in0=stage[1][:, t, :], scalar=1.0, in1=at,
                                             op0=ALU.add, op1=ALU.mult).then_inc(gate_done, 1)
                need(dve, gate_done, gates, NT)

            def turned_low(x, hi, out, width, high_at):
                dve.wait_ge(xhi, high_at + 1)
                dve.tensor_tensor(out, BX[x % 4][:, 0:width], hi.bitcast(F32), ALU.subtract)\
                    .then_inc(x_free, 1)

            def turned_chunk(x, xh, w):
                for k in range(2 * KPS):
                    turned_low(x + k, act_hi[:, k, :], act_lo[:, k, :], TOK, xh + k)
                for j in range(SPC):
                    for k in range(KPS * (j + 2), min(KPS * (j + 3), KT)):
                        turned_low(x + k, act_hi[:, k, :], act_lo[:, k, :], TOK, xh + k)
                    split_lo(At(w + j + 2))

            def residual(i, col):
                for t in range(NT):
                    own.add(dve.tensor_tensor(stage[0][:, t, :], stage[0][:, t, :],
                                              gate_bc[:, min(t, 1), bass.ds(col, CH)], ALU.mult))
                own.sync()
                for t in range(NT):
                    dve.tensor_tensor(u[:, t, bass.ds(col, CH)], stage[0][:, t, :], stage[1][:, t, :],
                                      ALU.add).then_inc(res_done, 1)

            dve.memset(silu_c[:], 0.0).then_inc(set_up, 1)
            dve.memset(mhalf[:], -0.5).then_inc(set_up, 1)
            dve.memset(ms[:], 1.0).then_inc(set_up, 1)
            columns = 0
            for first, counts in ((N_UA, (s_done, mx_ready, p_ready, pv_done, o_done)),
                                  (T_A, (t_done, t_free)), (RES_0, (res_done,)),
                                  (ROWS_0, (rows_free,))):
                for count in counts:
                    dve.memset(begun[:, columns:columns + 1], 0.0).then_inc(count, first)
                    columns += 1
            dve.wait_ge(set_up, 3)
            dve.wait_ge(x_done, X_VEC + 1)
            dve.tensor_copy(vecT[:].rearrange("p a k -> p (a k)"), BX[X_VEC % 4][:, 0:4 * KT])\
                .then_inc(x_free, 1)
            dve.wait_ge(tanh_ready, 1)
            own.add(dve.scalar_tensor_tensor(out=half_tanh[:], in0=half_tanh[:], scalar=1.0,
                                             in1=vecT[:, 0:2, :], op0=ALU.add, op1=ALU.mult))
            own.sync()
            dve.tensor_scalar(silu_c[:, :, 0:2].rearrange("p k v -> p v k"), half_tanh[:], 0.5, None,
                              ALU.mult).then_inc(silu_ready, 1)
            normalise_tokens(0)
            for t in range(NT):
                dve.tensor_scalar(u[:, t, :], u[:, t, :], rstd[:, t:t + 1], None, ALU.mult)\
                    .then_inc(xn_ready, 1)
            dve.wait_ge(rows_in, 8 * 16)
            add_rows(At(0))
            tokens_turned(X_X0)
            add_rows(At(1))
            split_lo(At(0))
            split_lo(At(1))
            dve.wait_ge(x_free, X_MOD0)
            modulation(X_MOD0, 0, 2)
            for k in range(2):
                modulate(k, 0)
            for k in range(2):
                act_low(k, 0)
            for j in range(SPC):
                for k in range(2 * j + 2, min(2 * j + 4, KT)):
                    modulate(k, 0)
                for k in range(2 * j + 2, min(2 * j + 4, KT)):
                    act_low(k, 0)
                split_lo(At(W_KV + j + 2))
            dve.wait_ge(ss_ready, 2 * NT)
            dve.wait_ge(const_in, CONSTS * 16)
            own.add(dve.tensor_scalar(gain_q[:], gain_q[:], SC0, None, ALU.mult))
            for t in range(NT):
                own.add(dve.reduce_sum(ss[:, 2 * t:2 * t + 2],
                                       stage[1][:, t, 0:2 * HEAD].rearrange("p (h d) -> p h d", h=2), X))
            root(None, 1, 2 * NT, 1.0 / HEAD)
            for t in range(NT):
                x = v4[:, KEY_TILE[t], 0:2 * HEAD].rearrange("p (h d) -> p h d", h=2)
                head_norm(x, 2, 2 * t, gain_k)
                if t > 0:
                    rotate(x, 2, HEAD, cos0[:, t - 1, :], sin0[:, t - 1, :])
            dve.memset(ms[:, 15:16], 1.0).then_inc(kvn_ready, 1)
            with dve.Fori(0, N_A) as i:
                m, tau, n0 = At(M_A, i, 2 * NT), At(T_A, i, T_A_PER), At(N_UA, i, UNITS)
                own.enter(i, OWN_A)
                for j in range(2 * SPC):
                    if j == 5:
                        copy_turned(tau, kT[:, 0, :], KEYS)
                    if j == SPC:
                        need(dve, ss_ready, At(3 * NT, i, NT))
                        own.add(dve.reduce_sum(ss[:, 0:NT * GROUP],
                                               stage[1].rearrange("p t (h d) -> p (t h) d", h=GROUP), X))
                        root(i, 2, NT * GROUP, 1.0 / HEAD)
                    if SPC <= j < SPC + 3:
                        t = j - SPC
                        x = stage[0][:, t, :].rearrange("p (h d) -> p h d", h=GROUP)
                        if t == 0:
                            r = rstd[:, 0:GROUP]
                            own.add(dve.tensor_tensor(x, x, spread(r, [[1, GROUP], [0, HEAD]]), ALU.mult))
                            own.sync()
                            dve.tensor_tensor(x, x, spread(gain_q[:], [[0, GROUP], [1, HEAD]]), ALU.mult)\
                                .then_inc(qn_ready, 1)
                        else:
                            head_norm(x, GROUP, t * GROUP, gain_q)
                            rotate(x, GROUP, HEAD, cos0[:, t - 1, :], sin0[:, t - 1, :], qn_ready)
                    if SPC + 4 <= j:
                        h = j - SPC - 4
                        copy_turned(tau.plus(1 + h), qT[:, h, :], TOK)
                    if j == 2 * SPC - 1:
                        maximum(n0, 0)
                        maximum(n0.plus(1), 1)
                    split_lo(At(W_A + j + 2, i, 2 * SPC))
                finish_gate(m.plus(NT), At(0, i, NT), i * CH)
                add_rows(At(2, i, 1))
                for n in range(UNITS):
                    t = n % NT
                    prob_copy(n0.plus(n), t, tau.plus(1 + GROUP + n))
                    if n + 2 < UNITS:
                        maximum(n0.plus(n + 2), (n + 2) % NT)
                    if n > 0:
                        output(n0.plus(n - 1), (n - 1) % NT, i * CH + (n - 1) // NT * P)
                output(n0.plus(UNITS - 1), NT - 1, i * CH + (GROUP - 1) * P)
                own_a = own.k
            own.leave(N_A)
            with dve.Fori(0, N_B) as i:
                m, tau, n0 = At(M_B, i, 4 * NT), At(T_B, i, T_B_PER), At(N_UB, i, UNITS)
                own.enter(i, OWN_B)
                for j in range(4 * SPC):
                    if SPC + 2 <= j < SPC + 6:
                        copy_turned(tau.plus(j - SPC - 2), qT[:, j - SPC - 2, :], TOK)
                    if 2 * SPC + 2 <= j < 2 * SPC + 6:
                        h = j - 2 * SPC - 2
                        copy_turned(tau.plus(GROUP + h), kT[:, h, :], KEYS)
                    if j == 4 * SPC - 1:
                        add_rows(At(2 + N_A, i, 1))
                        need(dve, bias_ready, At(1, i, 1))
                        maximum(n0, 0, 0, True)
                        maximum(n0.plus(1), 1, 0, True)
                    split_lo(At(W_B + j + 2, i, 4 * SPC))
                finish_gate(m.plus(3 * NT), At(N_A * NT, i, NT), i * CH + N_A * CH)
                for n in range(UNITS):
                    t = n % NT
                    prob_copy(n0.plus(n), t, tau.plus(2 * GROUP + n))
                    if n + 2 < UNITS:
                        maximum(n0.plus(n + 2), (n + 2) % NT, (n + 2) // NT, True)
                    if n > 0:
                        output(n0.plus(n - 1), (n - 1) % NT, i * CH + N_A * CH + (n - 1) // NT * P)
                output(n0.plus(UNITS - 1), NT - 1, i * CH + N_A * CH + (GROUP - 1) * P)
            own.leave(N_B)
            turned_chunk(X_U0, XH_U0, W_O0)
            modulation(X_MOD1, 3, 3)
            dve.wait_ge(evac, M_O0 + NT)
            dve.wait_ge(gbc_in, 32)
            dve.wait_ge(res_in, 32)
            residual(0, 0)
            with dve.Fori(0, N_OUT - 1) as i:
                own.enter(i, NT)
                for j in range(SPC):
                    split_lo(At(W_O0 + SPC + j + 2, i, SPC))
                need(dve, evac, At(M_O0 + 2 * NT, i, NT))
                need(dve, res_in, At(64, i, 32))
                residual(i, i * CH + CH)
            own.leave(N_OUT - 1)
            normalise_tokens(2 + N_A)
            dve.wait_ge(x1_out, N_OUT * 16)
            for t in range(NT):
                dve.tensor_scalar(u[:, t, :], u[:, t, :], rstd[:, t:t + 1], None, ALU.mult)\
                    .then_inc(xn_ready, 1)
            for k in range(2):
                modulate_turned(k)
            for k in range(2):
                act_low(k, KT)
            for c in range(2):
                for j in range(SPC):
                    if c == 0:
                        for k in range(2 * j + 2, min(2 * j + 4, KT)):
                            modulate_turned(k)
                        for k in range(2 * j + 2, min(2 * j + 4, KT)):
                            act_low(k, KT)
                    split_lo(At(W_QL + c * SPC + j + 2))
            split_lo(At(W_G + 1))
            dve.wait_ge(ss_ready, SS_LAT)
            dve.wait_ge(gain_in, 48)
            root(None, 3 + N_A, 2 * NT, 1.0 / CH)
            for t in range(NT):
                x = stage[0][:, t, :]
                dve.scalar_tensor_tensor(out=x, in0=x, scalar=rstd[:, t:t + 1], in1=gain_ql[:],
                                         op0=ALU.mult, op1=ALU.mult).then_inc(qn_ready, 1)
            for t in range(NT):
                x = v4[:, KEY_TILE[t], :]
                own.add(dve.scalar_tensor_tensor(out=x, in0=x, scalar=rstd[:, NT + t:NT + t + 1],
                                                 in1=gain_kv[:], op0=ALU.mult, op1=ALU.mult))
            dve.wait_ge(x_done, X_KROW + 1)
            place = BX[X_KROW % 4]
            own.add(dve.tensor_copy(krows[:, 0, 0, :], place[:, 0:ROPE]))
            dve.tensor_copy(krows[:, 2:4, 0, :], place[:, ROPE:3 * ROPE].rearrange("p (t d) -> p t d", t=2))\
                .then_inc(x_free, 1)
            dve.wait_ge(x_free, X_KROW + 1)
            own.sync()
            for t in range(2):
                rotate(krows[:, 2 + t, 0:1, :], 1, ROPE, cos1[:, t, :], sin1[:, t, :])
            dve.wait_ge(lc_in, 32)
            own.add(dve.tensor_copy(krows[:, :, 1, :], krows[:, :, 0, :]))
            own.sync()
            dve.memset(ms[:, 15:16], 1.0).then_inc(kvn_ready, 1)
            with dve.Fori(0, N_GATE - 1) as i:
                for j in range(SPC):
                    split_lo(At(W_G + j + 2, i, SPC))
                finish_gate(At(M_G, i, NT), At((N_A + N_B) * NT, i, NT), i * CH)
            done = N_GATE - 1
            for j in range(SPC):
                if j < 4:
                    turned_low(X_QN + j, qn_hi[:, j, :], qn_lo[:, j, :], TOK, XH_QN + j)
                else:
                    turned_low(X_CKV + j - 4, ckv_hi[:, j - 4, :], ckv_lo[:, j - 4, :], KEYS, XH_CKV + j - 4)
                split_lo(At(W_G + done * SPC + j + 2))
            finish_gate(At(M_G + done * NT), At((N_A + N_B + done) * NT), done * CH)
            dve.wait_ge(x_done, X_KR + 1)
            dve.tensor_copy(krT[:], BX[X_KR % 4][:]).then_inc(x_free, 1)

            def pair_out(g, c):
                if c in (1, 3):
                    need(dve, w_used, g.w, c // 2 + 1)
                    if c == 1 and g.index > 1:
                        need(dve, pv_done, g.n, -PAIR_UNITS)
                    dve.tensor_tensor(q_turned[:, 2 * g.parity + c // 2, :], PAIR_BANKS[c % 4][:, 0:TOK],
                                      rope_q[:], ALU.mult).then_inc(rope_ready, 1)
                if c % 2 == 1:
                    split_lo(g.w.plus(c // 2 + 2))

            def pair_output(g, n):
                output(g.n.plus(n), n % NT, g.column(n // NT))

            def pair_attention(g, following):
                for n in range(PAIR_UNITS):
                    at = g.n.plus(n)
                    prob_copy(at, n % NT, At(at.fixed + T_H - N_UH, at.turn, at.per))
                    if n + 2 < PAIR_UNITS or following is not None:
                        maximum(at.plus(2), (n + 2) % NT)
                    if n > 0:
                        pair_output(g, n - 1)
                    elif g.before is not None:
                        pair_output(g.before, PAIR_UNITS - 1)
                    for c in range(8):
                        if following is not None and load_step(c) == n:
                            pair_out(following, c)

            for c in range(8):
                pair_out(Pair(0), c)
            for n in range(2):
                maximum(At(N_UH + n), n)
            pair_attention(Pair(0), Pair(1))
            with dve.Fori(0, N_H - 1) as i:
                own.enter(i, 2 * PAIR_UNITS)
                for p in (1, 2):
                    pair_attention(Pair(p, i), Pair(p + 1, i))
            own.leave(N_H - 1)
            pair_attention(Pair(2 * N_H - 1), None)
            pair_output(Pair(2 * N_H - 1), PAIR_UNITS - 1)
            turned_chunk(X_U1, XH_U1, W_O1)
            dve.wait_ge(evac, M_O1 + NT)
            dve.wait_ge(gbc_in, 64)
            dve.wait_ge(res_in, 32 * N_OUT + 16)
            residual(0, 0)

            def out_chunk(i, place, last=False):
                for j in range(SPC):
                    if not (last and j >= SPC - 2):
                        split_lo(place(W_O1 + SPC + j + 2, SPC))
                need(dve, evac, place(M_O1 + 2 * NT, NT))
                need(dve, res_in, place(32 * N_OUT + 32, 16))
                residual(i, i * CH + CH)

            with dve.Fori(0, N_OUT - 2) as i:
                own.enter(i, NT)
                out_chunk(i, lambda fixed, per: At(fixed, i, per))
            own.leave(N_OUT - 2)
            out_chunk(N_OUT - 2, lambda fixed, per: At(fixed + (N_OUT - 2) * per), last=True)
            normalise_tokens(4 + N_A)
            dve.wait_ge(fn_in, 16)
            for t in range(NT):
                dve.scalar_tensor_tensor(out=u[:, t, :], in0=u[:, t, :], scalar=rstd[:, t:t + 1],
                                         in1=fnorm[:], op0=ALU.mult, op1=ALU.mult).then_inc(y_ready, 1)

        @block.gpsimd
        def _(pool):
            def power(at):
                need(pool, ms_ready, at, 1)
                pool.tensor_tensor(rstd[:], ms[:], mhalf[:], ALU.pow).then_inc(rstd_ready, 1)

            def to_all(out, vector, sem_):
                pool.dma_start(out, spread_rows(vector)).then_inc(sem_, 16)

            def spread_rows(vector):
                return bass.AP(vector.tensor, vector.offset, [[0, P]] + [list(d) for d in vector.ap])

            for name, tile in (("cos0", cos0), ("sin0", sin0), ("cos1", cos1), ("sin1", sin1),
                               ("mask", mask)):
                pool.dma_start(tile[:], t_in[name]).then_inc(const_in, 16)
            for name, tile in (("l0_q_norm", gain_q), ("l0_k_norm", gain_k)):
                to_all(tile[:], t_in[name], const_in)
            for layer in range(2):
                b = t_in[f"l{layer}_ada_b"]
                for g in range(4):
                    src = bass.AP(b.tensor, b.offset + g * CH, [[0, 32], [D, 3], [1, CH]])
                    pool.dma_start(rows[32 * g:32 * g + 32, 3 * layer:3 * layer + 3, :], src)\
                        .then_inc(rows_in, 16)
            pool.dma_start(v4[:, 1, 0:2 * HEAD], t_in["cache_l0_a_k"][0].rearrange("t h d -> t (h d)"))\
                .then_inc(cache_in, 16)
            pool.dma_start(v4[:, 1, 2 * HEAD:4 * HEAD], t_in["cache_l0_a_v"][0].rearrange("t h d -> t (h d)"))\
                .then_inc(cache_in, 16)
            pool.wait_ge(set_up, 3)
            power(At(0))
            power(At(1))
            pool.wait_ge(kvn_ready, 1)
            pool.dma_start(t_out["a_k"][0].rearrange("t h d -> t (h d)"), v4[:, 0, 0:2 * HEAD])\
                .then_inc(side_out, 16)
            pool.dma_start(t_out["a_v"][0].rearrange("t h d -> t (h d)"), v4[:, 0, 2 * HEAD:4 * HEAD])\
                .then_inc(side_out, 16)
            rpb = t_in["l0_rpb"]
            table = (2 * 8 - 1) * (2 * WIN - 1)
            for h in range(N_B * GROUP):
                for qr in range(4):
                    base = h * table + (7 - qr) * (2 * WIN - 1) + WIN - 1
                    src = bass.AP(rpb.tensor, base, [[2 * WIN - 1, 4], [-1, GRID_W], [1, GRID_W]])
                    pool.dma_start(bias_dram[h, GRID_W * qr:GRID_W * (qr + 1), :]
                                   .rearrange("q (r c) -> r q c", r=4), src).then_inc(table_out, 16)
            with pool.Fori(0, N_A) as i:
                power(At(2, i, 1))
            pool.wait_ge(table_out, 16 * 4 * N_B * GROUP)
            kc = t_in["cache_l0_b_k"][0].rearrange("t h d -> t (h d)")
            vc = t_in["cache_l0_b_v"][0].rearrange("t h d -> t (h d)")
            kb = t_out["b_k"][0].rearrange("t h d -> t (h d)")
            vb = t_out["b_v"][0].rearrange("t h d -> t (h d)")
            pool.wait_ge(side_out, 32)
            for i in range(N_B):
                m, n0 = At(M_B + i * 4 * NT), At(N_UB + i * UNITS)
                need(pool, o_done, n0)
                if i > 0:
                    pool.wait_ge(vb_out, 16 * i)
                pool.dma_start(kcache[:], kc[:, bass.ds(i * CH, CH)]).then_inc(kc_in, 16)
                pool.dma_start(v4[:, 1, :], vc[:, bass.ds(i * CH, CH)]).then_inc(vc_in, 16)
                pool.dma_start(bias[:].rearrange("p h q r c -> p (h q) (r c)"),
                               bias_dram.rearrange("h (q p) n -> p (h q) n", p=P)
                               [:, bass.ds(i * 2 * GROUP, 2 * GROUP), :]).then_inc(bias_in, 16)
                pool.wait_ge(bias_in, 16 * (i + 1))
                flat = bias[:].rearrange("p h q r c -> p (h q r) c")
                pool.tensor_tensor(flat, flat, spread(mask[:], [[0, 8 * GROUP], [1, GRID_W]]), ALU.add)\
                    .then_inc(bias_ready, 1)
                need(pool, evac, m, 2 * NT)
                pool.dma_start(kb[:, bass.ds(i * CH, CH)], stage[1][:, 0, :]).then_inc(kb_out, 16)
                need(pool, evac, m, 3 * NT)
                pool.dma_start(vb[:, bass.ds(i * CH, CH)], v4[:, 0, :]).then_inc(vb_out, 16)

            def gate_rows(layer, third, after):
                pool.wait_ge(*after)
                pool.wait_ge(rows_free, ROWS_0 + 6)
                for v in range(2):
                    pool.dma_start(gate_dram[layer, v].rearrange("(g n) -> g n", g=4),
                                   rows[v:v + 97:32, third, :]).then_inc(grow_out, 16)
                pool.wait_ge(grow_out, 32 * (layer + 1))
                for v in range(2):
                    to_all(gate_bc[:, v, :], gate_dram[layer, v], gbc_in)

            pool.wait_ge(o_done, N_UH)
            for name, tile in (("l1_q_a_norm", gain_ql), ("l1_kv_a_norm", gain_kv)):
                to_all(tile[:], t_in[name], gain_in)
            gate_rows(0, 2, (o_done, N_UH))
            pool.dma_start(rope_q[:], t_in["rope_q"]).then_inc(gain_in, 16)
            for i in range(N_OUT):
                need(pool, res_done, At(RES_0 + i * NT))
                cols = bass.ds(i * CH, CH)
                pool.dma_start(stage[1][:, 0, :], t_in["x_prompt"][0][:, cols]).then_inc(res_in, 16)
                pool.dma_start(stage[1][:, 1:3, :],
                               t_in["x_sample"][0].rearrange("(t p) n -> p t n", p=P)[:, :, cols])\
                    .then_inc(res_in, 16)
                need(pool, res_done, At(RES_0 + NT + i * NT))
                pool.dma_start(x1_dram[:, :, cols], u[:, :, cols]).then_inc(x1_out, 16)
            power(At(2 + N_A))
            pool.wait_ge(vb_out, N_B * 16)
            pool.dma_start(v4[:, 1, :], t_in["cache_l1_ckv"][0]).then_inc(lc_in, 16)
            pool.dma_start(krows[:, 1, 0, :], t_in["cache_l1_krope"][0]).then_inc(lc_in, 16)
            power(At(3 + N_A))
            pool.wait_ge(kvn_ready, 2)
            pool.dma_start(t_out["ckv"][0], v4[:, 0, :]).then_inc(side_out, 16)
            pool.dma_start(t_out["krope"][0], krows[:, 0, 0, :]).then_inc(side_out, 16)
            gate_rows(1, 5, (o_done, N_UH + N_H * UNITS))
            to_all(fnorm[:], t_in["final_norm"], fn_in)
            for i in range(N_OUT):
                need(pool, res_done, At(RES_0 + (N_OUT + i) * NT))
                pool.dma_start(stage[1], x1_dram[:, :, bass.ds(i * CH, CH)]).then_inc(res_in, 16)
            power(At(4 + N_A))
            pool.wait_ge(y_ready, 1)
            pool.dma_start(t_out["y_prompt"][0], u[:, 0, :]).then_inc(y_out, 16)
            for t in range(2):
                pool.wait_ge(y_ready, 2 + t)
                pool.dma_start(t_out["y_sample"][0, t * P:(t + 1) * P, :], u[:, 1 + t, :])\
                    .then_inc(y_out, 16)
            pool.wait_ge(y_out, 48)
            pool.wait_ge(side_out, 64)
            pool.wait_ge(kb_out, N_B * 16)
            pool.wait_ge(vb_out, N_B * 16)
            pool.wait_ge(x1_out, N_OUT * 16)


CONSTS = 7
OWN_A = 1 + 1 + 2 * (2 + 3) + UNITS
OWN_B = 2 * GROUP + UNITS
SS_OUT0 = (1 + 1 + N_A) * NT
SS_LAT = SS_OUT0 + N_OUT * NT + 2 * NT
SS_AT = {0: NT, 2 + N_A: SS_OUT0 + N_OUT * NT, 4 + N_A: SS_LAT + N_OUT * NT}


def slots(w, columns):
    out = []
    for c in columns:
        part = w[:, c:c + CH].reshape(KT // KPS, KPS, P, CH)
        out.append(part.transpose(0, 2, 1, 3).reshape(KT // KPS, P, SLOT))
    return out


def lay_out(x):
    f = {k: np.ascontiguousarray(v) for k, v in x.items()}
    kv, qb, gate = 1024, 1536, 4608
    parts = slots(f["l0_w_in"], [kv])
    for g in range(N_A):
        parts += slots(f["l0_w_in"], [g * CH, gate + g * CH])
    for g in range(N_B):
        parts += slots(f["l0_w_in"], [qb + g * CH, qb + 1024 + g * CH, qb + 2048 + g * CH,
                                      gate + (N_A + g) * CH])
    parts += slots(f["l0_w_out"], range(0, D, CH))
    parts += slots(f["l1_w_in"], [0, CH])
    parts.append(f["l1_w_in"][:, 2 * CH:2 * CH + ROPE].reshape(KT, P, ROPE).transpose(1, 0, 2)
                 .reshape(1, P, SLOT))
    parts += slots(f["l1_w_in"], range(2 * CH + ROPE, 2 * CH + ROPE + D, CH))
    partner = np.arange(ROPE).reshape(2, 2, ROPE // 4)[:, ::-1].reshape(ROPE)
    q = f["l1_w_q_b"].reshape(4, P, 16, HEAD + ROPE)
    q = np.concatenate([q, q[..., HEAD + partner]], -1).transpose(2, 1, 0, 3)
    kv = f["l1_w_kv_b"].reshape(4, P, 8, 2, 2, HEAD).transpose(2, 4, 1, 0, 3, 5)
    heads = np.concatenate([q.reshape(8, 2, P, SLOT), kv.reshape(8, 2, P, SLOT)], 1)
    parts.append(heads.reshape(8 * PAIR_SLOTS, P, SLOT))
    parts += slots(f["l1_w_out"], range(0, D, CH))
    arrays = {"w_all": np.concatenate(parts)}
    assert len(arrays["w_all"]) == W_END
    arrays["ada_all"] = np.stack([f["l0_ada_w"], f["l1_ada_w"]]).reshape(2, KT, P, 3, 2, SLOT)\
        .transpose(0, 3, 1, 4, 2, 5).reshape(6 * HALVES, P, SLOT)
    for name in NAMES:
        arrays[name] = f[name]
    token = np.arange(2 * P)
    for n, width in ((0, HEAD), (1, ROPE)):
        a = width // 2
        inv = (1.0 / (np.float32(10000.0) ** (np.arange(a // 2, dtype=np.float32) * np.float32(2.0) / np.float32(a)))).astype(np.float32)
        angles = [(np.float32(1) * pos.astype(np.float32))[:, None] * inv for pos in (token // GRID_W, token % GRID_W)]
        cos = np.concatenate([np.tile(np.cos(g), (1, 2)) for g in angles], 1)
        sin = np.concatenate([np.concatenate([-np.sin(g), np.sin(g)], 1) for g in angles], 1)
        for name, table in (("cos", cos), ("sin", sin)):
            arrays[f"{name}{n}"] = np.ascontiguousarray(
                table.astype(np.float32).reshape(2, P, width).transpose(1, 0, 2))
    turn_ = [np.concatenate([np.full((P, ROPE), one), arrays[n].transpose(1, 0, 2).reshape(2 * P, ROPE)])
             for n, one in (("cos1", 1.0), ("sin1", 0.0))]
    arrays["rope_q"] = np.ascontiguousarray((np.concatenate(turn_, 1).T * SC1).astype(np.float32))
    col = np.arange(P)[:, None] % GRID_W
    start = np.clip(col - WIN // 2, 0, GRID_W - WIN)
    key = np.arange(GRID_W)[None]
    arrays["mask"] = np.where((key >= start) & (key < start + WIN), 0.0, -1e30).astype(np.float32)
    arrays["ident"] = np.eye(P, dtype=np.float32)
    return arrays


NAMES = ["x_prompt", "x_sample", "cache_l0_a_k", "cache_l0_a_v", "cache_l0_b_k", "cache_l0_b_v",
         "cache_l1_ckv", "cache_l1_krope", "c", "c_ctx", "l0_norm", "l0_ada_b", "l0_q_norm",
         "l0_k_norm", "l0_rpb", "l1_norm", "l1_ada_b", "l1_q_a_norm", "l1_kv_a_norm", "final_norm"]
OUTS = [("y_prompt", (1, P, D)), ("y_sample", (1, 2 * P, D)), ("a_k", (1, P, 2, HEAD)),
        ("a_v", (1, P, 2, HEAD)), ("b_k", (1, P, 8, HEAD)), ("b_v", (1, P, 8, HEAD)),
        ("ckv", (1, P, CH)), ("krope", (1, P, ROPE))]


def kernel(**inputs):
    from concourse import bacc
    from concourse.bass_utils import run_bass_kernel_spmd

    nc = bacc.Bacc("TRN2", target_bir_lowering=False, num_devices=1)
    arrays = lay_out(inputs)
    t_in = {n: nc.dram_tensor(f"in_{n}", a.shape, F32, kind="ExternalInput").ap()
            for n, a in arrays.items()}
    t_out = {n: nc.dram_tensor(f"out_{n}", s, F32, kind="ExternalOutput").ap() for n, s in OUTS}
    build(nc, t_in, t_out)
    r = run_bass_kernel_spmd(nc, [{f"in_{n}": a for n, a in arrays.items()}], core_ids=[0])
    return tuple(r.results[0][f"out_{n}"] for n, _ in OUTS)
```

```python
from contextlib import ExitStack

import numpy as np

import concourse.bass as bass
from concourse import mybir

F32 = mybir.dt.float32
F32R = mybir.dt.float32r
ALU = mybir.AluOpType
ACT = mybir.ActivationFunctionType
X = mybir.AxisListType.X

P = 128
D = 2048
KT = D // P
CH = 512
NT = 3
TOK = NT * P
KEYS = 4 * P
KEY_TILE = [0, 2, 3]
GRID_W = 64
WIN = 16
HEAD = 128
ROPE = 64
SLOT = 1024
SPC = KT * CH // SLOT
KPS = SLOT // CH
RAW_RING, SPLIT_RING, ADA_RING = 4, 2, 8
QUARTERS, KPQ = D // CH, CH // P
HALVES = 2 * KT
EPS = 1e-6
SC0 = HEAD ** -0.5
SC1 = (HEAD + ROPE) ** -0.5
GROUP = 4
UNITS = GROUP * NT
PAIR_SLOTS = 4
PAIR_EVAC = 6
PAIR_UNITS = 2 * NT

N_A, N_B, N_OUT, N_GATE, N_H = 2, 2, D // CH, D // CH, 4
W_KV = 0
W_QA = W_KV + SPC
W_A = W_QA + SPC
W_B = W_A + N_A * 2 * SPC
W_O0 = W_B + (N_B * 4 - 1) * SPC
W_QL = W_O0 + N_OUT * SPC
W_KR = W_QL + 2 * SPC
W_G = W_KR + 1
W_H = W_G + N_GATE * SPC
W_O1 = W_H + N_H * 2 * PAIR_SLOTS
W_END = W_O1 + N_OUT * SPC
M_KV = 0
M_QA = M_KV + NT
M_A = M_QA + NT
M_B = M_A + N_A * 2 * NT
M_O0 = M_B + (N_B * 4 - 1) * NT
M_QL = M_O0 + N_OUT * NT
M_KR = M_QL + 2 * NT
M_G = M_KR + 1
M_H = M_G + N_GATE * NT
M_O1 = M_H + N_H * 2 * PAIR_EVAC
M_END = M_O1 + N_OUT * NT
T_A_PER = 1 + GROUP + UNITS
T_B_PER = 2 * GROUP + UNITS
T_H_PER = UNITS
T_M = 1
T_A = T_M + QUARTERS
T_B = T_A + N_A * T_A_PER
T_H = T_B + N_B * T_B_PER
X_VEC = 0
X_X0 = X_VEC + 1
X_U0 = X_X0 + KT
X_MOD1 = X_U0 + KT
X_X1 = X_MOD1 + 2
X_KROW = X_X1 + KT
X_QN = X_KROW + 1
X_CKV = X_QN + 4
X_KR = X_CKV + 4
X_U1 = X_KR + 1
X_END = X_U1 + KT
XH_U0, XH_QN, XH_CKV, XH_U1 = 0, KT, KT + 4, KT + 8
N_UA = 4
N_UB = N_UA + N_A * UNITS
N_UH = N_UB + N_B * UNITS
RES_0, ROWS_0 = 1, 1


MM_G = 2 * (M_KR - M_KV) // NT
MM_H = MM_G + 2 * N_GATE
MM_O1 = MM_H + N_H * 2 * PAIR_SLOTS


class At:

    def __init__(self, fixed, turn=None, per=0):
        self.fixed, self.turn, self.per = fixed, turn, per

    def plus(self, k):
        return At(self.fixed + k, self.turn, self.per)

    def count(self, off=0):
        c = self.fixed + off
        return c if self.turn is None else self.turn * self.per + c

    def ring(self, n):
        assert self.per % n == 0
        return self.fixed % n

    def lap(self, n):
        c = self.fixed // n
        return c if self.turn is None else self.turn * (self.per // n) + c


def finished(m):
    for start, base in ((M_O1, MM_O1), (M_G, MM_G), (M_KV, 0)):
        if m.fixed >= start:
            return At(base + 2 * ((m.fixed - start) // NT), m.turn, 2 * m.per // NT)


def need(eng, sem, at, off=0):
    if at.turn is None:
        if at.fixed + off > 0:
            eng.wait_ge(sem, at.fixed + off)
    else:
        assert at.fixed + off > 0
        eng.wait_ge(sem, at.count(off))


def landed(eng, sems, at):
    n = len(sems)
    lap = at.lap(n)
    eng.wait_ge(sems[at.ring(n)], lap * 16 + 16)


class Pair:

    def __init__(self, index, turn=None):
        def at(start, per):
            return At(start + index * per, turn, 2 * per)

        self.index, self.turn, self.parity = index, turn, index % 2
        self.w, self.m, self.mm = at(W_H, PAIR_SLOTS), at(M_H, PAIR_EVAC), at(MM_H, PAIR_SLOTS)
        self.r, self.n = at(0, 2), at(N_UH, PAIR_UNITS)
        self.before = Pair(index - 1, turn) if index > 0 else None

    def column(self, h):
        fixed = (2 * self.index + h) * P
        return fixed if self.turn is None else self.turn * (4 * P) + fixed


class Chain:

    def __init__(self, eng, sem):
        self.eng, self.sem, self.at, self.k = eng, sem, At(0), 0

    def add(self, ins):
        ins.then_inc(self.sem, 1)
        self.k += 1

    def sync(self):
        self.eng.wait_ge(self.sem, self.at.count(self.k))

    def enter(self, turn, per):
        self.at, self.k = At(self.at.fixed + self.k, turn, per), 0

    def leave(self, turns):
        assert self.k == self.at.per, (self.k, self.at.per)
        self.at, self.k = At(self.at.fixed + turns * self.k), 0


def at_(col, width):
    return slice(col, col + width) if isinstance(col, int) else bass.ds(col, width)


def spread(ap, dims):
    return bass.AP(ap.tensor, ap.offset, [list(ap.ap[0])] + dims)


def build(nc, t_in, t_out):
    ctx = ExitStack()
    with ctx:
        top = [(nc.sbuf_base + 63) // 64 * 64]

        def sb(name, shape, dt=F32, at=None):
            size = int(np.prod(shape[1:])) * 4
            offset = top[0] if at is None else at
            if at is None:
                top[0] += (size + 31) // 32 * 32
            return nc.alloc_sbuf_tensor_at(name, [P] + list(shape[1:]), dt, offset=offset)

        def sem(name):
            return ctx.enter_context(nc.semaphore(name))

        act_hi = sb("act_hi", [P, KT, TOK], F32R)
        lo_at = top[0]
        act_lo = sb("act_lo", [P, KT, TOK], F32R)
        act_f = sb("act_f", [P, KT, TOK], F32, at=lo_at)
        u = sb("u", [P, NT, D])
        w_raw = sb("w_raw", [P, RAW_RING, SLOT])
        w_hi = sb("w_hi", [P, SPLIT_RING, SLOT], F32R)
        w_lo = sb("w_lo", [P, SPLIT_RING, SLOT], F32R)
        ada_at = top[0]
        ada = sb("ada", [P, ADA_RING, SLOT])
        gate_bc = sb("gate_bc", [P, 2, D], F32, at=ada_at)
        fnorm = sb("fnorm", [P, D], F32, at=ada_at + 2 * D * 4)
        ckv_hi = sb("ckv_hi", [P, 4, KEYS], F32R, at=ada_at)
        ckv_lo = sb("ckv_lo", [P, 4, KEYS], F32R, at=ada_at + 4 * KEYS * 4)
        qn_hi = sb("qn_hi", [P, 4, TOK], F32R, at=ada_at + 8 * KEYS * 4)
        qn_lo = sb("qn_lo", [P, 4, TOK], F32R, at=ada_at + 8 * KEYS * 4 + 4 * TOK * 4)
        rope_q = sb("rope_q", [P, TOK], at=ada_at + 8 * (KEYS + TOK) * 4)
        st = sb("st", [P, 2, NT, CH])
        qT = sb("qT", [P, GROUP, TOK])
        kT = sb("kT", [P, GROUP, KEYS])
        k_group = kT[:, 1, :].rearrange("p (t d) -> p t d", t=4)
        v_group = kT[:, 2, :].rearrange("p (t d) -> p t d", t=4)
        v4 = sb("v4", [P, 4, CH])
        prob = sb("prob", [P, 3, 3 * P])
        probT = sb("probT", [P, 2, 3 * P])
        rows = sb("rows", [P, 6, CH])
        bias_at = top[0]
        bias = sb("bias", [P, GROUP, 2, 4, GRID_W])
        gain_ql = sb("gain_ql", [P, CH], at=bias_at)
        gain_kv = sb("gain_kv", [P, CH], at=bias_at + CH * 4)
        krot = qT[:, 0, :]
        krT = sb("krT", [P, KEYS], at=bias_at + 2 * CH * 4)
        krows = sb("krows", [P, 4, 2, ROPE], at=bias_at + (2 * CH + KEYS) * 4)
        swapped = sb("swapped", [P, CH])
        kcache = swapped
        cos0 = sb("cos0", [P, 2, HEAD]); sin0 = sb("sin0", [P, 2, HEAD])
        cos1 = sb("cos1", [P, 2, ROPE]); sin1 = sb("sin1", [P, 2, ROPE])
        mask = sb("mask", [P, GRID_W])
        ident = sb("ident", [P, P])
        gain_q = sb("gain_q", [P, HEAD]); gain_k = sb("gain_k", [P, HEAD])
        vec = sb("vec", [P, P])
        vecT = sb("vecT", [P, 4, KT])
        half_tanh = sb("half_tanh", [P, 2, KT])
        silu_c = sb("silu_c", [P, KT, 32])
        mod = sb("mod", [P, 2, 2, KT])
        ss = sb("ss", [P, 16]); ms = sb("ms", [P, 16]); rstd = sb("rstd", [P, 16])
        mhalf = sb("mhalf", [P, 16])
        begun = sb("begun", [P, 32])
        nmax = sb("nmax", [P, 4]); rsum = sb("rsum", [P, 4]); rinv = sb("rinv", [P, 4])
        assert top[0] <= nc.sbuf_usable_end, top[0] - nc.sbuf_usable_end
        stage = [st[:, 0], st[:, 1]]
        stage_flat = st[:, :, :, :].rearrange("p a t n -> p (a t n)")
        q_turned = stage[1].rearrange("p t n -> p (t n)").rearrange("p (h n) -> p h n", h=GROUP)

        def bank(name):
            return ctx.enter_context(nc.psum_tensor(name, [P, CH], F32))

        G = [bank(f"gemm{i}") for i in range(3)]
        AD = bank("ada_bank")
        S = [bank("scores0"), bank("scores1")]
        TB = bank("turned")
        OB = bank("attended")
        BX = [S[0], S[1], TB, OB]
        PAIR_BANKS = G + [AD]

        raw_in = [sem(f"raw_in{i}") for i in range(RAW_RING)]
        ada_in = [sem(f"ada_in{i}") for i in range(ADA_RING)]
        hi_ready = sem("hi_ready")
        lo_ready = sem("lo_ready")
        w_used = sem("w_used")
        ada_used = sem("ada_used")
        rows_free = sem("rows_free")
        mm_done = sem("mm_done")
        evac = sem("evac")
        t_done = sem("t_done"); t_free = sem("t_free")
        x_done = sem("x_done"); x_free = sem("x_free")
        xhi = sem("xhi")
        h_ready = sem("h_ready"); hhi = sem("hhi"); hlo = sem("hlo")
        s_done = sem("s_done"); mx_ready = sem("mx_ready"); p_ready = sem("p_ready")
        pv_done = sem("pv_done"); o_done = sem("o_done")
        v_own = sem("v_own")
        ss_ready = sem("ss_ready"); ms_ready = sem("ms_ready"); rstd_ready = sem("rstd_ready")
        xn_ready = sem("xn_ready")
        gate_done = sem("gate_done")
        tanh_ready = sem("tanh_ready"); silu_ready = sem("silu_ready")
        x_in = [sem(f"x_in{i}") for i in range(NT)]
        const_in = sem("const_in"); vec_in = sem("vec_in"); rows_in = sem("rows_in")
        set_up = sem("set_up")
        kvn_ready = sem("kvn_ready"); qn_ready = sem("qn_ready"); group_copied = sem("group_copied")
        cache_in = sem("cache_in"); kc_in = sem("kc_in"); vc_in = sem("vc_in")
        bias_in = sem("bias_in"); bias_ready = sem("bias_ready")
        kb_out = sem("kb_out"); vb_out = sem("vb_out"); side_out = sem("side_out")
        rope_ready = sem("rope_ready")
        grow_out = sem("grow_out"); gbc_in = sem("gbc_in"); res_in = sem("res_in")
        res_done = sem("res_done"); x1_out = sem("x1_out"); y_ready = sem("y_ready")
        y_out = sem("y_out"); fn_in = sem("fn_in"); lc_in = sem("lc_in"); table_out = sem("table_out"); gain_in = sem("gain_in")

        x1_dram = nc.dram_tensor("x1_scratch", [P, NT, D], F32, kind="Internal").ap()
        gate_dram = nc.dram_tensor("gate_scratch", [2, 2, D], F32, kind="Internal").ap()
        bias_dram = nc.dram_tensor("bias_scratch", [N_B * GROUP, 2 * P, 2 * P], F32,
                                   kind="Internal").ap()
        block = ctx.enter_context(nc.Block())

        def beside(n):
            return [j for j in range(SPC) if (3 * j + 2) // 2 == n]

        def ada_beside(j):
            return [2 * (j // 3) + j % 3] if j % 3 < 2 else []

        def load_step(c):
            return (0, 0, 1, 1, 2, 3, 4, 5)[c]

        def evac_of(pair, c):
            return pair.plus((0, None, 1, None, 2, 3, 4, 5)[c])

        @block.sync
        def _(sp):
            def load_w(w):
                need(sp, lo_ready, w, 1 - RAW_RING)
                r = w.ring(RAW_RING)
                sp.dma_start(w_raw[:, r, :], t_in["w_all"][w.count()])\
                    .then_inc(raw_in[r], 16)

            def load_ada(a):
                need(sp, ada_used, a, 1 - ADA_RING)
                r = a.ring(ADA_RING)
                sp.dma_start(ada[:, r, :], t_in["ada_all"][a.count()]).then_inc(ada_in[r], 16)

            for n, name in enumerate(("c_ctx", "c", "l0_norm", "l1_norm")):
                src = t_in[name]
                src = src[0] if name == "c" else src
                sp.dma_start(vec[KT * n:KT * n + KT, :], src.rearrange("(k p) -> k p", p=P))\
                    .then_inc(vec_in, 16)
            sp.dma_start(ident[:], t_in["ident"]).then_inc(vec_in, 16)
            for j in range(KT - 4):
                load_ada(At(j))
            for j in range(RAW_RING):
                load_w(At(W_KV + j))
            for j in range(KT - 4, KT):
                load_ada(At(j))
            with sp.Fori(0, QUARTERS - 1) as i:
                for j in range(RAW_RING):
                    for k in range(4):
                        load_ada(At(KT + 4 * j + k, i, KT))
                    load_w(At(W_KV + RAW_RING + j, i, RAW_RING))
            with sp.Fori(0, N_A) as i:
                for j in range(2 * SPC):
                    load_w(At(W_A + j, i, 2 * SPC))
                    for half in range(2):
                        load_ada(At(2 * HALVES + 2 * j + half, i, HALVES))
            for i in range(N_B):
                for j in range((4 if i < N_B - 1 else 3) * SPC):
                    load_w(At(W_B + i * 4 * SPC + j))
                    if j < 3 * SPC:
                        for k in ada_beside(j):
                            for half in range(2):
                                load_ada(At((2 + N_A + i) * HALVES + 2 * k + half))
            with sp.Fori(0, N_OUT) as i:
                for j in range(SPC):
                    load_w(At(W_O0 + j, i, SPC))
            for j in range(W_QL, W_G):
                load_w(At(j))
            with sp.Fori(0, N_GATE) as i:
                for j in range(SPC):
                    load_w(At(W_G + j, i, SPC))
            with sp.Fori(0, N_H) as i:
                for j in range(2 * PAIR_SLOTS):
                    load_w(At(W_H + j, i, 2 * PAIR_SLOTS))
            with sp.Fori(0, N_OUT) as i:
                for j in range(SPC):
                    load_w(At(W_O1 + j, i, SPC))

        @block.tensor
        def _(pe):
            def product(out, pairs):
                last = None
                for n, ((ahi, alo), (bhi, blo)) in enumerate(pairs):
                    pe.matmul(out, alo, bhi, start=(n == 0), stop=False)
                    pe.matmul(out, ahi, blo, start=False, stop=False)
                    last = pe.matmul(out, ahi, bhi, start=False, stop=(n == len(pairs) - 1))
                return last

            def split_pair(hi, lo, *index):
                return hi[index], lo[index]

            def chunk_slot(w, j, m, made=None, banks=None):
                r = w.ring(SPLIT_RING)
                need(pe, lo_ready, w, 1)
                if made is not None:
                    pe.wait_ge(made[0], made[1] + KPS * (j + 1))
                whi = w_hi[:, r, :].rearrange("p (k n) -> p k n", k=KPS)
                wlo = w_lo[:, r, :].rearrange("p (k n) -> p k n", k=KPS)
                for t in range(NT):
                    if j == 0 and banks is None:
                        need(pe, evac, m.plus(t), 1 - NT)
                    bank_ = (banks or G)[t]
                    rows_t = slice(t * P, (t + 1) * P)
                    for kk in range(KPS):
                        k = KPS * j + kk
                        first, end = (k == 0), (k == KT - 1)
                        ahi, alo = act_hi[:, k, rows_t], act_lo[:, k, rows_t]
                        pe.matmul(bank_[:], alo, whi[:, kk], start=first, stop=False)
                        pe.matmul(bank_[:], ahi, wlo[:, kk], start=False, stop=False)
                        last = pe.matmul(bank_[:], ahi, whi[:, kk], start=False, stop=end)
                    if j == SPC - 1 and t < NT - 1:
                        last.then_inc(mm_done, 1)
                last.then_inc(w_used, 1)

            def ada_k(a, k, third):
                if k == 0:
                    need(pe, rows_free, third)
                for half in range(2):
                    at = a.plus(2 * k + half)
                    landed(pe, ada_in, at)
                    r = at.ring(ADA_RING)
                    for gg in range(2):
                        g = 2 * half + gg
                        last = pe.matmul(AD[32 * g:32 * g + 32, :], silu_c[:, k, :],
                                         ada[:, r, gg * CH:(gg + 1) * CH],
                                         start=(k == 0), stop=(k == KT - 1), tile_position=(0, 32 * g))
                    last.then_inc(ada_used, 1)

            def ada_quarter(q, k):
                if k == 0:
                    pe.wait_ge(rows_free, ROWS_0 + q)
                at = At(KT * q + k)
                landed(pe, ada_in, at)
                for g in range(4):
                    last = pe.matmul(AD[32 * g:32 * g + 32, 0:CH // 2], silu_c[:, k, :],
                                     ada[:, at.ring(ADA_RING), g * CH // 2:(g + 1) * CH // 2],
                                     start=(k == 0), stop=(k == KT - 1), tile_position=(0, 32 * g))
                last.then_inc(ada_used, 1)

            def turn(bank_, parts, width=P, height=P):
                for n, part in enumerate(parts):
                    last = pe.transpose(bank_[0:width, n * height:(n + 1) * height], part,
                                        ident[0:height, 0:height])
                return last

            def turn_out(x, parts, width=P, height=P):
                need(pe, x_free, x, 1 - len(BX))
                turn(BX[x.ring(len(BX))], parts, width, height).then_inc(x_done, 1)

            def turn_in(tau, parts):
                need(pe, t_free, tau)
                turn(TB, parts).then_inc(t_done, 1)

            def token_blocks(rows_, col):
                return [rows_[:, t, col:col + P] for t in range(NT)]

            def turned_chunk(x, w, m, made, rows_made=None):
                for k in range(2 * KPS):
                    if rows_made and k == 0:
                        pe.wait_ge(rows_made, NT + NT)
                    turn_out(At(x + k), token_blocks(u, k * P))
                for j in range(SPC):
                    chunk_slot(At(w + j), j, At(m), made)
                    for k in range(KPS * (j + 2), min(KPS * (j + 3), KT)):
                        if rows_made and k % (CH // P) == 0:
                            pe.wait_ge(rows_made, NT + NT * (k // (CH // P) + 1))
                        turn_out(At(x + k), token_blocks(u, k * P))

            def score(n, h, t, kh, latent=False):
                need(pe, p_ready, n, -1)
                s = S[n.ring(2)]
                keys = slice(0, P) if t == 0 else slice(P, KEYS)
                width = P if t == 0 else 3 * P
                last = pe.matmul(s[:, 0:width], qT[:, h, t * P:(t + 1) * P], kT[:, kh, keys],
                                 start=True, stop=not latent)
                if latent:
                    last = pe.matmul(s[:, 0:width], q_turned[:, h, t * P:(t + 1) * P],
                                     krT[:, keys], start=False, stop=True)
                last.then_inc(s_done, 1)

            def prob_turn(n, t, tau):
                need(pe, p_ready, n, 1)
                blocks = [prob[:, n.ring(3), b * P:(b + 1) * P] for b in range(1 if t == 0 else 3)]
                turn_in(tau, blocks)

            def attend(n, t, tau, values):
                need(pe, t_free, tau, 1)
                need(pe, o_done, n)
                out = OB[:, n.ring(4) * P:(n.ring(4) + 1) * P]
                tiles = [0] if t == 0 else [1, 2, 3]
                for b, kt in enumerate(tiles):
                    last = pe.matmul(out, probT[:, n.ring(2), b * P:(b + 1) * P], values(kt),
                                     start=(b == 0), stop=(b == len(tiles) - 1))
                last.then_inc(pv_done, 1)

            pe.wait_ge(vec_in, 80)
            turn_out(At(X_VEC), [vec[0:4 * KT, :]], P, 4 * KT)
            pe.wait_ge(silu_ready, 1)
            for k in range(KT):
                ada_quarter(0, k)
            pe.wait_ge(xn_ready, NT)
            for k in range(KT):
                turn_out(At(X_X0 + k), token_blocks(u, k * P))
            pe.wait_ge(x_free, X_X0 + KT)
            for q in range(QUARTERS):
                pe.wait_ge(rows_free, ROWS_0 + q + 1)
                turn_in(At(T_M + q), [rows[:, q // 2, (q % 2) * CH // 2 + j * P:(q % 2) * CH // 2 + (j + 1) * P]
                                      for j in range(2)])
                for s_ in range(4):
                    if q + 1 < QUARTERS:
                        for k in range(4):
                            ada_quarter(q + 1, 4 * s_ + k)
                    c, j = s_ // 2, 2 * q + s_ % 2
                    chunk_slot(At(W_KV + 4 * q + s_), j, At((M_KV, M_QA)[c]), (hlo, 0), (G, [S[0], S[1], OB])[c])
            with pe.Fori(0, N_A) as i:
                m, tau, n0 = At(M_A, i, 2 * NT), At(T_A, i, T_A_PER), At(N_UA, i, UNITS)
                for j in range(SPC):
                    if j == SPC - 1:
                        need(pe, t_free, tau, 2)
                        score(n0, 0, 0, 0)
                        score(n0.plus(1), 0, 1, 0)
                    chunk_slot(At(W_A + j, i, 2 * SPC), j, m)
                    ada_k(At(2 * HALVES, i, HALVES), j, At(ROWS_0 + QUARTERS, i, 1))
                    if j == 2:
                        need(pe, group_copied, At(2, i, 2))
                        turn_in(tau, [k_group[:, kt, :] for kt in range(4)])
                    if j >= 4:
                        h = j - 4
                        if h == 0:
                            need(pe, qn_ready, At(NT, i, NT))
                        turn_in(tau.plus(1 + h), token_blocks(stage[0], h * P))

                def attend_a(n):
                    attend(n0.plus(n), n % NT, tau.plus(1 + GROUP + n), lambda kt: v_group[:, kt, :])

                for n in range(UNITS):
                    prob_turn(n0.plus(n), n % NT, tau.plus(1 + GROUP + n))
                    if n + 2 < UNITS:
                        if (n + 2) % NT == 0:
                            need(pe, t_free, tau, 2 + (n + 2) // NT)
                        score(n0.plus(n + 2), (n + 2) // NT, (n + 2) % NT, 0)
                    if n > 0:
                        attend_a(n - 1)
                    for j in beside(n):
                        chunk_slot(At(W_A + SPC + j, i, 2 * SPC), j, m.plus(NT))
                        ada_k(At(2 * HALVES, i, HALVES), SPC + j, At(ROWS_0 + QUARTERS, i, 1))
                attend_a(UNITS - 1)
            for i in range(N_B):
                w0, m = W_B + i * 4 * SPC, At(M_B + i * 4 * NT)
                tau, n0 = At(T_B + i * T_B_PER), At(N_UB + i * UNITS)
                for j in range(3 * SPC):
                    if j == 3 * SPC - 1:
                        need(pe, t_free, tau, 2 * GROUP)
                        score(n0, 0, 0, 0)
                        score(n0.plus(1), 0, 1, 0)
                    chunk_slot(At(w0 + j), j % SPC, m.plus(NT * (j // SPC)))
                    for k in ada_beside(j):
                        ada_k(At((2 + N_A + i) * HALVES), k, At(ROWS_0 + QUARTERS + N_A + i))
                    if 1 <= j < 5:
                        h = j - 1
                        need(pe, evac, m)
                        turn_in(tau.plus(h), token_blocks(stage[0], h * P))
                    if SPC + 1 <= j < SPC + 5:
                        h = j - SPC - 1
                        need(pe, evac, m, NT)
                        pe.wait_ge(kc_in, 16 * (i + 1))
                        b = token_blocks(stage[1], h * P)
                        turn_in(tau.plus(GROUP + h), [b[0], kcache[:, h * P:(h + 1) * P], b[1], b[2]])
                pe.wait_ge(vc_in, 16 * (i + 1))

                def attend_b(n):
                    h = n // NT
                    attend(n0.plus(n), n % NT, tau.plus(2 * GROUP + n),
                           lambda kt: v4[:, kt, h * P:(h + 1) * P])

                for n in range(UNITS):
                    prob_turn(n0.plus(n), n % NT, tau.plus(2 * GROUP + n))
                    if n + 2 < UNITS:
                        score(n0.plus(n + 2), (n + 2) // NT, (n + 2) % NT, (n + 2) // NT)
                    if n > 0:
                        attend_b(n - 1)
                    for j in beside(n) if i < N_B - 1 else []:
                        chunk_slot(At(w0 + 3 * SPC + j), j, m.plus(3 * NT))
                attend_b(UNITS - 1)
            pe.wait_ge(o_done, N_UH)
            pe.wait_ge(t_free, T_H)
            turned_chunk(X_U0, W_O0, M_O0, (x_free, X_U0))
            pe.wait_ge(rows_free, ROWS_0 + QUARTERS + 4)
            for which in range(2):
                turn_out(At(X_MOD1 + which), [rows[:, 3 + which, j * P:(j + 1) * P] for j in range(4)])
            with pe.Fori(0, N_OUT - 1) as i:
                for j in range(SPC):
                    chunk_slot(At(W_O0 + SPC + j, i, SPC), j, At(M_O0 + NT, i, NT))
            turned_chunk(X_X1, W_QL, M_QL, (hlo, KT), xn_ready)
            for j in range(SPC):
                chunk_slot(At(W_QL + SPC + j), j, At(M_QL + NT))
            w = At(W_KR)
            need(pe, lo_ready, w, 1)
            whi = w_hi[:, w.ring(SPLIT_RING), :].rearrange("p (k n) -> p k n", k=KT)
            wlo = w_lo[:, w.ring(SPLIT_RING), :].rearrange("p (k n) -> p k n", k=KT)
            product(AD[0:ROPE, 0:TOK], [((whi[:, k], wlo[:, k]), (act_hi[:, k, :], act_lo[:, k, :]))
                                        for k in range(KT)]).then_inc(w_used, 1)
            pe.wait_ge(evac, M_KR + 1)
            turn_out(At(X_KROW), [krot[0:ROPE, t * P:(t + 1) * P] for t in range(NT)], P, ROPE)
            with pe.Fori(0, N_GATE - 1) as i:
                for j in range(SPC):
                    chunk_slot(At(W_G + j, i, SPC), j, At(M_G, i, NT))
            pe.wait_ge(qn_ready, N_A * NT + NT)
            pe.wait_ge(kvn_ready, 2)
            pe.wait_ge(lc_in, 32)
            for j in range(SPC):
                chunk_slot(At(W_G + (N_GATE - 1) * SPC + j), j, At(M_G + (N_GATE - 1) * NT))
                if j < 4:
                    turn_out(At(X_QN + j), token_blocks(stage[0], j * P))
                else:
                    k = j - 4
                    turn_out(At(X_CKV + k), [v4[:, kt, k * P:(k + 1) * P] for kt in range(4)])
                if j == SPC - 1:
                    turn_out(At(X_KR), [krows[:, kt, :, :].rearrange("p s d -> p (s d)") for kt in range(4)])
            pe.wait_ge(x_free, X_U1)
            def pair_product(g, c):
                w, s_ = g.w.plus(c // 2), c // 2
                if c % 2 == 0:
                    need(pe, lo_ready, w, 1)
                hi_, lo_ = (x[:, w.ring(SPLIT_RING), :].rearrange("p (k n) -> p k n", k=4)
                            for x in (w_hi, w_lo))
                if c < NT and g.before is None:
                    pe.wait_ge(evac, M_H - NT + 1 + c)
                if c in (5, 7):
                    need(pe, rope_ready, g.r, (c - 3) // 2)
                elif c >= 4:
                    need(pe, evac, evac_of(g.m, c - 4), 1)
                else:
                    need(pe, evac, evac_of(g.m, c + 4), 1 - PAIR_EVAC)
                bank_ = PAIR_BANKS[c % 4]
                if c < 4:
                    cols = slice((c % 2) * P, (c % 2 + 1) * P)
                    last = product(bank_[:, 0:TOK], [((hi_[:, k, cols], lo_[:, k, cols]),
                                                      (qn_hi[:, k], qn_lo[:, k])) for k in range(4)])
                elif c < 6:
                    cols = slice((c - 4) * P, (c - 3) * P)
                    last = product(bank_[:], [((hi_[:, k, cols], lo_[:, k, cols]),
                                               (ckv_hi[:, k], ckv_lo[:, k])) for k in range(4)])
                else:
                    for n in range(2):
                        kt = 2 * (c - 6) + n
                        rows_t = slice(kt * P, (kt + 1) * P)
                        last = product(bank_[:, 2 * P * n:2 * P * (n + 1)],
                                       [((ckv_hi[:, k, rows_t], ckv_lo[:, k, rows_t]),
                                         (hi_[:, k], lo_[:, k])) for k in range(4)])
                last.then_inc(mm_done if c % 2 == 0 else w_used, 1)

            def head_score(g, n, at):
                h, t = n // NT, n % NT
                if t == 0:
                    need(pe, evac, evac_of(g.m, 4 + h), 1)
                    need(pe, rope_ready, g.r, h + 1)
                score(at, 2 * g.parity + h, t, 2 * g.parity + h, latent=True)

            def attend_pair(g, n, at):
                h = 2 * g.parity + n // NT
                if n == 0:
                    need(pe, evac, evac_of(g.m, 7), 1)
                attend(at, n % NT, At(T_H - N_UH).plus(at.fixed) if at.turn is None
                       else At(at.fixed + T_H - N_UH, at.turn, at.per),
                       lambda kt: v4[:, kt, h * P:(h + 1) * P])

            def pair_attention(g, following):
                for n in range(PAIR_UNITS):
                    at = g.n.plus(n)
                    prob_turn(at, n % NT, At(at.fixed + T_H - N_UH, at.turn, at.per))
                    if n + 2 < PAIR_UNITS:
                        head_score(g, n + 2, at.plus(2))
                    elif following is not None:
                        head_score(following, n + 2 - PAIR_UNITS, at.plus(2))
                    if n > 0:
                        attend_pair(g, n - 1, at.plus(-1))
                    elif g.before is not None:
                        attend_pair(g.before, PAIR_UNITS - 1, at.plus(-1))
                    if following is not None:
                        for c in range(8):
                            if load_step(c) == n:
                                pair_product(following, c)

            for c in range(8):
                pair_product(Pair(0), c)
            for n in range(2):
                head_score(Pair(0), n, Pair(0).n.plus(n))
            pair_attention(Pair(0), Pair(1))
            with pe.Fori(0, N_H - 1) as i:
                for p in (1, 2):
                    pair_attention(Pair(p, i), Pair(p + 1, i))
            pair_attention(Pair(2 * N_H - 1), None)
            attend_pair(Pair(2 * N_H - 1), PAIR_UNITS - 1, At(N_UH + N_H * UNITS - 1))
            pe.wait_ge(o_done, N_UH + N_H * UNITS)
            pe.wait_ge(t_free, T_H + N_H * T_H_PER)
            turned_chunk(X_U1, W_O1, M_O1, (x_free, X_U1))
            with pe.Fori(0, N_OUT - 1) as i:
                for j in range(SPC):
                    chunk_slot(At(W_O1 + SPC + j, i, SPC), j, At(M_O1 + NT, i, NT))

        @block.scalar
        def _(act):
            copy = lambda out, in_, scale=1.0: act.activation(out, in_, ACT.Copy, scale=scale)

            def split_hi(w, width=SLOT):
                landed(act, raw_in, w)
                need(act, w_used, w, 1 - SPLIT_RING)
                copy(w_hi[:, w.ring(SPLIT_RING), 0:width], w_raw[:, w.ring(RAW_RING), 0:width])\
                    .then_inc(hi_ready, 1)

            def act_high(k, base):
                if base == 0:
                    act.wait_ge(h_ready, k + 1)
                else:
                    act.wait_ge(x_free, X_X1 + k + 1)
                copy(act_hi[:, k, :], act_f[:, k, :]).then_inc(hhi, 1)

            def turned_high(x, out, width):
                need(act, x_done, x, 1)
                copy(out, BX[x.ring(len(BX))][:, 0:width]).then_inc(xhi, 1)

            def tile_done(m, w, t):
                if t < NT - 1:
                    need(act, mm_done, finished(m), t + 1)
                else:
                    need(act, w_used, w, 1)

            def evacuate(m, w, outs, scale=1.0, banks=G):
                for t, out in enumerate(outs):
                    tile_done(m, w, t)
                    copy(out, banks[t][:], scale).then_inc(evac, 1)

            def evacuate_gate(m, w, col, tiles=range(NT)):
                for t in tiles:
                    tile_done(m, w, t)
                    copy(u[:, t, at_(col, CH)], G[t][:], 0.5)
                    act.activation(stage[1][:, t, :], G[t][:], ACT.Tanh, scale=0.5).then_inc(evac, 1)

            def exponent(n, t):
                width = P if t == 0 else 3 * P
                need(act, mx_ready, n, 1)
                need(act, pv_done, n, -2)
                need(act, o_done, n, -3)
                act.activation(prob[:, n.ring(3), 0:width], S[n.ring(2)][:, 0:width], ACT.Exp,
                               bias=nmax[:, n.ring(4):n.ring(4) + 1],
                               accum_out=rsum[:, n.ring(4):n.ring(4) + 1]).then_inc(p_ready, 1)

            def square_sums(rows_, sizes, at, width, before):
                for t, tile in enumerate(sizes):
                    if before + t > 0:
                        act.wait_ge(ss_ready, before + t)
                    act.activation(stage_flat[:, 0:width], rows_[:, tile, 0:width], ACT.Square,
                                   accum_out=ss[:, at + t:at + t + 1]).then_inc(ss_ready, 1)

            act.dma_start(u[:, 0, :], t_in["x_prompt"][0]).then_inc(x_in[0], 16)
            for t in range(2):
                act.dma_start(u[:, 1 + t, :], t_in["x_sample"][0, t * P:(t + 1) * P, :])\
                    .then_inc(x_in[1 + t], 16)
            act.wait_ge(x_free, X_VEC + 1)
            act.activation(half_tanh[:], vecT[:, 0:2, :], ACT.Tanh, scale=0.5).then_inc(tanh_ready, 1)
            for t in range(NT):
                act.wait_ge(x_in[t], 16)
                square_sums(u, [t], t, D, t)
            split_hi(At(0))
            split_hi(At(1))
            for q in range(QUARTERS):
                for k in range(KPQ * q, KPQ * (q + 1)):
                    act_high(k, 0)
                for w in range(4 * q, 4 * q + 4):
                    if w == 2 * SPC - 3:
                        evacuate(At(M_KV), At(w), [v4[:, kt, :] for kt in KEY_TILE])
                    if w == 2 * SPC - 2:
                        act.wait_ge(evac, NT)
                        for t in range(NT):
                            act.activation(stage[1][:, t, 0:2 * HEAD], v4[:, KEY_TILE[t], 0:2 * HEAD],
                                           ACT.Square).then_inc(ss_ready, 1)
                    if w == 2 * SPC - 1:
                        evacuate(At(M_QA), At(w), [stage[0][:, t, :] for t in range(NT)],
                                 banks=[S[0], S[1], OB])
                    split_hi(At(w + 2))
            with act.Fori(0, N_A) as i:
                m, tau, n0 = At(M_A, i, 2 * NT), At(T_A, i, T_A_PER), At(N_UA, i, UNITS)
                for j in range(SPC):
                    w = At(W_A + j, i, 2 * SPC)
                    if j == 0:
                        need(act, evac, m)
                        need(act, o_done, n0)
                        act.wait_ge(ms_ready, 2)
                        for t in range(NT):
                            act.activation(stage[1][:, t, :], stage[0][:, t, :], ACT.Square)\
                                .then_inc(ss_ready, 1)
                    if j == 1:
                        act.wait_ge(kvn_ready, 1)
                        act.wait_ge(cache_in, 32)
                        need(act, t_done, tau)
                        need(act, pv_done, n0)
                        copy(k_group, v4[:, :, bass.ds(i * HEAD, HEAD)]).then_inc(group_copied, 1)
                        copy(v_group, v4[:, :, bass.ds(i * HEAD + 2 * HEAD, HEAD)])\
                            .then_inc(group_copied, 1)
                    if j == SPC - 1:
                        exponent(n0, 0)
                        exponent(n0.plus(1), 1)
                        need(act, qn_ready, At(NT, i, NT))
                        evacuate_gate(m, w, i * CH, [0])
                    split_hi(w.plus(2))
                exponent(n0.plus(2), 2)
                evacuate_gate(m, At(W_A + SPC - 1, i, 2 * SPC), i * CH, [1, 2])
                for n in range(UNITS):
                    if 2 < n + 2 < UNITS:
                        exponent(n0.plus(n + 2), (n + 2) % NT)
                    for j in beside(n):
                        w = At(W_A + SPC + j, i, 2 * SPC)
                        if j == SPC - 1:
                            evacuate(m.plus(NT), w, [stage[0][:, t, :] for t in range(NT)])
                        split_hi(w.plus(2))
            for i in range(N_B):
                m, tau = At(M_B + i * 4 * NT), At(T_B + i * T_B_PER)
                n0 = At(N_UB + i * UNITS)
                for j in range(3 * SPC):
                    w = At(W_B + i * 4 * SPC + j)
                    if j == SPC - 1:
                        need(act, o_done, n0)
                        evacuate(m, w, [stage[1][:, t, :] for t in range(NT)])
                    if j == 2 * SPC - 1:
                        act.wait_ge(kc_in, 16 * (i + 1))
                        evacuate(m.plus(NT), w, [v4[:, kt, :] for kt in KEY_TILE])
                    if j == 3 * SPC - 1:
                        exponent(n0, 0)
                        exponent(n0.plus(1), 1)
                        act.wait_ge(kb_out, 16 * (i + 1))
                        need(act, t_done, tau, 2 * GROUP)
                        evacuate_gate(m.plus(2 * NT), w, i * CH + N_A * CH, [0])
                    split_hi(w.plus(2))
                exponent(n0.plus(2), 2)
                evacuate_gate(m.plus(2 * NT), w, i * CH + N_A * CH, [1, 2])
                for n in range(UNITS):
                    if 2 < n + 2 < UNITS:
                        exponent(n0.plus(n + 2), (n + 2) % NT)
                    for j in beside(n) if i < N_B - 1 else []:
                        w = At(W_B + (i * 4 + 3) * SPC + j)
                        if j == SPC - 1:
                            evacuate(m.plus(3 * NT), w, [stage[0][:, t, :] for t in range(NT)])
                        split_hi(w.plus(2))

            def chunk_squares(i, res, sums):
                cols = bass.ds(i * CH, CH)
                for t in range(NT):
                    need(act, res_done, res, t + 1)
                    need(act, ss_ready, sums, t)
                    act.activation(prob[:, 0:2, :].rearrange("p a n -> p (a n)")[:, 0:CH], u[:, t, cols],
                                   ACT.Square, accum_out=ss[:, bass.ds(i * NT + t, 1)])\
                        .then_inc(ss_ready, 1)

            def out_product(x, xh, w, m, res, sums, last):
                for k in range(2 * KPS):
                    turned_high(At(x + k), act_hi[:, k, :], TOK)
                for j in range(SPC):
                    for k in range(KPS * (j + 2), min(KPS * (j + 3), KT)):
                        turned_high(At(x + k), act_hi[:, k, :], TOK)
                    if j == SPC - 1:
                        evacuate(At(m), At(w + j), [stage[0][:, t, :] for t in range(NT)])
                    split_hi(At(w + j + 2))

                def chunk(i, place, ends=False):
                    for j in range(SPC):
                        if j == SPC - 1:
                            chunk_squares(i, place(res, NT), place(sums, NT))
                            evacuate(place(m + NT, NT), place(w + SPC + j, SPC),
                                     [stage[0][:, t, :] for t in range(NT)])
                        if not (ends and j >= SPC - 2):
                            split_hi(place(w + SPC + j + 2, SPC))

                turns = N_OUT - 1 - last
                with act.Fori(0, turns) as i:
                    chunk(i, lambda fixed, per: At(fixed, i, per))
                if last:
                    chunk(turns, lambda fixed, per: At(fixed + turns * per), True)
                chunk_squares(N_OUT - 1, At(res + (N_OUT - 1) * NT), At(sums + (N_OUT - 1) * NT))

            out_product(X_U0, XH_U0, W_O0, M_O0, RES_0, SS_OUT0, False)
            act_high(0, KT)
            act_high(1, KT)
            for c in range(2):
                for j in range(SPC):
                    if c == 0:
                        for k in range(2 * j + 2, min(2 * j + 4, KT)):
                            act_high(k, KT)
                    if j == SPC - 1 and c == 0:
                        evacuate(At(M_QL), At(W_QL + j), [stage[0][:, t, :] for t in range(NT)])
                    if j == SPC - 1 and c == 1:
                        act.wait_ge(vb_out, N_B * 16)
                        evacuate(At(M_QL + NT), At(W_QL + SPC + j), [v4[:, kt, :] for kt in KEY_TILE])
                    split_hi(At(W_QL + c * SPC + j + 2))
            for t in range(NT):
                act.wait_ge(evac, M_QL + 1 + t)
                act.activation(stage[1][:, t, :], stage[0][:, t, :], ACT.Square,
                               accum_out=ss[:, t:t + 1]).then_inc(ss_ready, 1)
            act.wait_ge(w_used, W_KR + 1)
            copy(krot[0:ROPE, :], AD[0:ROPE, 0:TOK]).then_inc(evac, 1)
            split_hi(At(W_G + 1))
            for t in range(NT):
                act.wait_ge(evac, M_QL + NT + 1 + t)
                act.wait_ge(ss_ready, SS_LAT - 2 * NT + 1 + t)
                act.activation(stage[1][:, t, :], v4[:, KEY_TILE[t], :], ACT.Square,
                               accum_out=ss[:, NT + t:NT + t + 1]).then_inc(ss_ready, 1)

            def gate_chunk(place, last=False):
                for j in range(SPC):
                    if last and j < 4:
                        turned_high(At(X_QN + j), qn_hi[:, j, :], TOK)
                    elif last:
                        turned_high(At(X_CKV + j - 4), ckv_hi[:, j - 4, :], KEYS)
                    split_hi(place(W_G + j + 2, SPC))
                need(act, gate_done, place((N_A + N_B) * NT, NT))
                evacuate_gate(place(M_G, NT), place(W_G + SPC - 1, SPC), gate_column(place))

            def gate_column(place):
                return place(0, CH).count()

            with act.Fori(0, N_GATE - 1) as i:
                gate_chunk(lambda fixed, per: At(fixed, i, per))
            gate_chunk(lambda fixed, per: At(fixed + (N_GATE - 1) * per), True)
            act.wait_ge(side_out, 64)

            def pair_out(g, c):
                if c % 2 == 0:
                    need(act, mm_done, g.mm, c // 2 + 1)
                else:
                    need(act, w_used, g.w, c // 2 + 1)
                bank_, h = PAIR_BANKS[c % 4], 2 * g.parity
                if c == 0 and g.index > 1:
                    need(act, pv_done, g.n, -PAIR_UNITS)
                if c in (0, 2):
                    copy(qT[:, h + c // 2, :], bank_[:, 0:TOK], SC1).then_inc(evac, 1)
                elif c in (4, 5):
                    copy(kT[:, h + c - 4, :], bank_[:]).then_inc(evac, 1)
                elif c >= 6:
                    copy(v4[:, 2 * (c - 6):2 * (c - 5), h * P:(h + 2) * P],
                         bank_[:].rearrange("p (t d) -> p t d", t=2)).then_inc(evac, 1)
                if c % 2 == 1:
                    split_hi(g.w.plus(c // 2 + 2))

            def pair_attention(g, following):
                for n in range(PAIR_UNITS):
                    if n + 2 < PAIR_UNITS or following is not None:
                        exponent(g.n.plus(n + 2), (n + 2) % NT)
                    for c in range(8):
                        if following is not None and load_step(c) == n:
                            pair_out(following, c)

            for c in range(8):
                pair_out(Pair(0), c)
            for n in range(2):
                exponent(At(N_UH + n), n)
            pair_attention(Pair(0), Pair(1))
            with act.Fori(0, N_H - 1) as i:
                for p in (1, 2):
                    pair_attention(Pair(p, i), Pair(p + 1, i))
            pair_attention(Pair(2 * N_H - 1), None)
            out_product(X_U1, XH_U1, W_O1, M_O1, RES_0 + N_OUT * NT, SS_LAT, True)

        @block.vector
        def _(dve):
            own = Chain(dve, v_own)

            def split_lo(w, width=SLOT):
                need(dve, hi_ready, w, 1)
                r = w.ring(SPLIT_RING)
                dve.tensor_tensor(w_lo[:, r, 0:width], w_raw[:, w.ring(RAW_RING), 0:width],
                                  w_hi[:, r, 0:width].bitcast(F32), ALU.subtract).then_inc(lo_ready, 1)

            def modulate(k, base):
                for v, cols in ((0, slice(0, P)), (1, slice(P, TOK))):
                    last = dve.tensor_scalar(act_f[:, k, cols], act_f[:, k, cols], mod[:, 1, v, k:k + 1],
                                             mod[:, 0, v, k:k + 1], ALU.mult, ALU.add)
                last.then_inc(h_ready, 1)

            def modulate_turned(k):
                dve.wait_ge(x_done, X_X1 + k + 1)
                for v, cols in ((0, slice(0, P)), (1, slice(P, TOK))):
                    last = dve.tensor_scalar(act_f[:, k, cols], BX[(X_X1 + k) % 4][:, cols],
                                             mod[:, 1, v, k:k + 1], mod[:, 0, v, k:k + 1],
                                             ALU.mult, ALU.add)
                last.then_inc(x_free, 1)

            def act_low(k, base):
                dve.wait_ge(hhi, base + k + 1)
                dve.tensor_tensor(act_lo[:, k, :], act_f[:, k, :], act_hi[:, k, :].bitcast(F32),
                                  ALU.subtract).then_inc(hlo, 1)

            def tokens_turned(first):
                for k in range(KT):
                    dve.wait_ge(x_done, first + k + 1)
                    dve.tensor_copy(act_f[:, k, :], BX[(first + k) % 4][:, 0:TOK]).then_inc(x_free, 1)

            def modulation(first, third, gain):
                for which in range(2):
                    x = first + which
                    dve.wait_ge(x_done, x + 1)
                    for v in range(2):
                        part = BX[x % 4][:].rearrange("p (j g q) -> p q g j", j=4, g=4)[:, v]
                        out = mod[:, which, v, :].rearrange("p (g j) -> p g j", g=4)
                        if which == 0:
                            ins = dve.tensor_copy(out, part)
                        else:
                            ins = dve.scalar_tensor_tensor(
                                out=out, in0=part, scalar=1.0,
                                in1=vecT[:, gain, :].rearrange("p (g j) -> p g j", g=4),
                                op0=ALU.add, op1=ALU.mult)
                        if v == 0:
                            own.add(ins)
                    ins.then_inc(x_free, 1)
                dve.wait_ge(x_free, first + 2)
                own.sync()

            def modulation_quarter(q):
                tau = At(T_M + q)
                need(dve, t_done, tau, 1)
                for which in range(2):
                    for v in range(2):
                        part = TB[:, 0:CH // 2].rearrange("p (j g q) -> p q g j", j=2, g=4)\
                            [:, v, 2 * which:2 * which + 2]
                        out = mod[:, which, v, KPQ * q:KPQ * (q + 1)].rearrange("p (g j) -> p g j", g=2)
                        if which == 0:
                            own.add(dve.tensor_copy(out, part))
                        else:
                            ins = dve.scalar_tensor_tensor(
                                out=out, in0=part, scalar=1.0,
                                in1=vecT[:, 2, KPQ * q:KPQ * (q + 1)].rearrange("p (g j) -> p g j", g=2),
                                op0=ALU.add, op1=ALU.mult)
                            if v == 0:
                                own.add(ins)
                            else:
                                ins.then_inc(t_free, 1)
                need(dve, t_free, tau, 1)
                own.sync()

            def add_quarter(q):
                dve.wait_ge(ada_used, KT * (q + 1))
                at = rows[:, q // 2, (q % 2) * CH // 2:(q % 2 + 1) * CH // 2]
                dve.tensor_tensor(at, AD[:, 0:CH // 2], at, ALU.add).then_inc(rows_free, 1)

            def add_rows(third_at):
                need(dve, ada_used, At(HALVES * (third_at.fixed + 1), third_at.turn, HALVES * third_at.per))
                rows_at = rows[:, bass.ds(third_at.count(), 1), :].rearrange("p o n -> p (o n)") \
                    if third_at.turn is not None else rows[:, third_at.fixed, :]
                dve.tensor_tensor(rows_at, AD[:], rows_at, ALU.add).then_inc(rows_free, 1)

            powers = [0, None, 0]

            def root(turn, base, width, inverse, at=0):
                own.sync()
                dve.tensor_scalar(ms[:, 0:width], ss[:, at:at + width], inverse, EPS, ALU.mult, ALU.add)\
                    .then_inc(ms_ready, 1)
                need(dve, rstd_ready, At(base + 1, turn, 1) if turn is not None else At(base + 1))

            def normalise_tokens(power):
                dve.wait_ge(ss_ready, SS_AT[power])
                if power > 0:
                    own.add(dve.reduce_sum(ss[:, N_OUT * NT:N_OUT * NT + NT],
                                           spread(ss[:], [[1, NT], [NT, N_OUT]]), X))
                root(None, power, NT, 1.0 / D, 0 if power == 0 else N_OUT * NT)

            def head_norm(x, heads, at, gain):
                r = rstd[:, at:at + heads]
                own.add(dve.tensor_tensor(x, x, spread(r, [[1, heads], [0, HEAD]]), ALU.mult))
                own.sync()
                own.add(dve.tensor_tensor(x, x, spread(gain[:], [[0, heads], [1, HEAD]]), ALU.mult))
                own.sync()

            def rotate(x, heads, width, cos, sin, done=None):
                q = width // 4
                xr = x.rearrange("p h (a s m) -> p h a s m", a=2, s=2)
                sw = swapped[:, 0:heads * width].rearrange("p (h a s m) -> p h a s m", h=heads, a=2, s=2)
                sv = sin.rearrange("p (a s m) -> p a s m", a=2, s=2)
                for s in range(2):
                    tab = sv[:, :, s, :]
                    tab = spread(tab, [[0, heads]] + [list(d) for d in tab.ap[1:]])
                    own.add(dve.tensor_tensor(sw[:, :, :, s, :], xr[:, :, :, 1 - s, :], tab, ALU.mult))
                own.sync()
                own.add(dve.tensor_tensor(x, x, spread(cos, [[0, heads], [1, width]]), ALU.mult))
                own.sync()
                last = dve.tensor_tensor(x, x, swapped[:, 0:heads * width].rearrange("p (h d) -> p h d", h=heads),
                                         ALU.add)
                if done is None:
                    own.add(last)
                    own.sync()
                else:
                    last.then_inc(done, 1)

            def maximum(n, t, h=0, biased=False):
                width = P if t == 0 else 3 * P
                s = S[n.ring(2)]
                need(dve, s_done, n, 1)
                need(dve, p_ready, n, -3)
                if biased and t > 0:
                    own.add(dve.tensor_tensor(
                        s[:, P:3 * P], s[:, P:3 * P],
                        bias[:, h, t - 1, :, :].rearrange("p r c -> p (r c)"), ALU.add))
                    own.sync()
                dve.tensor_reduce(nmax[:, n.ring(4):n.ring(4) + 1], s[:, 0:width], X, ALU.max,
                                  negate=True).then_inc(mx_ready, 1)

            def copy_turned(tau, out, cols, scale=None):
                need(dve, t_done, tau, 1)
                if scale is None:
                    dve.tensor_copy(out, TB[:, 0:cols]).then_inc(t_free, 1)
                else:
                    dve.tensor_scalar(out, TB[:, 0:cols], scale, None, ALU.mult).then_inc(t_free, 1)

            def prob_copy(n, t, tau):
                need(dve, pv_done, n, -1)
                width = P if t == 0 else 3 * P
                copy_turned(tau, probT[:, n.ring(2), 0:width], width)

            def output(n, t, col):
                need(dve, p_ready, n, 1)
                own.add(dve.reciprocal(rinv[:, n.ring(4):n.ring(4) + 1], rsum[:, n.ring(4):n.ring(4) + 1]))
                own.sync()
                need(dve, pv_done, n, 1)
                at = u[:, t, at_(col, P)]
                dve.scalar_tensor_tensor(out=at, in0=OB[:, n.ring(4) * P:(n.ring(4) + 1) * P],
                                         scalar=rinv[:, n.ring(4):n.ring(4) + 1], in1=at,
                                         op0=ALU.mult, op1=ALU.mult).then_inc(o_done, 1)

            def finish_gate(m, gates, col):
                for t in range(NT):
                    need(dve, evac, m.plus(t), 1)
                    at = u[:, t, at_(col, CH)]
                    dve.scalar_tensor_tensor(out=at, in0=stage[1][:, t, :], scalar=1.0, in1=at,
                                             op0=ALU.add, op1=ALU.mult).then_inc(gate_done, 1)
                need(dve, gate_done, gates, NT)

            def turned_low(x, hi, out, width, high_at):
                dve.wait_ge(xhi, high_at + 1)
                dve.tensor_tensor(out, BX[x % 4][:, 0:width], hi.bitcast(F32), ALU.subtract)\
                    .then_inc(x_free, 1)

            def turned_chunk(x, xh, w):
                for k in range(2 * KPS):
                    turned_low(x + k, act_hi[:, k, :], act_lo[:, k, :], TOK, xh + k)
                for j in range(SPC):
                    for k in range(KPS * (j + 2), min(KPS * (j + 3), KT)):
                        turned_low(x + k, act_hi[:, k, :], act_lo[:, k, :], TOK, xh + k)
                    split_lo(At(w + j + 2))

            def key_norms():
                dve.wait_ge(ss_ready, 2 * NT)
                dve.wait_ge(const_in, CONSTS * 16)
                own.add(dve.tensor_scalar(gain_q[:], gain_q[:], SC0, None, ALU.mult))
                for t in range(NT):
                    own.add(dve.reduce_sum(ss[:, 2 * t:2 * t + 2],
                                           stage[1][:, t, 0:2 * HEAD].rearrange("p (h d) -> p h d", h=2), X))
                root(None, 1, 2 * NT, 1.0 / HEAD)
                for t in range(NT):
                    x = v4[:, KEY_TILE[t], 0:2 * HEAD].rearrange("p (h d) -> p h d", h=2)
                    head_norm(x, 2, 2 * t, gain_k)
                    if t > 0:
                        rotate(x, 2, HEAD, cos0[:, t - 1, :], sin0[:, t - 1, :])
                dve.memset(ms[:, 15:16], 1.0).then_inc(kvn_ready, 1)

            def residual(i, col):
                for t in range(NT):
                    own.add(dve.tensor_tensor(stage[0][:, t, :], stage[0][:, t, :],
                                              gate_bc[:, min(t, 1), at_(col, CH)], ALU.mult))
                own.sync()
                for t in range(NT):
                    dve.tensor_tensor(u[:, t, at_(col, CH)], stage[0][:, t, :], stage[1][:, t, :],
                                      ALU.add).then_inc(res_done, 1)

            dve.memset(silu_c[:], 0.0).then_inc(set_up, 1)
            dve.memset(mhalf[:], -0.5).then_inc(set_up, 1)
            dve.memset(ms[:], 1.0).then_inc(set_up, 1)
            columns = 0
            for first, counts in ((N_UA, (s_done, mx_ready, p_ready, pv_done, o_done)),
                                  (T_M, (t_done, t_free)), (RES_0, (res_done,)),
                                  (ROWS_0, (rows_free,))):
                for count in counts:
                    dve.memset(begun[:, columns:columns + 1], 0.0).then_inc(count, first)
                    columns += 1
            dve.wait_ge(set_up, 3)
            dve.wait_ge(x_done, X_VEC + 1)
            dve.tensor_copy(vecT[:].rearrange("p a k -> p (a k)"), BX[X_VEC % 4][:, 0:4 * KT])\
                .then_inc(x_free, 1)
            dve.wait_ge(tanh_ready, 1)
            own.add(dve.scalar_tensor_tensor(out=half_tanh[:], in0=half_tanh[:], scalar=1.0,
                                             in1=vecT[:, 0:2, :], op0=ALU.add, op1=ALU.mult))
            own.sync()
            dve.tensor_scalar(silu_c[:, :, 0:2].rearrange("p k v -> p v k"), half_tanh[:], 0.5, None,
                              ALU.mult).then_inc(silu_ready, 1)
            normalise_tokens(0)
            for t in range(NT):
                dve.tensor_scalar(u[:, t, :], u[:, t, :], rstd[:, t:t + 1], None, ALU.mult)\
                    .then_inc(xn_ready, 1)
            dve.wait_ge(rows_in, 12 * 16)
            add_quarter(0)
            tokens_turned(X_X0)
            split_lo(At(0))
            split_lo(At(1))
            dve.wait_ge(x_free, X_X0 + KT)
            for q in range(QUARTERS):
                modulation_quarter(q)
                for k in range(KPQ * q, KPQ * (q + 1), 2):
                    modulate(k, 0)
                    modulate(k + 1, 0)
                    act_low(k, 0)
                    act_low(k + 1, 0)
                for w in range(4 * q, 4 * q + 4):
                    if w % 4 == 3 and q + 1 < QUARTERS:
                        add_quarter(q + 1)
                    split_lo(At(w + 2))
            key_norms()
            with dve.Fori(0, N_A) as i:
                m, tau, n0 = At(M_A, i, 2 * NT), At(T_A, i, T_A_PER), At(N_UA, i, UNITS)
                own.enter(i, OWN_A)
                for j in range(SPC):
                    if j == 1:
                        need(dve, ss_ready, At(3 * NT, i, NT))
                        own.add(dve.reduce_sum(ss[:, 0:NT * GROUP],
                                               stage[1].rearrange("p t (h d) -> p (t h) d", h=GROUP), X))
                        root(i, 2, NT * GROUP, 1.0 / HEAD)
                    if j == 3:
                        copy_turned(tau, kT[:, 0, :], KEYS)
                    if 1 <= j < 4:
                        t = j - 1
                        x = stage[0][:, t, :].rearrange("p (h d) -> p h d", h=GROUP)
                        if t == 0:
                            r = rstd[:, 0:GROUP]
                            own.add(dve.tensor_tensor(x, x, spread(r, [[1, GROUP], [0, HEAD]]), ALU.mult))
                            own.sync()
                            dve.tensor_tensor(x, x, spread(gain_q[:], [[0, GROUP], [1, HEAD]]), ALU.mult)\
                                .then_inc(qn_ready, 1)
                        else:
                            head_norm(x, GROUP, t * GROUP, gain_q)
                            rotate(x, GROUP, HEAD, cos0[:, t - 1, :], sin0[:, t - 1, :], qn_ready)
                    if j >= 5:
                        copy_turned(tau.plus(1 + j - 5), qT[:, j - 5, :], TOK)
                    if j == SPC - 1:
                        maximum(n0, 0)
                        maximum(n0.plus(1), 1)
                    split_lo(At(W_A + j + 2, i, 2 * SPC))
                copy_turned(tau.plus(GROUP), qT[:, GROUP - 1, :], TOK)
                for n in range(UNITS):
                    prob_copy(n0.plus(n), n % NT, tau.plus(1 + GROUP + n))
                    if n + 2 < UNITS:
                        maximum(n0.plus(n + 2), (n + 2) % NT)
                    if n == 1:
                        finish_gate(m, At(0, i, NT), i * CH)
                    if n > 0:
                        output(n0.plus(n - 1), (n - 1) % NT, i * CH + (n - 1) // NT * P)
                    for j in beside(n):
                        split_lo(At(W_A + SPC + j + 2, i, 2 * SPC))
                output(n0.plus(UNITS - 1), NT - 1, i * CH + (GROUP - 1) * P)
                add_rows(At(2, i, 1))
            own.leave(N_A)
            for i in range(N_B):
                m, tau = At(M_B + i * 4 * NT), At(T_B + i * T_B_PER)
                n0, col = At(N_UB + i * UNITS), (N_A + i) * CH
                for j in range(3 * SPC):
                    if 2 <= j < 6:
                        copy_turned(tau.plus(j - 2), qT[:, j - 2, :], TOK)
                    if SPC + 2 <= j < SPC + 6:
                        h = j - SPC - 2
                        copy_turned(tau.plus(GROUP + h), kT[:, h, :], KEYS, scale=SC0)
                    if j == 3 * SPC - 1:
                        add_rows(At(2 + N_A + i))
                        dve.wait_ge(bias_ready, i + 1)
                        maximum(n0, 0, 0, True)
                        maximum(n0.plus(1), 1, 0, True)
                    split_lo(At(W_B + i * 4 * SPC + j + 2))
                for n in range(UNITS):
                    prob_copy(n0.plus(n), n % NT, tau.plus(2 * GROUP + n))
                    if n + 2 < UNITS:
                        maximum(n0.plus(n + 2), (n + 2) % NT, (n + 2) // NT, True)
                    if n == 1:
                        finish_gate(m.plus(2 * NT), At((N_A + i) * NT), col)
                    if n > 0:
                        output(n0.plus(n - 1), (n - 1) % NT, col + (n - 1) // NT * P)
                    for j in beside(n) if i < N_B - 1 else []:
                        split_lo(At(W_B + (i * 4 + 3) * SPC + j + 2))
                output(n0.plus(UNITS - 1), NT - 1, col + (GROUP - 1) * P)
            turned_chunk(X_U0, XH_U0, W_O0)
            modulation(X_MOD1, 3, 3)
            dve.wait_ge(evac, M_O0 + NT)
            dve.wait_ge(gbc_in, 32)
            dve.wait_ge(res_in, 32)
            residual(0, 0)
            with dve.Fori(0, N_OUT - 1) as i:
                own.enter(i, NT)
                for j in range(SPC):
                    split_lo(At(W_O0 + SPC + j + 2, i, SPC))
                need(dve, evac, At(M_O0 + 2 * NT, i, NT))
                need(dve, res_in, At(64, i, 32))
                residual(i, i * CH + CH)
            own.leave(N_OUT - 1)
            normalise_tokens(2 + N_A)
            dve.wait_ge(x1_out, N_OUT * 16)
            for c in range(N_OUT):
                for t in range(NT):
                    part = u[:, t, c * CH:(c + 1) * CH]
                    dve.tensor_scalar(part, part, rstd[:, t:t + 1], None, ALU.mult)\
                        .then_inc(xn_ready, 1)
            for k in range(2):
                modulate_turned(k)
            for k in range(2):
                act_low(k, KT)
            for c in range(2):
                for j in range(SPC):
                    if c == 0:
                        for k in range(2 * j + 2, min(2 * j + 4, KT)):
                            modulate_turned(k)
                        for k in range(2 * j + 2, min(2 * j + 4, KT)):
                            act_low(k, KT)
                    split_lo(At(W_QL + c * SPC + j + 2))
            split_lo(At(W_G + 1))
            dve.wait_ge(ss_ready, SS_LAT)
            dve.wait_ge(gain_in, 48)
            root(None, 3 + N_A, 2 * NT, 1.0 / CH)
            for t in range(NT):
                x = stage[0][:, t, :]
                dve.scalar_tensor_tensor(out=x, in0=x, scalar=rstd[:, t:t + 1], in1=gain_ql[:],
                                         op0=ALU.mult, op1=ALU.mult).then_inc(qn_ready, 1)
            for t in range(NT):
                x = v4[:, KEY_TILE[t], :]
                own.add(dve.scalar_tensor_tensor(out=x, in0=x, scalar=rstd[:, NT + t:NT + t + 1],
                                                 in1=gain_kv[:], op0=ALU.mult, op1=ALU.mult))
            dve.wait_ge(x_done, X_KROW + 1)
            place = BX[X_KROW % 4]
            own.add(dve.tensor_copy(krows[:, 0, 0, :], place[:, 0:ROPE]))
            dve.tensor_copy(krows[:, 2:4, 0, :], place[:, ROPE:3 * ROPE].rearrange("p (t d) -> p t d", t=2))\
                .then_inc(x_free, 1)
            dve.wait_ge(x_free, X_KROW + 1)
            own.sync()
            for t in range(2):
                rotate(krows[:, 2 + t, 0:1, :], 1, ROPE, cos1[:, t, :], sin1[:, t, :])
            dve.wait_ge(lc_in, 32)
            own.add(dve.tensor_copy(krows[:, :, 1, :], krows[:, :, 0, :]))
            own.sync()
            dve.memset(ms[:, 15:16], 1.0).then_inc(kvn_ready, 1)
            with dve.Fori(0, N_GATE - 1) as i:
                for j in range(SPC):
                    split_lo(At(W_G + j + 2, i, SPC))
                finish_gate(At(M_G, i, NT), At((N_A + N_B) * NT, i, NT), i * CH)
            done = N_GATE - 1
            for j in range(SPC):
                if j < 4:
                    turned_low(X_QN + j, qn_hi[:, j, :], qn_lo[:, j, :], TOK, XH_QN + j)
                else:
                    turned_low(X_CKV + j - 4, ckv_hi[:, j - 4, :], ckv_lo[:, j - 4, :], KEYS, XH_CKV + j - 4)
                split_lo(At(W_G + done * SPC + j + 2))
            dve.wait_ge(x_done, X_KR + 1)
            dve.tensor_copy(krT[:], BX[X_KR % 4][:]).then_inc(x_free, 1)
            finish_gate(At(M_G + done * NT), At((N_A + N_B + done) * NT), done * CH)

            def pair_out(g, c):
                if c in (1, 3):
                    need(dve, w_used, g.w, c // 2 + 1)
                    if c == 1 and g.index > 1:
                        need(dve, pv_done, g.n, -PAIR_UNITS)
                    dve.tensor_tensor(q_turned[:, 2 * g.parity + c // 2, :], PAIR_BANKS[c % 4][:, 0:TOK],
                                      rope_q[:], ALU.mult).then_inc(rope_ready, 1)
                if c % 2 == 1:
                    split_lo(g.w.plus(c // 2 + 2))

            def pair_output(g, n):
                output(g.n.plus(n), n % NT, g.column(n // NT))

            def pair_attention(g, following):
                for n in range(PAIR_UNITS):
                    at = g.n.plus(n)
                    prob_copy(at, n % NT, At(at.fixed + T_H - N_UH, at.turn, at.per))
                    if n + 2 < PAIR_UNITS or following is not None:
                        maximum(at.plus(2), (n + 2) % NT)
                    if n > 0:
                        pair_output(g, n - 1)
                    elif g.before is not None:
                        pair_output(g.before, PAIR_UNITS - 1)
                    for c in range(8):
                        if following is not None and load_step(c) == n:
                            pair_out(following, c)

            for c in range(8):
                pair_out(Pair(0), c)
            for n in range(2):
                maximum(At(N_UH + n), n)
            pair_attention(Pair(0), Pair(1))
            with dve.Fori(0, N_H - 1) as i:
                own.enter(i, 2 * PAIR_UNITS)
                for p in (1, 2):
                    pair_attention(Pair(p, i), Pair(p + 1, i))
            own.leave(N_H - 1)
            pair_attention(Pair(2 * N_H - 1), None)
            pair_output(Pair(2 * N_H - 1), PAIR_UNITS - 1)
            turned_chunk(X_U1, XH_U1, W_O1)
            dve.wait_ge(evac, M_O1 + NT)
            dve.wait_ge(gbc_in, 64)
            dve.wait_ge(res_in, 32 * N_OUT + 16)
            residual(0, 0)

            def out_chunk(i, place, last=False):
                for j in range(SPC):
                    if not (last and j >= SPC - 2):
                        split_lo(place(W_O1 + SPC + j + 2, SPC))
                need(dve, evac, place(M_O1 + 2 * NT, NT))
                need(dve, res_in, place(32 * N_OUT + 32, 16))
                residual(i, i * CH + CH)

            with dve.Fori(0, N_OUT - 2) as i:
                own.enter(i, NT)
                out_chunk(i, lambda fixed, per: At(fixed, i, per))
            own.leave(N_OUT - 2)
            out_chunk(N_OUT - 2, lambda fixed, per: At(fixed + (N_OUT - 2) * per), last=True)
            normalise_tokens(4 + N_A)
            dve.wait_ge(fn_in, 16)
            for t in range(NT):
                dve.scalar_tensor_tensor(out=u[:, t, :], in0=u[:, t, :], scalar=rstd[:, t:t + 1],
                                         in1=fnorm[:], op0=ALU.mult, op1=ALU.mult).then_inc(y_ready, 1)

        @block.gpsimd
        def _(pool):
            def power(at):
                need(pool, ms_ready, at, 1)
                pool.tensor_tensor(rstd[:], ms[:], mhalf[:], ALU.pow).then_inc(rstd_ready, 1)

            def to_all(out, vector, sem_):
                pool.dma_start(out, spread_rows(vector)).then_inc(sem_, 16)

            def spread_rows(vector):
                return bass.AP(vector.tensor, vector.offset, [[0, P]] + [list(d) for d in vector.ap])

            for name, tile in (("cos0", cos0), ("sin0", sin0), ("cos1", cos1), ("sin1", sin1),
                               ("mask", mask)):
                pool.dma_start(tile[:], t_in[name]).then_inc(const_in, 16)
            for name, tile in (("l0_q_norm", gain_q), ("l0_k_norm", gain_k)):
                to_all(tile[:], t_in[name], const_in)
            b0, b1 = t_in["l0_ada_b"], t_in["l1_ada_b"]
            for g in range(4):
                group = slice(32 * g, 32 * g + 32)
                quarters = bass.AP(b0.tensor, b0.offset + (g // 2) * D + (g % 2) * CH // 2,
                                   [[0, 32], [CH, QUARTERS], [1, CH // 2]])
                pool.dma_start(rows[group, 0:2, :].rearrange("p a (b n) -> p (a b) n", b=2), quarters)\
                    .then_inc(rows_in, 16)
                pool.dma_start(rows[group, 2, :], bass.AP(b0.tensor, b0.offset + 2 * D + g * CH,
                                                          [[0, 32], [1, CH]])).then_inc(rows_in, 16)
                pool.dma_start(rows[group, 3:6, :], bass.AP(b1.tensor, b1.offset + g * CH,
                                                            [[0, 32], [D, 3], [1, CH]])).then_inc(rows_in, 16)
            pool.dma_start(v4[:, 1, 0:2 * HEAD], t_in["cache_l0_a_k"][0].rearrange("t h d -> t (h d)"))\
                .then_inc(cache_in, 16)
            pool.dma_start(v4[:, 1, 2 * HEAD:4 * HEAD], t_in["cache_l0_a_v"][0].rearrange("t h d -> t (h d)"))\
                .then_inc(cache_in, 16)
            pool.wait_ge(set_up, 3)
            power(At(0))
            rpb = t_in["l0_rpb"]
            table = (2 * 8 - 1) * (2 * WIN - 1)

            def bias_tables(heads):
                for h in heads:
                    pool.wait_ge(w_used, W_A + 2 + 2 * h)
                    for qr in range(4):
                        base = h * table + (7 - qr) * (2 * WIN - 1) + WIN - 1
                        src = bass.AP(rpb.tensor, base, [[2 * WIN - 1, 4], [-1, GRID_W], [1, GRID_W]])
                        pool.dma_start(bias_dram[h, GRID_W * qr:GRID_W * (qr + 1), :]
                                       .rearrange("q (r c) -> r q c", r=4), src).then_inc(table_out, 16)

            power(At(1))
            pool.wait_ge(kvn_ready, 1)
            pool.dma_start(t_out["a_k"][0].rearrange("t h d -> t (h d)"), v4[:, 0, 0:2 * HEAD])\
                .then_inc(side_out, 16)
            pool.dma_start(t_out["a_v"][0].rearrange("t h d -> t (h d)"), v4[:, 0, 2 * HEAD:4 * HEAD])\
                .then_inc(side_out, 16)
            power(At(2))
            bias_tables(range(N_B * GROUP))
            power(At(3))
            pool.wait_ge(table_out, 16 * 4 * N_B * GROUP)
            kc = t_in["cache_l0_b_k"][0].rearrange("t h d -> t (h d)")
            vc = t_in["cache_l0_b_v"][0].rearrange("t h d -> t (h d)")
            kb = t_out["b_k"][0].rearrange("t h d -> t (h d)")
            vb = t_out["b_v"][0].rearrange("t h d -> t (h d)")
            pool.wait_ge(side_out, 32)
            for i in range(N_B):
                m, n0 = At(M_B + i * 4 * NT), At(N_UB + i * UNITS)
                need(pool, o_done, n0)
                if i > 0:
                    pool.wait_ge(vb_out, 16 * i)
                pool.dma_start(kcache[:], kc[:, bass.ds(i * CH, CH)]).then_inc(kc_in, 16)
                pool.dma_start(v4[:, 1, :], vc[:, bass.ds(i * CH, CH)]).then_inc(vc_in, 16)
                pool.dma_start(bias[:].rearrange("p h q r c -> p (h q) (r c)"),
                               bias_dram.rearrange("h (q p) n -> p (h q) n", p=P)
                               [:, bass.ds(i * 2 * GROUP, 2 * GROUP), :]).then_inc(bias_in, 16)
                pool.wait_ge(bias_in, 16 * (i + 1))
                flat = bias[:].rearrange("p h q r c -> p (h q r) c")
                pool.tensor_tensor(flat, flat, spread(mask[:], [[0, 8 * GROUP], [1, GRID_W]]), ALU.add)\
                    .then_inc(bias_ready, 1)
                need(pool, evac, m, NT)
                pool.dma_start(kb[:, bass.ds(i * CH, CH)], stage[1][:, 0, :]).then_inc(kb_out, 16)
                need(pool, evac, m, 2 * NT)
                pool.dma_start(vb[:, bass.ds(i * CH, CH)], v4[:, 0, :]).then_inc(vb_out, 16)

            def gate_rows(layer, third, after):
                pool.wait_ge(*after)
                pool.wait_ge(rows_free, ROWS_0 + QUARTERS + 4)
                for v in range(2):
                    pool.dma_start(gate_dram[layer, v].rearrange("(g n) -> g n", g=4),
                                   rows[v:v + 97:32, third, :]).then_inc(grow_out, 16)
                pool.wait_ge(grow_out, 32 * (layer + 1))
                for v in range(2):
                    to_all(gate_bc[:, v, :], gate_dram[layer, v], gbc_in)

            pool.wait_ge(o_done, N_UH)
            for name, tile in (("l1_q_a_norm", gain_ql), ("l1_kv_a_norm", gain_kv)):
                to_all(tile[:], t_in[name], gain_in)
            gate_rows(0, 2, (o_done, N_UH))
            pool.dma_start(rope_q[:], t_in["rope_q"]).then_inc(gain_in, 16)
            for i in range(N_OUT):
                need(pool, res_done, At(RES_0 + i * NT))
                cols = bass.ds(i * CH, CH)
                pool.dma_start(stage[1][:, 0, :], t_in["x_prompt"][0][:, cols]).then_inc(res_in, 16)
                pool.dma_start(stage[1][:, 1:3, :],
                               t_in["x_sample"][0].rearrange("(t p) n -> p t n", p=P)[:, :, cols])\
                    .then_inc(res_in, 16)
                need(pool, res_done, At(RES_0 + NT + i * NT))
                pool.dma_start(x1_dram[:, :, cols], u[:, :, cols]).then_inc(x1_out, 16)
            power(At(2 + N_A))
            pool.wait_ge(vb_out, N_B * 16)
            pool.dma_start(v4[:, 1, :], t_in["cache_l1_ckv"][0]).then_inc(lc_in, 16)
            pool.dma_start(krows[:, 1, 0, :], t_in["cache_l1_krope"][0]).then_inc(lc_in, 16)
            power(At(3 + N_A))
            pool.wait_ge(kvn_ready, 2)
            pool.dma_start(t_out["ckv"][0], v4[:, 0, :]).then_inc(side_out, 16)
            pool.dma_start(t_out["krope"][0], krows[:, 0, 0, :]).then_inc(side_out, 16)
            gate_rows(1, 5, (o_done, N_UH + N_H * UNITS))
            to_all(fnorm[:], t_in["final_norm"], fn_in)
            for i in range(N_OUT):
                need(pool, res_done, At(RES_0 + (N_OUT + i) * NT))
                pool.dma_start(stage[1], x1_dram[:, :, bass.ds(i * CH, CH)]).then_inc(res_in, 16)
            power(At(4 + N_A))
            pool.wait_ge(y_ready, 1)
            pool.dma_start(t_out["y_prompt"][0], u[:, 0, :]).then_inc(y_out, 16)
            for t in range(2):
                pool.wait_ge(y_ready, 2 + t)
                pool.dma_start(t_out["y_sample"][0, t * P:(t + 1) * P, :], u[:, 1 + t, :])\
                    .then_inc(y_out, 16)
            pool.wait_ge(y_out, 48)
            pool.wait_ge(side_out, 64)
            pool.wait_ge(kb_out, N_B * 16)
            pool.wait_ge(vb_out, N_B * 16)
            pool.wait_ge(x1_out, N_OUT * 16)


CONSTS = 7
OWN_A = 1 + 1 + 2 * (2 + 3) + UNITS
SS_OUT0 = (1 + 1 + N_A) * NT
SS_LAT = SS_OUT0 + N_OUT * NT + 2 * NT
SS_AT = {0: NT, 2 + N_A: SS_OUT0 + N_OUT * NT, 4 + N_A: SS_LAT + N_OUT * NT}


def slots(w, columns):
    out = []
    for c in columns:
        part = w[:, c:c + CH].reshape(KT // KPS, KPS, P, CH)
        out.append(part.transpose(0, 2, 1, 3).reshape(KT // KPS, P, SLOT))
    return out


def lay_out(x):
    f = {k: np.ascontiguousarray(v) for k, v in x.items()}
    kv, qb, gate = 1024, 1536, 4608
    query = [g * CH for g in range(N_A)] + [qb + g * CH for g in range(N_B)]
    columns = [kv, query[0]]
    for g in range(N_A + N_B):
        if g >= N_A:
            columns += [qb + 1024 + (g - N_A) * CH, qb + 2048 + (g - N_A) * CH]
        columns.append(gate + g * CH)
        columns += query[g + 1:g + 2]
    parts = slots(f["l0_w_in"], columns)
    parts += slots(f["l0_w_out"], range(0, D, CH))
    parts += slots(f["l1_w_in"], [0, CH])
    parts.append(f["l1_w_in"][:, 2 * CH:2 * CH + ROPE].reshape(KT, P, ROPE).transpose(1, 0, 2)
                 .reshape(1, P, SLOT))
    parts += slots(f["l1_w_in"], range(2 * CH + ROPE, 2 * CH + ROPE + D, CH))
    partner = np.arange(ROPE).reshape(2, 2, ROPE // 4)[:, ::-1].reshape(ROPE)
    q = f["l1_w_q_b"].reshape(4, P, 16, HEAD + ROPE)
    q = np.concatenate([q, q[..., HEAD + partner]], -1).transpose(2, 1, 0, 3)
    kv = f["l1_w_kv_b"].reshape(4, P, 8, 2, 2, HEAD).transpose(2, 4, 1, 0, 3, 5)
    heads = np.concatenate([q.reshape(8, 2, P, SLOT), kv.reshape(8, 2, P, SLOT)], 1)
    parts.append(heads.reshape(8 * PAIR_SLOTS, P, SLOT))
    parts += slots(f["l1_w_out"], range(0, D, CH))
    arrays = {"w_all": np.concatenate(parts)}
    assert len(arrays["w_all"]) == W_END
    first = arrays["w_all"][:2 * SPC].reshape(2, SPC // 2, 2, P, SLOT)
    arrays["w_all"][:2 * SPC] = first.transpose(1, 0, 2, 3, 4).reshape(2 * SPC, P, SLOT)
    arrays["ada_all"] = np.stack([f["l0_ada_w"], f["l1_ada_w"]]).reshape(2, KT, P, 3, 2, SLOT)\
        .transpose(0, 3, 1, 4, 2, 5).reshape(6 * HALVES, P, SLOT)
    arrays["ada_all"][:2 * HALVES] = f["l0_ada_w"][:, :2 * D].reshape(KT, P, 2, QUARTERS, CH)\
        .transpose(3, 0, 1, 2, 4).reshape(2 * HALVES, P, SLOT)
    for name in NAMES:
        arrays[name] = f[name]
    token = np.arange(2 * P)
    for n, width in ((0, HEAD), (1, ROPE)):
        a = width // 2
        inv = (1.0 / (np.float32(10000.0) ** (np.arange(a // 2, dtype=np.float32) * np.float32(2.0) / np.float32(a)))).astype(np.float32)
        angles = [(np.float32(1) * pos.astype(np.float32))[:, None] * inv for pos in (token // GRID_W, token % GRID_W)]
        cos = np.concatenate([np.tile(np.cos(g), (1, 2)) for g in angles], 1)
        sin = np.concatenate([np.concatenate([-np.sin(g), np.sin(g)], 1) for g in angles], 1)
        for name, table in (("cos", cos), ("sin", sin)):
            arrays[f"{name}{n}"] = np.ascontiguousarray(
                table.astype(np.float32).reshape(2, P, width).transpose(1, 0, 2))
    turn_ = [np.concatenate([np.full((P, ROPE), one), arrays[n].transpose(1, 0, 2).reshape(2 * P, ROPE)])
             for n, one in (("cos1", 1.0), ("sin1", 0.0))]
    arrays["rope_q"] = np.ascontiguousarray((np.concatenate(turn_, 1).T * SC1).astype(np.float32))
    col = np.arange(P)[:, None] % GRID_W
    start = np.clip(col - WIN // 2, 0, GRID_W - WIN)
    key = np.arange(GRID_W)[None]
    arrays["mask"] = np.where((key >= start) & (key < start + WIN), 0.0, -1e30).astype(np.float32)
    arrays["ident"] = np.eye(P, dtype=np.float32)
    return arrays


NAMES = ["x_prompt", "x_sample", "cache_l0_a_k", "cache_l0_a_v", "cache_l0_b_k", "cache_l0_b_v",
         "cache_l1_ckv", "cache_l1_krope", "c", "c_ctx", "l0_norm", "l0_ada_b", "l0_q_norm",
         "l0_k_norm", "l0_rpb", "l1_norm", "l1_ada_b", "l1_q_a_norm", "l1_kv_a_norm", "final_norm"]
OUTS = [("y_prompt", (1, P, D)), ("y_sample", (1, 2 * P, D)), ("a_k", (1, P, 2, HEAD)),
        ("a_v", (1, P, 2, HEAD)), ("b_k", (1, P, 8, HEAD)), ("b_v", (1, P, 8, HEAD)),
        ("ckv", (1, P, CH)), ("krope", (1, P, ROPE))]


def kernel(**inputs):
    from concourse import bacc
    from concourse.bass_utils import run_bass_kernel_spmd

    nc = bacc.Bacc("TRN2", target_bir_lowering=False, num_devices=1)
    arrays = lay_out(inputs)
    t_in = {n: nc.dram_tensor(f"in_{n}", a.shape, F32, kind="ExternalInput").ap()
            for n, a in arrays.items()}
    t_out = {n: nc.dram_tensor(f"out_{n}", s, F32, kind="ExternalOutput").ap() for n, s in OUTS}
    build(nc, t_in, t_out)
    r = run_bass_kernel_spmd(nc, [{f"in_{n}": a for n, a in arrays.items()}], core_ids=[0])
    return tuple(r.results[0][f"out_{n}"] for n, _ in OUTS)
```
